# Optimizing a Trainium2 kernel written in Bass

```python
import jax, jax.numpy as jnp
from jax import lax
import numpy as np

D_MODEL = 1024
BATCH = 1
SEQ = 256
DEPTH = 2
DEC_BATCH = 1
DEC_SEQ = 32
PAST_LEN = 128

CHUNK = 64
Q_BLOCK = 128
HEAD_DIM = 64
ROPE_THETA = 10000.0
N_HEADS_A = 4
N_KV_A = 2
WINDOW_A = 128
N_HEADS_B = 4
N_IDX_HEADS = 4
IDX_DIM = 64
TOPK_MAX = 256
N_HEADS_C = 4
N_HEADS_D = 4
Q_LORA = 256
KV_LORA = 128
NOPE_DIM = 64
ROPE_DIM = 32
V_DIM_D = 64
D_MIX = (N_HEADS_A + N_HEADS_B + N_HEADS_C) * HEAD_DIM + N_HEADS_D * V_DIM_D
D_FF = 2816
DN_ALPHA = (2 * DEPTH) ** 0.25
DN_BETA = (8 * DEPTH) ** -0.25
LN_EPS = 1e-5
RMS_EPS = 1e-6
IN_SPLITS = (
    N_HEADS_A * HEAD_DIM, N_KV_A * HEAD_DIM, N_KV_A * HEAD_DIM,
    N_HEADS_B * HEAD_DIM, HEAD_DIM, HEAD_DIM,
    N_IDX_HEADS * IDX_DIM, IDX_DIM, N_IDX_HEADS,
    N_HEADS_C * HEAD_DIM, N_HEADS_C * HEAD_DIM, N_HEADS_C * HEAD_DIM,
    Q_LORA, KV_LORA, ROPE_DIM,
)
D_IN = sum(IN_SPLITS)

kernel_name = 'hybrid_streaming_encoder_step'

def layer_norm(x, g, b):
    xf = x.astype(jnp.float32)
    mu = jnp.mean(xf, -1, keepdims=True)
    var = jnp.mean(jnp.square(xf - mu), -1, keepdims=True)
    return ((xf - mu) * lax.rsqrt(var + LN_EPS) * g + b).astype(x.dtype)

def rms_norm(x, g):
    xf = x.astype(jnp.float32)
    return (xf * lax.rsqrt(jnp.mean(xf * xf, -1, keepdims=True) + RMS_EPS) * g).astype(x.dtype)

def rope(x, pos):
    half = x.shape[-1] // 2
    inv = jnp.power(ROPE_THETA, -jnp.arange(half, dtype=jnp.float32) / half)
    ang = pos.astype(jnp.float32)[:, None] * inv[None, :]
    cos = jnp.cos(ang)[:, None, :]
    sin = jnp.sin(ang)[:, None, :]
    x1 = x[..., :half].astype(jnp.float32)
    x2 = x[..., half:].astype(jnp.float32)
    return jnp.concatenate([x1 * cos - x2 * sin, x2 * cos + x1 * sin], -1).astype(x.dtype)

def swiglu(x, w_gate, w_up, w_down):
    return (jax.nn.silu(x @ w_gate) * (x @ w_up)) @ w_down

def chunk_visible(q_pos, k_pos):
    return (k_pos // CHUNK)[None, :] <= (q_pos // CHUNK)[:, None]

def sweep_query_blocks(fn, q_args, q_pos):
    S = q_pos.shape[0]
    if S <= Q_BLOCK:
        return fn(*q_args, q_pos)
    nb = S // Q_BLOCK

    def blocks(a):
        return jnp.swapaxes(a.reshape((a.shape[0], nb, Q_BLOCK) + a.shape[2:]), 0, 1)

    xs = (tuple(blocks(a) for a in q_args), q_pos.reshape(nb, Q_BLOCK))
    out = lax.map(lambda z: fn(*z[0], z[1]), xs)
    out = jnp.swapaxes(out, 0, 1)
    return out.reshape((out.shape[0], S) + out.shape[3:])

def project(h, pos, w_in, g_cq, g_ckv, w_uq):
    B, S, _ = h.shape
    offs = np.cumsum(IN_SPLITS)[:-1].tolist()
    (qa, ka, va, qb, kb, vb, qi, ki, wi, qc, kc, vc, cq, ckv, kr) = jnp.split(h @ w_in, offs, axis=-1)
    qd = (rms_norm(cq, g_cq) @ w_uq).reshape(B, S, N_HEADS_D, NOPE_DIM + ROPE_DIM)
    qd = jnp.concatenate([qd[..., :NOPE_DIM], rope(qd[..., NOPE_DIM:], pos)], -1)
    return dict(
        qa=rope(qa.reshape(B, S, N_HEADS_A, HEAD_DIM), pos),
        ka=rope(ka.reshape(B, S, N_KV_A, HEAD_DIM), pos),
        va=va.reshape(B, S, N_KV_A, HEAD_DIM),
        qb=rope(qb.reshape(B, S, N_HEADS_B, HEAD_DIM), pos),
        kb=rope(kb.reshape(B, S, 1, HEAD_DIM), pos).reshape(B, S, HEAD_DIM),
        vb=vb,
        qi=rope(qi.reshape(B, S, N_IDX_HEADS, IDX_DIM), pos),
        ki=rope(ki.reshape(B, S, 1, IDX_DIM), pos).reshape(B, S, IDX_DIM),
        wi=wi * (N_IDX_HEADS * IDX_DIM) ** -0.5,
        qc=qc.reshape(B, S, N_HEADS_C, HEAD_DIM),
        kc=kc.reshape(B, S, N_HEADS_C, HEAD_DIM),
        vc=vc.reshape(B, S, N_HEADS_C, HEAD_DIM),
        qd=qd,
        ckv=rms_norm(ckv, g_ckv),
        kr=rope(kr.reshape(B, S, 1, ROPE_DIM), pos).reshape(B, S, ROPE_DIM),
    )

def sink_attend(q, k, v, sinks, mask):
    kv, g = q.shape[-3], q.shape[-2]
    s = jnp.einsum('...tkgd,...skd->...kgts', q, k).astype(jnp.float32) * HEAD_DIM ** -0.5
    if mask is not None:
        s = jnp.where(mask, s, -jnp.inf)
    sink = sinks.astype(jnp.float32).reshape(kv, g, 1, 1)
    m = jnp.maximum(jnp.max(s, -1, keepdims=True), sink)
    p = jnp.exp(s - m)
    p = p / (jnp.sum(p, -1, keepdims=True) + jnp.exp(sink - m))
    return jnp.einsum('...kgts,...skd->...tkgd', p.astype(v.dtype), v)

def swa_banded(q, k, v, sinks):
    B, S, H, D = q.shape
    nb, W, G = S // CHUNK, WINDOW_A // CHUNK, N_HEADS_A // N_KV_A
    qb = q.reshape(B, nb, CHUNK, N_KV_A, G, D)

    def band(x):
        xb = x.reshape(B, nb, CHUNK, N_KV_A, D)
        xp = jnp.pad(xb, ((0, 0), (W, 0), (0, 0), (0, 0), (0, 0)))
        return jnp.concatenate([xp[:, j:j + nb] for j in range(W + 1)], axis=2)

    src = jnp.arange(nb)[:, None] - W + jnp.arange(W + 1)[None, :]
    valid = jnp.repeat(src >= 0, CHUNK, axis=1)
    o = sink_attend(qb, band(k), band(v), sinks, valid[:, None, None, None, :])
    return o.reshape(B, S, H * D)

def dsa_block(q, qi, w, q_pos, k, v, ki, k_pos, topk):
    logits = jnp.einsum('bthd,bsd->bths', qi, ki)
    score = jnp.einsum('bths,bth->bts', jax.nn.relu(logits), w).astype(jnp.float32)
    score = jnp.where(chunk_visible(q_pos, k_pos), score, -jnp.inf)
    top_val, sel = lax.top_k(score, topk)
    valid = jnp.isfinite(top_val)
    gather = jax.vmap(lambda a, i: a[i])
    kg = gather(k, sel)
    vg = gather(v, sel)
    s = jnp.einsum('bthd,btkd->bhtk', q, kg).astype(jnp.float32) * HEAD_DIM ** -0.5
    s = jnp.where(valid[:, None], s, -jnp.inf)
    p = jax.nn.softmax(s, axis=-1)
    return jnp.einsum('bhtk,btkd->bthd', p.astype(vg.dtype), vg)

def sb_block(q, q_pos, k, v, k_pos):
    z = jnp.einsum('bthd,bshd->bhts', q, k).astype(jnp.float32) * HEAD_DIM ** -0.5
    causal = k_pos[None, :] < q_pos[:, None]
    log_beta = jax.nn.log_sigmoid(z)
    log_keep = jnp.where(causal, jax.nn.log_sigmoid(-z), 0.0)
    between = lax.cumsum(log_keep, axis=3, reverse=True) - log_keep
    a = jnp.where(causal, jnp.exp(log_beta + between), 0.0)
    return jnp.einsum('bhts,bshd->bthd', a.astype(v.dtype), v)

def mla_keys(ckv, kr, w_ukv):
    B, L, _ = ckv.shape
    kv = (ckv @ w_ukv).reshape(B, L, N_HEADS_D, NOPE_DIM + V_DIM_D)
    k = jnp.concatenate([kv[..., :NOPE_DIM],
                         jnp.broadcast_to(kr[:, :, None, :], (B, L, N_HEADS_D, ROPE_DIM))], -1)
    return k, kv[..., NOPE_DIM:]

def chunk_causal_attend(q, q_pos, k, v, k_pos):
    s = jnp.einsum('bthd,bshd->bhts', q, k).astype(jnp.float32) * (NOPE_DIM + ROPE_DIM) ** -0.5
    s = jnp.where(chunk_visible(q_pos, k_pos), s, -jnp.inf)
    p = jax.nn.softmax(s, axis=-1)
    return jnp.einsum('bhts,bshd->bthd', p.astype(v.dtype), v)

def mix_prompt(h, w_in, sinks, g_cq, g_ckv, w_uq, w_ukv, w_o):
    B, S, _ = h.shape
    pos = jnp.arange(S, dtype=jnp.int32)
    p = project(h, pos, w_in, g_cq, g_ckv, w_uq)
    o_a = swa_banded(p['qa'], p['ka'], p['va'], sinks)
    topk = min(TOPK_MAX, S // 4)
    o_b = sweep_query_blocks(
        lambda q, qi, w, qp: dsa_block(q, qi, w, qp, p['kb'], p['vb'], p['ki'], pos, topk),
        (p['qb'], p['qi'], p['wi']), pos)
    o_c = sweep_query_blocks(lambda q, qp: sb_block(q, qp, p['kc'], p['vc'], pos), (p['qc'],), pos)
    k_d, v_d = mla_keys(p['ckv'], p['kr'], w_ukv)
    o_d = sweep_query_blocks(lambda q, qp: chunk_causal_attend(q, qp, k_d, v_d, pos), (p['qd'],), pos)
    o = jnp.concatenate([o_a, o_b.reshape(B, S, -1), o_c.reshape(B, S, -1), o_d.reshape(B, S, -1)], -1) @ w_o
    state = (p['ka'][:, -WINDOW_A:], p['va'][:, -WINDOW_A:], p['kb'], p['vb'], p['ki'],
             p['kc'], p['vc'], p['ckv'], p['kr'])
    return o, state

def mix_step(h, caches, w_in, sinks, g_cq, g_ckv, w_uq, w_ukv, w_o):
    (c_ak, c_av, c_bk, c_bv, c_bi, c_ck, c_cv, c_dl, c_dr) = caches
    B, T, _ = h.shape
    P = c_bk.shape[1]
    pos = P + jnp.arange(T, dtype=jnp.int32)
    k_pos = jnp.arange(P + T, dtype=jnp.int32)
    p = project(h, pos, w_in, g_cq, g_ckv, w_uq)
    ka = jnp.concatenate([c_ak, p['ka']], 1)
    va = jnp.concatenate([c_av, p['va']], 1)
    qa = p['qa'].reshape(B, T, N_KV_A, N_HEADS_A // N_KV_A, HEAD_DIM)
    o_a = sink_attend(qa, ka, va, sinks, None).reshape(B, T, -1)
    kb = jnp.concatenate([c_bk, p['kb']], 1)
    vb = jnp.concatenate([c_bv, p['vb']], 1)
    ki = jnp.concatenate([c_bi, p['ki']], 1)
    topk = min(TOPK_MAX, (P + T) // 4)
    o_b = dsa_block(p['qb'], p['qi'], p['wi'], pos, kb, vb, ki, k_pos, topk)
    kc = jnp.concatenate([c_ck, p['kc']], 1)
    vc = jnp.concatenate([c_cv, p['vc']], 1)
    o_c = sb_block(p['qc'], pos, kc, vc, k_pos)
    k_d, v_d = mla_keys(jnp.concatenate([c_dl, p['ckv']], 1), jnp.concatenate([c_dr, p['kr']], 1), w_ukv)
    o_d = chunk_causal_attend(p['qd'], pos, k_d, v_d, k_pos)
    o = jnp.concatenate([o_a, o_b.reshape(B, T, -1), o_c.reshape(B, T, -1), o_d.reshape(B, T, -1)], -1) @ w_o
    state = (ka[:, -WINDOW_A:], va[:, -WINDOW_A:], p['kb'], p['vb'], p['ki'],
             p['kc'], p['vc'], p['ckv'], p['kr'])
    return o, state

def encoder_layer(h, mixer, ln_g, ln_b, f_gate, f_up, f_down):
    h = layer_norm(DN_ALPHA * h + 0.5 * swiglu(h, f_gate[0], f_up[0], f_down[0]), ln_g[0], ln_b[0])
    o, state = mixer(h)
    h = layer_norm(DN_ALPHA * h + o, ln_g[1], ln_b[1])
    h = layer_norm(DN_ALPHA * h + 0.5 * swiglu(h, f_gate[1], f_up[1], f_down[1]), ln_g[2], ln_b[2])
    return h, state

def setup_inputs(seed: int = 0) -> dict:
    key = jax.random.key(seed)
    ks = jax.random.split(key, 24)

    def nrm(k, shape, scale):
        return jax.random.normal(k, shape, jnp.float32) * scale

    win = min(WINDOW_A, PAST_LEN)
    return {
        'x_prompt': nrm(ks[0], (BATCH, SEQ, D_MODEL), 1.0),
        'x_sample': nrm(ks[1], (DEC_BATCH, DEC_SEQ, D_MODEL), 1.0),
        'cache_a_k': nrm(ks[2], (DEPTH, DEC_BATCH, win, N_KV_A, HEAD_DIM), 1.0),
        'cache_a_v': nrm(ks[3], (DEPTH, DEC_BATCH, win, N_KV_A, HEAD_DIM), 1.0),
        'cache_b_k': nrm(ks[4], (DEPTH, DEC_BATCH, PAST_LEN, HEAD_DIM), 1.0),
        'cache_b_v': nrm(ks[5], (DEPTH, DEC_BATCH, PAST_LEN, HEAD_DIM), 1.0),
        'cache_b_kidx': nrm(ks[6], (DEPTH, DEC_BATCH, PAST_LEN, IDX_DIM), 1.0),
        'cache_c_k': nrm(ks[7], (DEPTH, DEC_BATCH, PAST_LEN, N_HEADS_C, HEAD_DIM), 1.0),
        'cache_c_v': nrm(ks[8], (DEPTH, DEC_BATCH, PAST_LEN, N_HEADS_C, HEAD_DIM), 1.0),
        'cache_d_ckv': nrm(ks[9], (DEPTH, DEC_BATCH, PAST_LEN, KV_LORA), 1.0),
        'cache_d_krope': nrm(ks[10], (DEPTH, DEC_BATCH, PAST_LEN, ROPE_DIM), 1.0),
        'ln_g': 1.0 + nrm(ks[11], (DEPTH, 3, D_MODEL), 0.02),
        'ln_b': nrm(ks[12], (DEPTH, 3, D_MODEL), 0.02),
        'ffn_gate': nrm(ks[13], (DEPTH, 2, D_MODEL, D_FF), D_MODEL ** -0.5),
        'ffn_up': nrm(ks[14], (DEPTH, 2, D_MODEL, D_FF), D_MODEL ** -0.5),
        'ffn_down': nrm(ks[15], (DEPTH, 2, D_FF, D_MODEL), DN_BETA * D_FF ** -0.5),
        'w_in': nrm(ks[16], (DEPTH, D_MODEL, D_IN), D_MODEL ** -0.5),
        'attn_sinks': nrm(ks[17], (DEPTH, N_HEADS_A), 0.5),
        'g_cq': 1.0 + nrm(ks[18], (DEPTH, Q_LORA), 0.02),
        'g_ckv': 1.0 + nrm(ks[19], (DEPTH, KV_LORA), 0.02),
        'w_uq': nrm(ks[20], (DEPTH, Q_LORA, N_HEADS_D * (NOPE_DIM + ROPE_DIM)), Q_LORA ** -0.5),
        'w_ukv': nrm(ks[21], (DEPTH, KV_LORA, N_HEADS_D * (NOPE_DIM + V_DIM_D)), KV_LORA ** -0.5),
        'w_o': nrm(ks[22], (DEPTH, D_MIX, D_MODEL), DN_BETA * D_MIX ** -0.5),
    }

def reference(x_prompt, x_sample, cache_a_k, cache_a_v, cache_b_k, cache_b_v, cache_b_kidx,
              cache_c_k, cache_c_v, cache_d_ckv, cache_d_krope,
              ln_g, ln_b, ffn_gate, ffn_up, ffn_down, w_in, attn_sinks, g_cq, g_ckv, w_uq, w_ukv, w_o):
    hp, hs = x_prompt, x_sample
    states_p, states_s = [], []
    for l in range(DEPTH):
        mix_w = (w_in[l], attn_sinks[l], g_cq[l], g_ckv[l], w_uq[l], w_ukv[l], w_o[l])
        caches = (cache_a_k[l], cache_a_v[l], cache_b_k[l], cache_b_v[l], cache_b_kidx[l],
                  cache_c_k[l], cache_c_v[l], cache_d_ckv[l], cache_d_krope[l])
        norm_ffn = (ln_g[l], ln_b[l], ffn_gate[l], ffn_up[l], ffn_down[l])
        hp, st_p = encoder_layer(hp, lambda h: mix_prompt(h, *mix_w), *norm_ffn)
        hs, st_s = encoder_layer(hs, lambda h: mix_step(h, caches, *mix_w), *norm_ffn)
        states_p.append(st_p)
        states_s.append(st_s)
    (a_k_p, a_v_p, b_k_p, b_v_p, b_i_p, c_k_p, c_v_p, d_l_p, d_r_p) = [jnp.stack(z) for z in zip(*states_p)]
    (a_k_s, a_v_s, b_k_s, b_v_s, b_i_s, c_k_s, c_v_s, d_l_s, d_r_s) = [jnp.stack(z) for z in zip(*states_s)]
    return (hp, hs,
            a_k_p, a_v_p, b_k_p, b_v_p, b_i_p, c_k_p, c_v_p, d_l_p, d_r_p,
            a_k_s, a_v_s, b_k_s, b_v_s, b_i_s, c_k_s, c_v_s, d_l_s, d_r_s)


_drawn_inputs = setup_inputs


def setup_inputs(seed=0):
    import zlib

    import numpy as np

    out = dict(_drawn_inputs(seed))
    spreads = {}
    factors = {'cache_c_k': 4.801,
     'cache_d_krope': 3.36,
     'attn_sinks': 54.134,
     'g_cq': 8.0,
     'g_ckv': 2.867}
    for name, (base, spread) in spreads.items():
        noise = np.random.default_rng([zlib.crc32(name.encode()), seed]).standard_normal(out[name].shape)
        drawn = base * np.exp(spread * noise) if base else spread * noise
        out[name] = __import__('jax').numpy.asarray(drawn.astype(out[name].dtype))
    for name, factor in factors.items():
        out[name] = (out[name] * factor).astype(out[name].dtype)
    return out
```

```python
from contextlib import ExitStack

import concourse.bass as bass
from concourse import mybir

ALU = mybir.AluOpType
ACT = mybir.ActivationFunctionType
F32 = mybir.dt.float32
F32R = mybir.dt.float32r
BF16 = mybir.dt.bfloat16
AX_X = mybir.AxisListType.X

P = 128
DEPTH = 2
D_MODEL, D_FF = 1024, 2816
SEQ, DEC, PAST = 256, 32, 128
TOK = SEQ + DEC
KEYS = TOK + PAST
SKEYS = PAST + DEC
KD = D_MODEL // P
KF = D_FF // P
HD = 64
Q_LORA, KV_LORA, ROPE_D = 256, 128, 32
V_A, V_B, V_C, W_I = 0, 128, 192, 448
V_TOK = 452
TOPK_PROMPT, TOPK_SAMPLE = min(256, SEQ // 4), min(256, SKEYS // 4)
DN_ALPHA = (2 * DEPTH) ** 0.25
LN_EPS, RMS_EPS = 1e-5, 1e-6
HIDE = -1e30
TAKEN = -3e38

CH = 2048
GU_CHUNKS = KF
DOWN_SPLIT = (8, 8, 6)
DOWN_CHUNKS = 4 * len(DOWN_SPLIT)
FFN_CHUNKS = GU_CHUNKS + DOWN_CHUNKS
TM_CHUNKS, FM_CHUNKS = 2, 9
MIX_CHUNKS = TM_CHUNKS + FM_CHUNKS + 1
WO_CHUNKS = 4
FFN0_AT, MIX_AT = 0, FFN_CHUNKS
WO_AT = MIX_AT + MIX_CHUNKS
FFN1_AT = WO_AT + WO_CHUNKS
LAYER_CHUNKS = FFN1_AT + FFN_CHUNKS
NRAW, NSPLIT = 3, 3
assert LAYER_CHUNKS % NRAW == 0 and LAYER_CHUNKS % NSPLIT == 0


def chunk_width(local):
    for at in (FFN0_AT, FFN1_AT):
        if at + GU_CHUNKS <= local < at + FFN_CHUNKS:
            return DOWN_SPLIT[(local - at - GU_CHUNKS) % 3] * 256
    if MIX_AT <= local < MIX_AT + TM_CHUNKS:
        return 4 * V_TOK
    if local == MIX_AT + TM_CHUNKS + FM_CHUNKS - 1:
        return 8 * P
    if local == WO_AT - 1:
        return 2 * 3 * P + 512
    return CH


QI, QB, QA, QC = 0, 2, 4, 6
KI, KB, KR, KA, CKV, KC = 0, 1, 2, 3, 4, 5
ROPE_PAIRS = (("q", QI), ("k", KI), ("q", QB), ("k", KR), ("q", QA))
RUN = ("A", "C", "D", "B")
WO_ROW = {"A": 0, "B": 1, "C": 2, "D": 3}


def encoder_program(nc, weights, x_in, ln_gb, rms_g, sinks, k_cache, v_cache, tables, mats, masks,
                    out_y, out_k, out_ka, out_v, out_vs, out_va):
    ctx = ExitStack()
    with ctx:
        at = [16512]

        def sb(name, shape, dt=F32, offset=None):
            size = 2 if dt == BF16 else 4
            n = size
            for d in shape[1:]:
                n *= d
            n = (n + 31) // 32 * 32
            if offset is None:
                offset = at[0]
                at[0] += n
            return nc.alloc_sbuf_tensor_at(name, shape, dt, offset=offset), offset + n

        raw, _ = sb("raw", [P, NRAW, CH])
        w_high, _ = sb("w_high", [P, NSPLIT, CH], F32R)
        w_low, _ = sb("w_low", [P, NSPLIT, CH], F32R)
        hT, _ = sb("hT", [P, KD, TOK])
        x_high, _ = sb("x_high", [P, KD, TOK], F32R)
        x_low, _ = sb("x_low", [P, KD, TOK], F32R)
        z_at = at[0]
        z, _ = sb("z", [P, KD, TOK])
        rope_x, e = sb("rope_x", [P, 2, 2, TOK], offset=z_at)
        rope_a, e = sb("rope_a", [P, 2, TOK], offset=e)
        rope_b, e = sb("rope_b", [P, 2, TOK], offset=e)
        c_z, _ = sb("c_z", [P, 1792], offset=z_at)
        tab, _ = sb("tab", [P, 2, 2, TOK])
        mat, _ = sb("mat", [P, 5, P])
        msk, _ = sb("msk", [P, 1056], BF16)
        gb, _ = sb("gb", [P, DEPTH, 3, 2, KD])
        rg, _ = sb("rg", [P, DEPTH, 3])
        snk, _ = sb("snk", [P, DEPTH, 9])
        eps, _ = sb("eps", [P, 1])
        zsq, _ = sb("zsq", [P, 2, TOK])
        zsum, _ = sb("zsum", [P, 2, TOK])
        zsqsum, _ = sb("zsqsum", [P, 2, TOK])
        msq, _ = sb("msq", [P, TOK])
        var, _ = sb("var", [P, TOK])
        rstd, _ = sb("rstd", [P, TOK])
        phase_at = at[0]
        hid_high, e = sb("hid_high", [P, KF, TOK], F32R, offset=phase_at)
        hid_low, e = sb("hid_low", [P, KF, TOK], F32R, offset=e)
        silu_g, e = sb("silu_g", [P, 2, TOK], offset=e)
        gated, e = sb("gated", [P, 2, TOK], offset=e)
        ends = [e]
        qT, e = sb("qT", [P, 8, TOK], offset=phase_at)
        kT, e = sb("kT", [P, 7, KEYS], offset=e)
        qd, e = sb("qd", [P, 3, TOK], offset=e)
        kd, e = sb("kd", [P, 2, KEYS], offset=e)
        cq_high, e = sb("cq_high", [P, 2, TOK], F32R, offset=e)
        cq_low, e = sb("cq_low", [P, 2, TOK], F32R, offset=e)
        ckv_high, e = sb("ckv_high", [P, KEYS], F32R, offset=e)
        ckv_low, e = sb("ckv_low", [P, KEYS], F32R, offset=e)
        v_tok, e = sb("v_tok", [P, 3, V_TOK], offset=e)
        v_past, e = sb("v_past", [P, 448], offset=e)
        v_d, e = sb("v_d", [P, 4, 256], offset=e)
        prob, e = sb("prob", [P, 2, 1792], offset=e)
        probT, e = sb("probT", [P, 1792], offset=e)
        relu_l, e = sb("relu_l", [P, 1024], offset=e)
        score, e = sb("score", [P, 128 + 256 + 160], offset=e)
        hide_b, e = sb("hide_b", [P, 128 + 256 + 160], BF16, offset=e)
        w_idx, e = sb("w_idx", [P, 3, 4], offset=e)
        best8, e = sb("best8", [P, 8], offset=e)
        top_s, e = sb("top_s", [P, 9], offset=e)
        neg_m, e = sb("neg_m", [P, 9], offset=e)
        sums, e = sb("sums", [P, 9], offset=e)
        sink_e, e = sb("sink_e", [P, 9], offset=e)
        recip, e = sb("recip", [P, 9], offset=e)
        ends.append(e)
        assert max(ends) <= 229344, ends
        ps = ctx.enter_context(nc.psum_tensor("ps", [P, 8, 512], F32))

        swap_r, swap_a, ident, ones, later = (mat[:, i, :] for i in range(5))
        m_blk0, m_a1, m_c1 = msk[:, 0:128], msk[:, 128:384], msk[:, 384:640]
        m_strict, id_bf = msk[:, 640:896], msk[:, 896:1024]
        zeros_bf, _ = sb("zeros_bf", [P, 160], BF16, offset=max(ends))
        rep_bf, _ = sb("rep_bf", [32, P], BF16, offset=max(ends) + 320)

        def sem(name):
            return ctx.enter_context(nc.semaphore(name))

        const_landed, x_landed, cache_landed = sem("const_landed"), sem("x_landed"), sem("cache_landed")
        raw_landed = [sem(f"raw_landed{i}") for i in range(NRAW)]
        high_ready, low_ready, chunk_used = sem("high_ready"), sem("low_ready"), sem("chunk_used")
        x_high_ready, x_low_ready = sem("x_high_ready"), sem("x_low_ready")
        silu_ready, gated_ready, hid_high_ready, hid_low_ready = (
            sem("silu_ready"), sem("gated_ready"), sem("hid_high_ready"), sem("hid_low_ready"))
        sums_ready_q = sem("sums_ready_q")
        z_ready, zsq_ready, sums_ready, stat_ready = sem("z_ready"), sem("zsq_ready"), sem("sums_ready"), sem("stat_ready")
        msq_ready, var_ready, rstd_ready, norm_ready = sem("msq_ready"), sem("var_ready"), sem("rstd_ready"), sem("norm_ready")
        tm_copied, proj_copied, swapped, roped = sem("tm_copied"), sem("proj_copied"), sem("swapped"), sem("roped")
        plain_copied, rms_sq, rms_sum, rms_rstd = sem("plain_copied"), sem("rms_sq"), sem("rms_sum"), sem("rms_rstd")
        rms_done, rms_high, rms_low = sem("rms_done"), sem("rms_high"), sem("rms_low")
        logits_ready, relu_ready, scored = sem("logits_ready"), sem("relu_ready"), sem("scored")
        d_proj, d_copied = sem("d_proj"), sem("d_copied")
        s_ready, max_ready, exp_ready, p_ready = sem("s_ready"), sem("max_ready"), sem("exp_ready"), sem("p_ready")
        t_ready, t_act, t_dve = sem("t_ready"), sem("t_act"), sem("t_dve")
        pv_ready, o_high, o_low = sem("pv_ready"), sem("o_high"), sem("o_low")
        c_copied, c_ln, c_soft, c_sum, c_w, c_a = (sem("c_copied"), sem("c_ln"), sem("c_soft"), sem("c_sum"),
                                                   sem("c_w"), sem("c_a"))
        topk_done = sem("topk_done")
        act_link, dve_link, pe_link, stored = sem("act_link"), sem("dve_link"), sem("pe_link"), sem("stored")

        def ge(eng, semaphore, value):
            if value > 0:
                eng.wait_ge(semaphore, value)

        def chunk(local):
            n = chunk_width(local)
            return raw[:, local % NRAW, 0:n], w_high[:, local % NSPLIT, 0:n], w_low[:, local % NSPLIT, 0:n]

        block = ctx.enter_context(nc.Block())

        @block.sync
        def _(sp):
            for pair in range(4):
                sp.dma_start(hT[:, 2 * pair:2 * pair + 2, :], x_in[:, 2 * pair:2 * pair + 2, :]).then_inc(x_landed, 16)
            for l in range(DEPTH):
                for local in range(LAYER_CHUNKS):
                    c = l * LAYER_CHUNKS + local
                    ge(sp, low_ready, c - NRAW + 1)
                    n = chunk_width(local)
                    sp.dma_start(raw[:, local % NRAW, 0:n], weights[l, local, :, 0:n]).then_inc(raw_landed[c % NRAW], 16)

        @block.gpsimd
        def _(pool):
            for dst, src in ((tab, tables), (mat, mats), (gb, ln_gb), (rg, rms_g), (snk, sinks)):
                pool.dma_start(dst[:], src).then_inc(const_landed, 16)
            pool.dma_start(msk[:, 0:1024], masks[:, 0:1024]).then_inc(const_landed, 16)
            pool.dma_start(zeros_bf[:, :], masks[:, 1024:1184]).then_inc(const_landed, 16)
            pool.dma_start(rep_bf[:, :], masks[0:32, 1184:1312]).then_inc(const_landed, 16)
            for l in range(DEPTH):
                pool.wait_ge(chunk_used, l * LAYER_CHUNKS + FFN_CHUNKS)
                pool.dma_start(kT[:, :, TOK:KEYS], k_cache[l]).then_inc(cache_landed, 16)
                pool.dma_start(v_past[:, :], v_cache[l]).then_inc(cache_landed, 16)
                pool.wait_ge(tm_copied, 3 * (l + 1))
                pool.dma_start(out_v[l], v_tok[:, 0:2, 0:448]).then_inc(stored, 16)
                pool.dma_start(out_vs[l], v_tok[0:32, 2, 0:448]).then_inc(stored, 16)
                pool.wait_ge(cache_landed, 32 * (l + 1))
                pool.dma_start(out_va[l], v_past[32:128, 0:128]).then_inc(stored, 16)
                pool.wait_ge(roped, 6 * l + 5)
                pool.wait_ge(rms_done, 2 * (l + 1))
                pool.wait_ge(plain_copied, 3 * (l + 1))
                pool.dma_start(out_k[l], kT[:, :, 0:TOK]).then_inc(stored, 16)
                pool.dma_start(out_ka[l], kT[:, KA, TOK + 32:KEYS]).then_inc(stored, 16)
                pool.wait_ge(stored, 5 * 16 * (l + 1))
            pool.wait_ge(x_high_ready, 4 * (3 * DEPTH + 1))
            pool.dma_start(out_y, hT[:, :, :]).then_inc(stored, 16)
            pool.wait_ge(stored, 5 * 16 * DEPTH + 16)

        @block.tensor
        def _(pe):
            links = [0]

            def link(mm):
                links[0] += 1
                mm.then_inc(pe_link, 1)
                pe.wait_ge(pe_link, links[0])

            def three(out, wh, wl, xh, xl, first, last):
                pe.matmul(out, wh, xh, start=first, stop=False, skip_group_check=True)
                pe.matmul(out, wh, xl, start=False, stop=False, skip_group_check=True)
                return pe.matmul(out, wl, xh, start=False, stop=last, skip_group_check=True)

            def ffn(l, i):
                f, base = 2 * l + i, (FFN0_AT, FFN1_AT)[i]
                event = 3 * l + (0, 2)[i]
                for t in range(GU_CHUNKS):
                    local = base + t
                    _, wh, wl = (a.rearrange("p (g k n) -> p g k n", g=2, k=KD) if a is not None else a
                                 for a in chunk(local))
                    pe.wait_ge(low_ready, l * LAYER_CHUNKS + local + 1)
                    ge(pe, gated_ready, f * KF + t - 1)
                    for k in range(KD):
                        if t == 0 and k % 2 == 0:
                            pe.wait_ge(x_low_ready, 4 * event + k // 2 + 1)
                        for g in range(2):
                            mm = three(ps[:, 2 * (t % 2) + g, 0:TOK], wh[:, g, k, :], wl[:, g, k, :],
                                       x_high[:, k, :], x_low[:, k, :], k == 0, k == KD - 1)
                    mm.then_inc(chunk_used, 1)
                for q in range(4):
                    ge(pe, z_ready, 4 * event + q - 1)
                    tile = 0
                    for third, n in enumerate(DOWN_SPLIT):
                        local = base + GU_CHUNKS + 3 * q + third
                        _, wh, wl = (a.rearrange("p (f n) -> p f n", f=n) for a in chunk(local))
                        pe.wait_ge(low_ready, l * LAYER_CHUNKS + local + 1)
                        for j in range(n):
                            if q == 0:
                                pe.wait_ge(hid_low_ready, f * KF + tile + 1)
                            for d in range(2):
                                mm = three(ps[:, 4 + 2 * (q % 2) + d, 0:TOK], wh[:, j, d * P:(d + 1) * P],
                                           wl[:, j, d * P:(d + 1) * P], hid_high[:, tile, :], hid_low[:, tile, :],
                                           tile == 0, tile == KF - 1)
                            tile += 1
                        mm.then_inc(chunk_used, 1)

            def stats(n):
                pe.wait_ge(sums_ready, n + 1)
                for j in range(2):
                    pe.matmul(ps[:, 2, 0:TOK], ones, zsum[:, j, :], start=(j == 0), stop=(j == 1))
                for j in range(2):
                    mm = pe.matmul(ps[:, 3, 0:TOK], ones, zsqsum[:, j, :], start=(j == 0), stop=(j == 1))
                mm.then_inc(stat_ready, 1)

            def swap(l, r):
                pe.wait_ge(proj_copied, 7 * l + r + 1)
                ge(pe, roped, 6 * l + r)
                for j in range(2):
                    m = swap_r if (r == 3 and j == 0) else swap_a
                    mm = pe.matmul(ps[:, 6 + j, 0:TOK], m, rope_x[:, r % 2, j, :], start=True, stop=True)
                mm.then_inc(swapped, 1)

            def head(h):
                return slice(64 * (h % 2), 64 * (h % 2) + 64)

            def indexer(l, g):
                ge(pe, relu_ready, 3 * l + g)
                if g == 0:
                    pe.wait_ge(roped, 6 * l + 2)
                else:
                    pe.wait_ge(cache_landed, 32 * (l + 1))
                for half in range(2):
                    for h in (half, half + 2):
                        q, k = qT[head(h), QI + h // 2, :], kT[head(h), KI, :]
                        if g == 0:
                            mm = pe.matmul(ps[:, 4 + h // 2, 256 * half:256 * half + 256], q[:, 128:256], k[:, 0:256],
                                           start=True, stop=True, skip_group_check=True)
                        if g == 1:
                            mm = pe.matmul(ps[:, 4, 128 * h:128 * h + 128], q[:, 0:128], k[:, 0:128],
                                           start=True, stop=True, skip_group_check=True)
                        if g == 1 + h // 2:
                            bank, at_ = 6 - g, SKEYS * half
                            pe.matmul(ps[0:32, bank, at_:at_ + PAST], q[:, SEQ:TOK], k[:, TOK:KEYS],
                                      start=True, stop=True, skip_group_check=True)
                            mm = pe.matmul(ps[0:32, bank, at_ + PAST:at_ + SKEYS], q[:, SEQ:TOK], k[:, SEQ:TOK],
                                           start=True, stop=True, skip_group_check=True)
                    if half == 0:
                        link(mm)
                mm.then_inc(logits_ready, 1)

            def scores(l, s, groups, mask1, mask0, mask_s):
                for b in range(2):
                    pe.matmul(ps[:, 2 + b, :], id_bf, bcast(mask1, 2), start=True, stop=False, skip_group_check=True)
                pe.matmul(ps[:, 4, :], id_bf, bcast(mask0, 4), start=True, stop=False, skip_group_check=True)
                mm = pe.matmul(ps[:, 5, 0:SKEYS], rep_bf[:, :], mask_s, start=True, stop=False, skip_group_check=True)
                for group in groups:
                    link(mm)
                    last = group is groups[-1]
                    for h, q, k in group:
                        pe.matmul(ps[:, 2 + h // 2, 256 * (h % 2):256 * (h % 2) + 256], q[:, 128:256], k[:, 0:256],
                                  start=False, stop=last, skip_group_check=True)
                        pe.matmul(ps[:, 4, 128 * h:128 * h + 128], q[:, 0:128], k[:, 0:128],
                                  start=False, stop=last, skip_group_check=True)
                        pe.matmul(ps[32 * h:32 * h + 32, 5, 0:PAST], q[:, SEQ:TOK], k[:, TOK:KEYS],
                                  start=False, stop=False, skip_group_check=True)
                        mm = pe.matmul(ps[32 * h:32 * h + 32, 5, PAST:SKEYS], q[:, SEQ:TOK], k[:, SEQ:TOK],
                                       start=False, stop=last, skip_group_check=True)
                mm.then_inc(s_ready, 1)

            def bcast(m, n):
                return m.rearrange("p (o k) -> p o k", o=1).to_broadcast([P, n, m.shape[-1]])

            def transposes(l, s):
                pe.wait_ge(p_ready, 3 * l + s + 1)
                pr = prob[:, s % 2, :]
                for g in range(4):
                    u = 4 * (3 * l + s) + g
                    ge(pe, (t_act, t_dve)[g % 2], u // 2)
                    bank = g % 2
                    if g < 3:
                        for h in range(4):
                            src = pr[:, 128 * h:128 * h + 128] if g == 0 else \
                                pr[:, 512 + 256 * h + 128 * (g - 1):512 + 256 * h + 128 * g]
                            mm = pe.transpose(ps[:, bank, 128 * h:128 * h + 128], src, ident)
                    else:
                        pe.transpose(ps[:, bank, 0:128], pr[:, 1536:1664], ident)
                        mm = pe.transpose(ps[0:32, bank, 128:256], pr[:, 1664:1696], ident)
                    mm.then_inc(t_ready, 1)

            def values(name, h):
                if name == "D":
                    c = slice(64 * h, 64 * h + 64)
                    return v_d[:, 0, c], v_d[:, 1, c], v_d[:, 3, c], v_d[0:32, 2, c]
                c = {"A": V_A + 64 * (h // 2), "B": V_B, "C": V_C + 64 * h}[name]
                c = slice(c, c + 64)
                return v_tok[:, 0, c], v_tok[:, 1, c], v_past[:, c], v_tok[0:32, 2, c]

            def weighted(l, run):
                name = RUN[run]
                ge(pe, o_low, 4 * l + run)
                if name == "C":
                    pe.wait_ge(c_a, l + 1)
                for h in range(4):
                    v0, v1, vp, vn = values(name, h)
                    o = ps[64 * (h % 2):64 * (h % 2) + 64, 6 + h // 2, :]
                    if name == "C":
                        a0, a1 = c_z[:, 256 * h:256 * h + 256], c_z[:, 1024 + 128 * h:1152 + 128 * h]
                        sp_, sn = c_z[:, 1536 + 32 * h:1568 + 32 * h], c_z[0:32, 1664 + 32 * h:1696 + 32 * h]
                        pe.matmul(o[:, 0:256], v0, a0, start=True, stop=False, skip_group_check=True)
                        pe.matmul(o[:, 128:256], v1, a1, start=False, stop=True, skip_group_check=True)
                    else:
                        if h == 0:
                            s = {"A": 0, "D": 1, "B": 2}[name]
                            u = 2 * (3 * l + s) + 2
                            pe.wait_ge(t_act, u)
                            pe.wait_ge(t_dve, u)
                        p0 = probT[:, 128 * h:128 * h + 128]
                        p10, p11 = (probT[:, 512 * (1 + b) + 128 * h:512 * (1 + b) + 128 * h + 128] for b in range(2))
                        sp_, sn = probT[:, 1536 + 32 * h:1568 + 32 * h], probT[0:32, 1664 + 32 * h:1696 + 32 * h]
                        pe.matmul(o[:, 0:128], v0, p0, start=True, stop=True, skip_group_check=True)
                        pe.matmul(o[:, 128:256], v0, p10, start=True, stop=False, skip_group_check=True)
                        pe.matmul(o[:, 128:256], v1, p11, start=False, stop=True, skip_group_check=True)
                    pe.matmul(o[:, 256:288], vp, sp_, start=True, stop=False, skip_group_check=True)
                    mm = pe.matmul(o[:, 256:288], vn, sn, start=False, stop=True, skip_group_check=True)
                mm.then_inc(pv_ready, 1)

            def heads_of(q0, k0, shared):
                return [[(h, qT[head(h), q0 + h // 2, :], kT[head(h), k0 if shared else k0 + h // 2, :])
                         for h in (half, half + 2)] for half in range(2)]

            groups_a = [[(h, qT[64 * g:64 * g + 64, QA + h % 2, :], kT[64 * g:64 * g + 64, KA, :])
                         for h in (2 * g, 2 * g + 1)] for g in range(2)]
            groups_d = [[(h, qd[head(h), h // 2, :], kd[head(h), h // 2, :]) for h in (half, half + 2)]
                        for half in range(2)] + \
                [[(h, qd[32 * h:32 * h + 32, 2, :], kT[32 * h:32 * h + 32, KR, :])] for h in range(4)]

            def mixer(l):
                event = 3 * l + 1
                for half in range(2):
                    local = MIX_AT + half
                    _, wh, wl = (a.rearrange("p (k n) -> p k n", k=4) for a in chunk(local))
                    pe.wait_ge(low_ready, l * LAYER_CHUNKS + local + 1)
                    for kk in range(4):
                        k = 4 * half + kk
                        if kk % 2 == 0:
                            pe.wait_ge(x_low_ready, 4 * event + k // 2 + 1)
                        for b, (lo, hi) in enumerate(((0, 128), (128, 256), (256, 288))):
                            out = ps[0:hi - lo, 4 + b, 0:V_TOK]
                            pe.matmul(out, x_high[:, k, lo:hi], wh[:, kk, :], start=(k == 0), stop=False, skip_group_check=True)
                            pe.matmul(out, x_low[:, k, lo:hi], wh[:, kk, :], start=False, stop=False, skip_group_check=True)
                            mm = pe.matmul(out, x_high[:, k, lo:hi], wl[:, kk, :], start=False, stop=(k == KD - 1),
                                           skip_group_check=True)
                    mm.then_inc(chunk_used, 1)
                for i in range(FM_CHUNKS):
                    local = MIX_AT + TM_CHUNKS + i
                    tiles = 1 if i == FM_CHUNKS - 1 else 2
                    _, wh, wl = (a.rearrange("p (k n) -> p k n", k=KD) for a in chunk(local))
                    pe.wait_ge(low_ready, l * LAYER_CHUNKS + local + 1)
                    if 2 <= i < 9:
                        pe.wait_ge(proj_copied, 7 * l + i - 1)
                    if i == 8:
                        pe.wait_ge(proj_copied, 7 * l + 7)
                        pe.wait_ge(rms_sq, 2 * l + 1)
                    for k in range(KD):
                        for j in range(tiles):
                            mm = three(ps[:, 2 * (i % 2) + j, 0:TOK], wh[:, k, j * P:(j + 1) * P],
                                       wl[:, k, j * P:(j + 1) * P], x_high[:, k, :], x_low[:, k, :],
                                       k == 0, k == KD - 1)
                    mm.then_inc(chunk_used, 1)
                    if i == 1:
                        pe.wait_ge(tm_copied, 3 * (l + 1))
                    if 1 <= i <= 5:
                        swap(l, i - 1)
                    if 3 <= i <= 5:
                        indexer(l, i - 3)
                    if i == 6 or i == 7:
                        r = i - 6
                        pe.wait_ge(rms_sq, 2 * l + r + 1)
                        pe.wait_ge(roped, 6 * l + 5)
                        for j in range(2 - r):
                            mm = pe.matmul(ps[:, 6 + r, 0:TOK], ones, zsq[:, j, :] if r == 0 else zsum[:, 0, :],
                                           start=(j == 0), stop=(j == 1 - r))
                        mm.then_inc(rms_sum, 1)
                pe.wait_ge(plain_copied, 3 * l + 2)
                pe.wait_ge(relu_ready, 3 * (l + 1))
                scores(l, 0, groups_a, m_a1, m_blk0, zeros_bf[0:32, :])
                local = WO_AT - 1
                _, wh, wl = chunk(local)
                uqh, uql = (a[:, 0:768].rearrange("p (k n) -> p k n", k=2) for a in (wh, wl))
                ukh, ukl = (a[:, 768:1280] for a in (wh, wl))
                pe.wait_ge(low_ready, l * LAYER_CHUNKS + local + 1)
                pe.wait_ge(rms_low, 2 * l + 2)
                pe.wait_ge(plain_copied, 3 * (l + 1))
                for j, bank in enumerate((0, 1, 6)):
                    for k in range(2):
                        mm = three(ps[:, bank, 0:TOK], uqh[:, k, j * P:(j + 1) * P], uql[:, k, j * P:(j + 1) * P],
                                   cq_high[:, k, :], cq_low[:, k, :], k == 0, k == 1)
                mm.then_inc(d_proj, 1)
                pe.wait_ge(d_copied, 4 * l + 1)
                pe.matmul(ps[:, 7, 0:TOK], swap_r, rope_x[:, 0, 0, :], start=True, stop=True).then_inc(swapped, 1)
                pe.wait_ge(d_copied, 4 * l + 2)
                for j in range(2):
                    mm = three(ps[:, j, 0:KEYS], ukh[:, j * P:(j + 1) * P], ukl[:, j * P:(j + 1) * P],
                               ckv_high[:, :], ckv_low[:, :], True, True)
                mm.then_inc(d_proj, 1)
                pe.wait_ge(roped, 6 * (l + 1))
                for b, lo in enumerate((0, 128, 256, 288)):
                    rows = 32 if b == 2 else 128
                    xh, xl = ckv_high[:, lo:lo + rows], ckv_low[:, lo:lo + rows]
                    out = ps[0:rows, 6 + b // 2, 256 * (b % 2):256 * (b % 2) + 256]
                    pe.matmul(out, xh, ukh[:, 256:512], start=True, stop=False, skip_group_check=True)
                    pe.matmul(out, xl, ukh[:, 256:512], start=False, stop=False, skip_group_check=True)
                    mm = pe.matmul(out, xh, ukl[:, 256:512], start=False, stop=True, skip_group_check=True)
                mm.then_inc(chunk_used, 1)
                pe.wait_ge(exp_ready, 3 * l + 1)
                for b in range(2):
                    pe.matmul(ps[:, 2 + b, :], id_bf, bcast(m_strict, 2), start=True, stop=False, skip_group_check=True)
                pe.matmul(ps[:, 4, :], id_bf, bcast(m_strict[:, 0:128], 4), start=True, stop=False, skip_group_check=True)
                pe.matmul(ps[:, 5, 0:128], id_bf, zeros_bf[:, 0:128], start=True, stop=False, skip_group_check=True)
                mm = pe.matmul(ps[:, 5, 128:256], id_bf, bcast(m_strict[:, 0:32], 4), start=False, stop=False,
                               skip_group_check=True)
                for half, group in enumerate(heads_of(QC, KC, False)):
                    link(mm)
                    for h, q, k in group:
                        pe.matmul(ps[:, 2 + h // 2, 256 * (h % 2):256 * (h % 2) + 256], k[:, 0:128], q[:, 0:256],
                                  start=False, stop=(half == 1), skip_group_check=True)
                        pe.matmul(ps[:, 4, 128 * h:128 * h + 128], k[:, 128:256], q[:, 128:256],
                                  start=False, stop=(half == 1), skip_group_check=True)
                        pe.matmul(ps[:, 5, 32 * h:32 * h + 32], k[:, TOK:KEYS], q[:, SEQ:TOK],
                                  start=False, stop=(half == 1), skip_group_check=True)
                        mm = pe.matmul(ps[0:32, 5, 128 + 32 * h:160 + 32 * h], k[:, SEQ:TOK], q[:, SEQ:TOK],
                                       start=False, stop=(half == 1), skip_group_check=True)
                mm.then_inc(c_sum, 1)
                pe.wait_ge(d_copied, 4 * (l + 1))
                transposes(l, 0)
                weighted(l, 0)
                pe.wait_ge(c_soft, l + 1)
                sp_ = prob[:, 1, :]
                for b in range(2):
                    pe.matmul(ps[:, 2 + b, :], later, sp_[:, 512 * b:512 * b + 512], start=True, stop=False,
                              skip_group_check=True)
                    for j in range(2):
                        pe.matmul(ps[:, 2 + b, 256 * j + 128:256 * j + 256], ones,
                                  sp_[:, 1024 + 128 * (2 * b + j):1152 + 128 * (2 * b + j)],
                                  start=False, stop=(j == 1), skip_group_check=True)
                pe.matmul(ps[:, 4, :], later, sp_[:, 1024:1536], start=True, stop=True)
                pe.matmul(ps[:, 5, 0:256], later, sp_[:, 1536:1792], start=True, stop=False, skip_group_check=True)
                pe.matmul(ps[:, 5, 0:128], ones, sp_[:, 1664:1792], start=False, stop=True,
                          skip_group_check=True).then_inc(c_sum, 1)
                pe.wait_ge(c_w, l + 1)
                scores(l, 1, groups_d, m_c1, m_blk0, zeros_bf[0:32, :])
                weighted(l, 1)
                pe.wait_ge(exp_ready, 3 * l + 2)
                pe.wait_ge(topk_done, l + 1)
                scores(l, 2, heads_of(QB, KB, True), hide_b[:, 128:384], hide_b[:, 0:128], hide_b[0:32, 384:544])
                transposes(l, 1)
                weighted(l, 2)
                transposes(l, 2)
                weighted(l, 3)
                for q in range(4):
                    local = WO_AT + q
                    _, wh, wl = (a.rearrange("p (k n) -> p k n", k=KD) for a in chunk(local))
                    pe.wait_ge(low_ready, l * LAYER_CHUNKS + local + 1)
                    ge(pe, z_ready, 4 * event + q - 1)
                    first = True
                    for run, name in enumerate(RUN):
                        pe.wait_ge(o_low, 4 * l + run + 1)
                        for k in (2 * WO_ROW[name], 2 * WO_ROW[name] + 1):
                            for d in range(2):
                                mm = three(ps[:, 4 + 2 * (q % 2) + d, 0:TOK], wh[:, k, d * P:(d + 1) * P],
                                           wl[:, k, d * P:(d + 1) * P], x_high[:, k, :], x_low[:, k, :],
                                           first, run == 3 and k % 2 == 1)
                            first = False
                    mm.then_inc(chunk_used, 1)

            pe.wait_ge(const_landed, 8 * 16)
            for l in range(DEPTH):
                ffn(l, 0)
                stats(3 * l)
                mixer(l)
                stats(3 * l + 1)
                ffn(l, 1)
                stats(3 * l + 2)

        @block.scalar
        def _(act):
            links = [0]

            def link(ins):
                links[0] += 1
                ins.then_inc(act_link, 1)
                act.wait_ge(act_link, links[0])

            split = [0]

            def high_until(n):
                while split[0] < min(n, DEPTH * LAYER_CHUNKS):
                    c = split[0]
                    local = c % LAYER_CHUNKS
                    r, wh, _ = chunk(local)
                    act.wait_ge(raw_landed[c % NRAW], 16 * (c // NRAW + 1))
                    ge(act, chunk_used, c - NSPLIT + 1)
                    act.activation(wh, r, ACT.Copy).then_inc(high_ready, 1)
                    split[0] += 1

            def ffn(l, i):
                f, base = 2 * l + i, l * LAYER_CHUNKS + (FFN0_AT, FFN1_AT)[i]

                def high(t):
                    act.wait_ge(gated_ready, f * KF + t + 1)
                    act.activation(hid_high[:, t, :], gated[:, t % 2, :], ACT.Copy).then_inc(hid_high_ready, 1)

                if i == 1:
                    act.wait_ge(stored, 80 * (l + 1))
                for t in range(GU_CHUNKS):
                    high_until(base + t + NSPLIT)
                    act.wait_ge(chunk_used, base + t + 1)
                    ge(act, gated_ready, f * KF + t - 1)
                    act.activation(silu_g[:, t % 2, :], ps[:, 2 * (t % 2), 0:TOK], ACT.Silu).then_inc(silu_ready, 1)
                    if t > 0:
                        high(t - 1)
                high(GU_CHUNKS - 1)
                for q in range(4):
                    for third in range(3):
                        high_until(base + GU_CHUNKS + 3 * q + third + NSPLIT)
                    square(3 * l + (0, 2)[i], q)

            def square(n, q):
                act.wait_ge(z_ready, 4 * n + q + 1)
                if q == 0:
                    act.activation(zsqsum[:, :, :], z[:, 0:2, :], ACT.Square).then_inc(zsq_ready, 1)
                else:
                    if q > 1:
                        act.wait_ge(sums_ready_q, 3 * n + q - 1)
                    act.activation(zsq[:, :, :], z[:, 2 * q:2 * q + 2, :], ACT.Square).then_inc(zsq_ready, 1)

            def norm(n):
                l, which = n // 3, n % 3
                act.wait_ge(stat_ready, n + 1)
                act.activation(msq[:, :], ps[:, 2, 0:TOK], ACT.Square, scale=1.0 / D_MODEL).then_inc(msq_ready, 1)
                act.wait_ge(var_ready, n + 1)
                link(act.activation(rstd[:, :], var[:, :], ACT.Ln))
                act.activation(rstd[:, :], rstd[:, :], ACT.Exp, scale=-0.5).then_inc(rstd_ready, 1)
                for pair in range(4):
                    act.wait_ge(norm_ready, 4 * n + pair + 1)
                    for j in (2 * pair, 2 * pair + 1):
                        last = act.activation(hT[:, j, :], z[:, j, :], ACT.Identity, bias=gb[:, l, which, 1, j:j + 1],
                                              scale=gb[:, l, which, 0, j:j + 1])
                        link(last)
                    act.activation(x_high[:, 2 * pair:2 * pair + 2, :], hT[:, 2 * pair:2 * pair + 2, :],
                                   ACT.Copy).then_inc(x_high_ready, 1)

            def softmax(l, s, scale):
                act.wait_ge(max_ready, 3 * l + s + 1)
                pr = prob[:, s % 2, :]
                for h in range(4):
                    act.activation(pr[:, 512 + 256 * h:768 + 256 * h], ps[:, 2 + h // 2, 256 * (h % 2):256 * (h % 2) + 256],
                                   ACT.Exp, bias=neg_m[:, 4 + h:5 + h], scale=scale, accum_out=sums[:, 4 + h:5 + h])
                for h in range(4):
                    act.activation(pr[:, 128 * h:128 * h + 128], ps[:, 4, 128 * h:128 * h + 128],
                                   ACT.Exp, bias=neg_m[:, h:h + 1], scale=scale, accum_out=sums[:, h:h + 1])
                if s == 0:
                    act.activation(sink_e[:, :], top_s[:, :], ACT.Exp)
                act.activation(pr[:, 1536:1696], ps[:, 5, 0:SKEYS], ACT.Exp, bias=neg_m[:, 8:9], scale=scale,
                               accum_out=sums[:, 8:9]).then_inc(exp_ready, 1)

            def copy_t(l, s):
                for g in (0, 2):
                    act.wait_ge(t_ready, 4 * (3 * l + s) + g + 1)
                    if g == 0 and s > 0:
                        act.wait_ge(pv_ready, 4 * l + (1, 1, 3)[s])
                    act.activation(probT[:, 512 * g // 1:512 * g + 512] if g == 0 else probT[:, 1024:1536],
                                   ps[:, 0, :], ACT.Copy).then_inc(t_act, 1)

            def out_high(l, run):
                act.wait_ge(pv_ready, 4 * l + run + 1)
                k = 2 * WO_ROW[RUN[run]]
                act.activation(x_high[:, k:k + 2, :], ps[:, 6:8, 0:TOK], ACT.Copy).then_inc(o_high, 1)

            def mixer(l):
                base = l * LAYER_CHUNKS + MIX_AT
                high_until(base + 1 + NSPLIT)
                act.wait_ge(chunk_used, base + 2)
                for b in range(3):
                    rows = 32 if b == 2 else 128
                    act.activation(v_tok[0:rows, b, :], ps[0:rows, 4 + b, 0:V_TOK], ACT.Copy).then_inc(tm_copied, 1)
                for b in range(3):
                    rows = 32 if b == 2 else 128
                    ins = act.activation(w_idx[0:rows, b, :], ps[0:rows, 4 + b, W_I:V_TOK], ACT.Copy, scale=1.0 / 16)
                link(ins)
                for i in range(FM_CHUNKS):
                    c = base + TM_CHUNKS + i
                    high_until(c + NSPLIT)
                    act.wait_ge(chunk_used, c + 1)
                    pair = ps[:, 2 * (i % 2):2 * (i % 2) + 2, 0:TOK]
                    if i < 5:
                        if i >= 2:
                            act.wait_ge(roped, 6 * l + i - 1)
                        act.activation(rope_x[:, i % 2, :, :], pair, ACT.Copy).then_inc(proj_copied, 1)
                    if i == 5:
                        act.wait_ge(roped, 6 * l + 4)
                        link(act.activation(zsq[:, :, :], pair, ACT.Square))
                        act.activation(rope_x[:, 1, :, :], pair, ACT.Copy).then_inc(rms_sq, 1)
                        act.sem_inc(proj_copied, 1)
                    if i == 6:
                        act.wait_ge(roped, 6 * l + 5)
                        act.activation(zsum[:, 0, :], pair[:, 0, :], ACT.Square).then_inc(rms_sq, 1)
                        act.activation(rope_x[:, 0, 0, :], pair[:, 0, :], ACT.Copy).then_inc(proj_copied, 1)
                        act.activation(kT[:, KC, 0:TOK], pair[:, 1, :], ACT.Copy).then_inc(plain_copied, 1)
                    if i == 7:
                        act.activation(kT[:, KC + 1, 0:TOK], pair[:, 0, :], ACT.Copy)
                        act.activation(qT[:, QC, :], pair[:, 1, :], ACT.Copy).then_inc(plain_copied, 1)
                    if i == 8:
                        act.activation(qT[:, QC + 1, :], pair[:, 0, :], ACT.Copy).then_inc(plain_copied, 1)
                    if 3 <= i <= 5:
                        g = i - 3
                        act.wait_ge(logits_ready, 3 * l + g + 1)
                        ge(act, scored, 3 * l + g)
                        if g == 0:
                            act.activation(relu_l[:, :], ps[:, 4:6, :], ACT.Relu).then_inc(relu_ready, 1)
                        if g == 1:
                            act.activation(relu_l[:, 0:512], ps[:, 4, :], ACT.Relu)
                            act.activation(relu_l[0:32, 512:832], ps[0:32, 5, 0:320], ACT.Relu).then_inc(relu_ready, 1)
                        if g == 2:
                            act.activation(relu_l[0:32, 0:320], ps[0:32, 4, 0:320], ACT.Relu).then_inc(relu_ready, 1)
                    if i >= 6 and i - 6 < 2:
                        r = i - 6
                        act.wait_ge(rms_sum, 2 * l + r + 1)
                        out = (msq, var)[r]
                        link(act.activation(out[:, :], ps[:, 6 + r, 0:TOK], ACT.Ln, bias=eps[:, :],
                                            scale=1.0 / (Q_LORA, KV_LORA)[r]))
                        act.activation(out[:, :], out[:, :], ACT.Exp, scale=-0.5).then_inc(rms_rstd, 1)
                act.wait_ge(rms_done, 2 * l + 1)
                act.activation(cq_high[:, :, :], rope_x[:, 1, :, :], ACT.Copy).then_inc(rms_high, 1)
                act.wait_ge(rms_done, 2 * l + 2)
                act.wait_ge(cache_landed, 32 * (l + 1))
                act.activation(ckv_high[:, :], kT[:, CKV, :], ACT.Copy).then_inc(rms_high, 1)
                high_until(base + MIX_CHUNKS - 1 + NSPLIT)
                softmax(l, 0, 0.125)
                act.wait_ge(d_proj, 2 * l + 1)
                act.activation(rope_x[:, 0, 0, :], ps[:, 6, 0:TOK], ACT.Copy).then_inc(d_copied, 1)
                act.activation(qd[:, 0:2, :], ps[:, 0:2, 0:TOK], ACT.Copy).then_inc(d_copied, 1)
                act.wait_ge(d_proj, 2 * l + 2)
                act.activation(kd[:, :, :], ps[:, 0:2, 0:KEYS], ACT.Copy).then_inc(d_copied, 1)
                act.wait_ge(chunk_used, base + MIX_CHUNKS)
                act.activation(v_d[:, 0:2, :], ps[:, 6, :], ACT.Copy)
                act.activation(v_d[0:32, 2, :], ps[0:32, 7, 0:256], ACT.Copy)
                act.activation(v_d[:, 3, :], ps[:, 7, 256:512], ACT.Copy).then_inc(d_copied, 1)
                act.wait_ge(c_sum, 2 * l + 1)
                act.wait_ge(roped, 6 * (l + 1))
                zc, ec = c_z[:, :], prob[:, 1, :]
                flat = ps[:, 2:6, :].rearrange("p b n -> p (b n)")[:, 0:1792]
                link(act.activation(zc, flat, ACT.Copy, scale=0.125))
                act.sem_inc(c_copied, 1)
                link(act.activation(ec, zc, ACT.Abs))
                link(act.activation(ec, ec, ACT.Exp, scale=-1.0))
                act.activation(ec, ec, ACT.Ln, bias=1.0).then_inc(c_ln, 1)
                high_until(base + MIX_CHUNKS + NSPLIT)
                copy_t(l, 0)
                out_high(l, 0)
                act.wait_ge(c_w, l + 1)
                act.activation(zc, zc, ACT.Exp).then_inc(c_a, 1)
                softmax(l, 1, 96 ** -0.5)
                out_high(l, 1)
                copy_t(l, 1)
                out_high(l, 2)
                softmax(l, 2, 0.125)
                copy_t(l, 2)
                out_high(l, 3)
                for q in range(4):
                    high_until(base + MIX_CHUNKS + q + NSPLIT)
                    square(3 * l + 1, q)

            for pair in range(4):
                act.wait_ge(x_landed, 64)
                act.activation(x_high[:, 2 * pair:2 * pair + 2, :], hT[:, 2 * pair:2 * pair + 2, :],
                               ACT.Copy).then_inc(x_high_ready, 1)
            act.wait_ge(const_landed, 8 * 16)
            for l in range(DEPTH):
                ffn(l, 0)
                norm(3 * l)
                mixer(l)
                norm(3 * l + 1)
                ffn(l, 1)
                norm(3 * l + 2)

        @block.vector
        def _(dve):
            links = [0]

            def link(ins):
                links[0] += 1
                ins.then_inc(dve_link, 1)
                dve.wait_ge(dve_link, links[0])

            split = [0]

            def low_until(n):
                while split[0] < min(n, DEPTH * LAYER_CHUNKS):
                    c = split[0]
                    r, wh, wl = chunk(c % LAYER_CHUNKS)
                    dve.wait_ge(high_ready, c + 1)
                    dve.tensor_tensor(wl, r, wh.bitcast(F32), ALU.subtract).then_inc(low_ready, 1)
                    split[0] += 1

            def ffn(l, i):
                f, base = 2 * l + i, l * LAYER_CHUNKS + (FFN0_AT, FFN1_AT)[i]

                def low(t):
                    dve.wait_ge(hid_high_ready, f * KF + t + 1)
                    dve.tensor_tensor(hid_low[:, t, :], gated[:, t % 2, :], hid_high[:, t, :].bitcast(F32),
                                      ALU.subtract).then_inc(hid_low_ready, 1)

                for t in range(GU_CHUNKS):
                    low_until(base + t + NSPLIT)
                    dve.wait_ge(silu_ready, f * KF + t + 1)
                    ge(dve, hid_low_ready, f * KF + t - 1)
                    dve.scalar_tensor_tensor(out=gated[:, t % 2, :], in0=silu_g[:, t % 2, :], scalar=0.5,
                                             in1=ps[:, 2 * (t % 2) + 1, 0:TOK], op0=ALU.mult, op1=ALU.mult)\
                       .then_inc(gated_ready, 1)
                    if t > 0:
                        low(t - 1)
                low(GU_CHUNKS - 1)
                for q in range(4):
                    for third in range(3):
                        low_until(base + GU_CHUNKS + 3 * q + third + NSPLIT)
                    residual(3 * l + (0, 2)[i], q, base + GU_CHUNKS + 3 * q + 3)

            def residual(n, q, used):
                dve.wait_ge(chunk_used, used)
                zq = z[:, 2 * q:2 * q + 2, :]
                dve.scalar_tensor_tensor(out=zq, in0=hT[:, 2 * q:2 * q + 2, :], scalar=DN_ALPHA,
                                         in1=ps[:, 4 + 2 * (q % 2):6 + 2 * (q % 2), 0:TOK],
                                         op0=ALU.mult, op1=ALU.add).then_inc(z_ready, 1)
                if q == 0:
                    return
                dve.wait_ge(z_ready, 4 * n + q + 1)
                link(dve.tensor_tensor(zsum[:, :, :], z[:, 0:2, :] if q == 1 else zsum[:, :, :], zq, ALU.add))
                dve.wait_ge(zsq_ready, 4 * n + q + 1)
                ins = dve.tensor_tensor(zsqsum[:, :, :], zsqsum[:, :, :], zsq[:, :, :], ALU.add)
                ins.then_inc(sums_ready_q, 1)
                dve.wait_ge(sums_ready_q, 3 * n + q)
                if q == 3:
                    dve.sem_inc(sums_ready, 1)

            def norm(n):
                dve.wait_ge(msq_ready, n + 1)
                link(dve.scalar_tensor_tensor(out=var[:, :], in0=ps[:, 3, 0:TOK], scalar=1.0 / D_MODEL, in1=msq[:, :],
                                              op0=ALU.mult, op1=ALU.subtract))
                dve.tensor_scalar(var[:, :], var[:, :], 0.0, LN_EPS, ALU.max, ALU.add).then_inc(var_ready, 1)
                mean = ps[:, 2:3, 0:TOK].to_broadcast([P, 2, TOK])
                for pair in range(4):
                    zq = z[:, 2 * pair:2 * pair + 2, :]
                    link(dve.scalar_tensor_tensor(out=zq, in0=mean, scalar=-1.0 / D_MODEL, in1=zq,
                                                  op0=ALU.mult, op1=ALU.add))
                dve.wait_ge(rstd_ready, n + 1)
                rs = rstd[:, :].rearrange("p (o t) -> p o t", o=1).to_broadcast([P, 2, TOK])

                def low(pair):
                    dve.wait_ge(x_high_ready, 4 * (n + 1) + pair + 1)
                    dve.tensor_tensor(x_low[:, 2 * pair:2 * pair + 2, :], hT[:, 2 * pair:2 * pair + 2, :],
                                      x_high[:, 2 * pair:2 * pair + 2, :].bitcast(F32), ALU.subtract)\
                       .then_inc(x_low_ready, 1)

                for pair in range(4):
                    zq = z[:, 2 * pair:2 * pair + 2, :]
                    dve.tensor_tensor(zq, zq, rs, ALU.mult).then_inc(norm_ready, 1)
                    if pair > 0:
                        low(pair - 1)
                low(3)

            def rope(l, r):
                kind, tile = ROPE_PAIRS[r]
                both = r == 3
                dst = qT[:, tile:tile + 2, :] if kind == "q" else kT[:, tile:tile + 2, 0:TOK]
                cos, sin = (tab[:, i, :, :] if both else tab[:, i, 1:2, :].to_broadcast([P, 2, TOK]) for i in range(2))
                dve.wait_ge(proj_copied, 7 * l + r + 1)
                link(dve.tensor_tensor(rope_a[:, :, :], rope_x[:, r % 2, :, :], cos, ALU.mult))
                dve.wait_ge(swapped, 6 * l + r + 1)
                link(dve.tensor_tensor(rope_b[:, :, :], ps[:, 6:8, 0:TOK], sin, ALU.mult))
                dve.tensor_tensor(dst, rope_a[:, :, :], rope_b[:, :, :], ALU.add).then_inc(roped, 1)
                dve.wait_ge(roped, 6 * l + r + 1)

            s_blk0, s_blk1, s_smp = score[:, 0:128], score[:, 128:384], score[0:32, 384:544]

            def weigh(l, out, mask, relu, h, b, rows, n):
                link(dve.scalar_tensor_tensor(out=out, in0=relu, scalar=w_idx[0:rows, b, h:h + 1],
                                              in1=mask if h == 0 else out, op0=ALU.mult, op1=ALU.add))

            def indexer(l, g):
                dve.wait_ge(relu_ready, 3 * l + g + 1)
                if g == 0:
                    for h in range(4):
                        weigh(l, s_blk1, m_c1, relu_l[:, 256 * h:256 * h + 256], h, 1, P, 256)
                if g == 1:
                    for h in range(4):
                        weigh(l, s_blk0, m_blk0, relu_l[:, 128 * h:128 * h + 128], h, 0, P, 128)
                    for h in range(2):
                        weigh(l, s_smp, zeros_bf[0:32, :], relu_l[0:32, 512 + 160 * h:672 + 160 * h], h, 2, 32, 160)
                if g == 2:
                    for h in range(2, 4):
                        weigh(l, s_smp, None, relu_l[0:32, 160 * (h - 2):160 * (h - 1)], h, 2, 32, 160)
                dve.sem_inc(scored, 1)

            def best(s, k):
                rows = s.shape[0]
                for _ in range(k // 8):
                    yield
                    link(dve.max(best8[0:rows, :], s))
                    link(dve.match_replace(s, best8[0:rows, :], s, TAKEN))

            def choose():
                yield from best(s_blk1, TOPK_PROMPT)
                yield from best(s_blk0, TOPK_PROMPT)
                yield from best(s_smp, TOPK_SAMPLE)
                yield
                for rows, a, b in ((P, 0, 128), (P, 128, 384), (32, 384, 544)):
                    link(dve.tensor_scalar(hide_b[0:rows, a:b], score[0:rows, a:b], TAKEN, HIDE,
                                           ALU.not_equal, ALU.mult))
                dve.sem_inc(topk_done, 1)

            def largest(l, s, scale):
                dve.wait_ge(s_ready, 3 * l + s + 1)
                dve.reduce_max(top_s[:, 4:8], ps[:, 2:4, :].rearrange("p b (h k) -> p (b h) k", h=2), AX_X)
                dve.reduce_max(top_s[:, 0:4], ps[:, 4, :].rearrange("p (h k) -> p h k", h=4), AX_X)
                link(dve.reduce_max(top_s[:, 8:9], ps[:, 5, 0:SKEYS], AX_X))
                if s == 0:
                    sk = snk[:, l, :]
                    link(dve.tensor_scalar(top_s[:, :], top_s[:, :], scale, None, ALU.mult))
                    link(dve.tensor_tensor(top_s[:, :], top_s[:, :], sk, ALU.max))
                    link(dve.tensor_scalar(neg_m[:, :], top_s[:, :], -1.0, None, ALU.mult))
                    link(dve.tensor_tensor(top_s[:, :], sk, neg_m[:, :], ALU.add))
                else:
                    link(dve.tensor_scalar(neg_m[:, :], top_s[:, :], -scale, None, ALU.mult))
                dve.sem_inc(max_ready, 1)

            def divide(l, s):
                dve.wait_ge(exp_ready, 3 * l + s + 1)
                if s == 0:
                    link(dve.tensor_tensor(sums[:, :], sums[:, :], sink_e[:, :], ALU.add))
                link(dve.reciprocal(recip[:, :], sums[:, :]))
                pr = prob[:, s % 2, :]
                for a, n in ((0, 128), (512, 256)):
                    v = pr[:, a:a + 4 * n].rearrange("p (h k) -> p h k", h=4)
                    r = recip[:, 4 * (a > 0):4 * (a > 0) + 4].rearrange("p (h o) -> p h o", o=1).to_broadcast([P, 4, n])
                    dve.tensor_tensor(v, v, r, ALU.mult)
                link(dve.tensor_scalar(pr[:, 1536:1696], pr[:, 1536:1696], recip[:, 8:9], None, ALU.mult))
                dve.sem_inc(p_ready, 1)

            def copy_t(l, s):
                for g in (1, 3):
                    dve.wait_ge(t_ready, 4 * (3 * l + s) + g + 1)
                    if g == 1:
                        if s > 0:
                            dve.wait_ge(pv_ready, 4 * l + (1, 1, 3)[s])
                        dve.tensor_copy(probT[:, 512:1024], ps[:, 1, :]).then_inc(t_dve, 1)
                    else:
                        link(dve.tensor_copy(probT[:, 1536:1664], ps[:, 1, 0:128]))
                        dve.tensor_copy(probT[0:32, 1664:1792], ps[0:32, 1, 128:256]).then_inc(t_dve, 1)

            def out_low(l, run):
                dve.wait_ge(o_high, 4 * l + run + 1)
                k = 2 * WO_ROW[RUN[run]]
                dve.tensor_tensor(x_low[:, k:k + 2, :], ps[:, 6:8, 0:TOK], x_high[:, k:k + 2, :].bitcast(F32),
                                  ALU.subtract).then_inc(o_low, 1)

            def mixer(l):
                base = l * LAYER_CHUNKS + MIX_AT
                low_until(base + 1 + NSPLIT)
                rounds = choose()
                for i in range(FM_CHUNKS):
                    low_until(base + TM_CHUNKS + i + NSPLIT)
                    if 1 <= i <= 5:
                        rope(l, i - 1)
                    if 3 <= i <= 5:
                        indexer(l, i - 3)
                    if i >= 6:
                        for _ in range(3):
                            next(rounds)
                dve.wait_ge(rms_rstd, 2 * l + 1)
                for j in range(2):
                    ins = dve.scalar_tensor_tensor(out=rope_x[:, 1, j, :], in0=rope_x[:, 1, j, :], scalar=rg[:, l, j:j + 1],
                                                   in1=msq[:, :], op0=ALU.mult, op1=ALU.mult)
                ins.then_inc(rms_done, 1)
                dve.wait_ge(rms_rstd, 2 * l + 2)
                dve.scalar_tensor_tensor(out=kT[:, CKV, 0:TOK], in0=rope_x[:, 0, 0, :], scalar=rg[:, l, 2:3],
                                         in1=var[:, :], op0=ALU.mult, op1=ALU.mult).then_inc(rms_done, 1)
                dve.wait_ge(rms_high, 2 * l + 1)
                dve.tensor_tensor(cq_low[:, :, :], rope_x[:, 1, :, :], cq_high[:, :, :].bitcast(F32),
                                  ALU.subtract).then_inc(rms_low, 1)
                dve.wait_ge(rms_high, 2 * l + 2)
                dve.tensor_tensor(ckv_low[:, :], kT[:, CKV, :], ckv_high[:, :].bitcast(F32),
                                  ALU.subtract).then_inc(rms_low, 1)
                low_until(base + MIX_CHUNKS - 1 + NSPLIT)
                largest(l, 0, 0.125)
                dve.wait_ge(d_copied, 4 * l + 1)
                link(dve.tensor_tensor(rope_a[:, 0, :], rope_x[:, 0, 0, :], tab[:, 0, 0, :], ALU.mult))
                dve.wait_ge(swapped, 6 * (l + 1))
                link(dve.tensor_tensor(rope_b[:, 0, :], ps[:, 7, 0:TOK], tab[:, 1, 0, :], ALU.mult))
                dve.tensor_tensor(qd[:, 2, :], rope_a[:, 0, :], rope_b[:, 0, :], ALU.add).then_inc(roped, 1)
                divide(l, 0)
                dve.wait_ge(c_ln, l + 1)
                dve.scalar_tensor_tensor(out=prob[:, 1, :], in0=c_z[:, :], scalar=0.0, in1=prob[:, 1, :],
                                         op0=ALU.max, op1=ALU.add).then_inc(c_soft, 1)
                low_until(base + MIX_CHUNKS + NSPLIT)
                copy_t(l, 0)
                out_low(l, 0)
                dve.wait_ge(c_sum, 2 * l + 2)
                flat = ps[:, 2:6, :].rearrange("p b n -> p (b n)")[:, 0:1792]
                dve.scalar_tensor_tensor(out=c_z[:, :], in0=flat, scalar=-1.0, in1=c_z[:, :],
                                         op0=ALU.mult, op1=ALU.add).then_inc(c_w, 1)
                for _ in rounds:
                    pass
                largest(l, 1, 96 ** -0.5)
                out_low(l, 1)
                divide(l, 1)
                copy_t(l, 1)
                out_low(l, 2)
                largest(l, 2, 0.125)
                divide(l, 2)
                copy_t(l, 2)
                out_low(l, 3)
                for q in range(4):
                    low_until(base + MIX_CHUNKS + q + NSPLIT)
                    residual(3 * l + 1, q, base + MIX_CHUNKS + q + 1)

            dve.memset(eps[:, :], RMS_EPS).then_inc(dve_link, 1)
            links[0] += 1
            for pair in range(4):
                dve.wait_ge(x_high_ready, pair + 1)
                dve.tensor_tensor(x_low[:, 2 * pair:2 * pair + 2, :], hT[:, 2 * pair:2 * pair + 2, :],
                                  x_high[:, 2 * pair:2 * pair + 2, :].bitcast(F32), ALU.subtract).then_inc(x_low_ready, 1)
            dve.wait_ge(const_landed, 8 * 16)
            for l in range(DEPTH):
                ffn(l, 0)
                norm(3 * l)
                mixer(l)
                norm(3 * l + 1)
                ffn(l, 1)
                norm(3 * l + 2)


def _pack_weights(ins, np):
    w = np.zeros((DEPTH, LAYER_CHUNKS, P, CH), np.float32)
    offs = {}
    at = 0
    for name, n in (("qa", 256), ("ka", 128), ("va", 128), ("qb", 256), ("kb", 64), ("vb", 64), ("qi", 256),
                    ("ki", 64), ("wi", 4), ("qc", 256), ("kc", 256), ("vc", 256), ("cq", 256), ("ckv", 128), ("kr", 32)):
        offs[name] = np.arange(at, at + n)
        at += n

    def heads(name, *hs):
        return np.concatenate([offs[name][64 * h:64 * h + 64] for h in hs])

    fm = [heads("qi", 0, 1), heads("qi", 2, 3), heads("ki", 0, 0), heads("kb", 0, 0), heads("qb", 0, 1),
          heads("qb", 2, 3), np.tile(offs["kr"], 4), offs["ka"], heads("qa", 0, 2), heads("qa", 1, 3),
          offs["cq"][0:128], offs["cq"][128:256], offs["ckv"], heads("kc", 0, 1), heads("kc", 2, 3),
          heads("qc", 0, 1), heads("qc", 2, 3)]
    tm = np.concatenate([offs["va"], offs["vb"], offs["vc"], offs["wi"]])

    def tiles(a, k):
        return a.reshape(k, P, -1).transpose(1, 0, 2).reshape(P, -1)

    for l in range(DEPTH):
        for i, base in enumerate((FFN0_AT, FFN1_AT)):
            g, u, d = ins["ffn_gate"][l, i], ins["ffn_up"][l, i], ins["ffn_down"][l, i]
            for t in range(KF):
                w[l, base + t, :, 0:1024] = tiles(g[:, t * P:(t + 1) * P], KD)
                w[l, base + t, :, 1024:2048] = tiles(u[:, t * P:(t + 1) * P], KD)
            for q in range(4):
                f = 0
                for third, n in enumerate(DOWN_SPLIT):
                    w[l, base + KF + 3 * q + third, :, 0:256 * n] = tiles(
                        d[f * P:(f + n) * P, 256 * q:256 * q + 256], n)
                    f += n
        win = ins["w_in"][l]
        for half in range(2):
            w[l, MIX_AT + half, :, 0:4 * V_TOK] = tiles(win[512 * half:512 * half + 512][:, tm], 4)
        for i in range(FM_CHUNKS):
            cols = np.concatenate(fm[2 * i:2 * i + 2])
            w[l, MIX_AT + 2 + i, :, 0:8 * len(cols)] = tiles(win[:, cols], KD)
        uq = ins["w_uq"][l].reshape(Q_LORA, 4, 96)
        uq = np.concatenate([uq[:, :, 0:64].reshape(Q_LORA, 256), uq[:, :, 64:96].reshape(Q_LORA, 128)], 1)
        ukv = ins["w_ukv"][l].reshape(KV_LORA, 4, 128)
        w[l, WO_AT - 1, :, 0:768] = tiles(uq, 2)
        w[l, WO_AT - 1, :, 768:1024] = ukv[:, :, 0:64].reshape(KV_LORA, 256)
        w[l, WO_AT - 1, :, 1024:1280] = ukv[:, :, 64:128].reshape(KV_LORA, 256)
        for q in range(4):
            w[l, WO_AT + q] = tiles(ins["w_o"][l][:, 256 * q:256 * q + 256], KD)
    return w


def _constants(np, bf16):
    pos = np.arange(TOK, dtype=np.float32)
    pos[SEQ:] += PAST - SEQ
    tab = np.zeros((P, 2, 2, TOK), np.float32)
    mats = np.zeros((P, 5, P), np.float32)
    for which, half in ((0, 16), (1, 32)):
        inv = np.power(np.float32(10000.0), -np.arange(half, dtype=np.float32) / np.float32(half)).astype(np.float32)
        p = np.arange(P)
        ang = (pos[None, :] * inv[p % half][:, None]).astype(np.float32).astype(np.float64)
        sign = np.where(p % (2 * half) < half, -1.0, 1.0)[:, None]
        tab[:, 0, which] = np.cos(ang)
        tab[:, 1, which] = sign * np.sin(ang)
        mats[p, which, np.where(p % (2 * half) < half, p + half, p - half)] = 1.0
    i = np.arange(P)
    mats[i, 2, i] = 1.0
    mats[:, 3, :] = 1.0
    mats[:, 4, :] = i[:, None] >= i[None, :]
    masks = np.zeros((P, 1312), np.float32)
    q0, q1, k = i[:, None], i[:, None] + 128, np.arange(256)[None, :]
    masks[:, 0:128] = np.where(k[:, 0:128] // 64 <= q0 // 64, 0.0, HIDE)
    masks[:, 128:384] = np.where((k // 64 <= q1 // 64) & (k // 64 >= q1 // 64 - 2), 0.0, HIDE)
    masks[:, 384:640] = np.where(k // 64 <= q1 // 64, 0.0, HIDE)
    masks[:, 640:896] = np.where(i[:, None] < k, 0.0, HIDE)
    masks[i, 896 + i] = 1.0
    for h in range(4):
        j = np.arange(32)
        masks[j, 1184 + 32 * h + j] = 1.0
    return tab, mats, masks.astype(bf16)


def kernel(**inputs):
    import ml_dtypes
    import numpy as np
    import concourse.bacc as bacc
    from concourse.bass_utils import run_bass_kernel_spmd

    ins = {k: np.asarray(v) for k, v in inputs.items()}
    tab, mats, masks = _constants(np, ml_dtypes.bfloat16)
    x = np.concatenate([ins["x_prompt"][0], ins["x_sample"][0]], 0)
    x = x.T.reshape(KD, P, TOK).transpose(1, 0, 2)
    gb = np.stack([ins["ln_g"], ins["ln_b"]], 2).reshape(DEPTH, 3, 2, KD, P).transpose(4, 0, 1, 2, 3)
    rg = np.concatenate([ins["g_cq"], ins["g_ckv"]], 1).reshape(DEPTH, 3, P).transpose(2, 0, 1)
    sink = ins["attn_sinks"]
    sinks = np.concatenate([np.broadcast_to(sink, (P, DEPTH, 4)), np.broadcast_to(sink, (P, DEPTH, 4)),
                            np.repeat(sink, 32, axis=1).T[:, :, None]], 2)
    bk, bi, kr = (ins[n][:, 0].transpose(0, 2, 1) for n in ("cache_b_k", "cache_b_kidx", "cache_d_krope"))
    ka = ins["cache_a_k"][:, 0].reshape(DEPTH, PAST, 128).transpose(0, 2, 1)
    kc = ins["cache_c_k"][:, 0].reshape(DEPTH, PAST, 256).transpose(0, 2, 1)
    k_cache = np.stack([np.tile(bi, (1, 2, 1)), np.tile(bk, (1, 2, 1)), np.tile(kr, (1, 4, 1)), ka,
                        ins["cache_d_ckv"][:, 0].transpose(0, 2, 1), kc[:, 0:128], kc[:, 128:256]], 2)
    v_cache = np.concatenate([ins["cache_a_v"][:, 0].reshape(DEPTH, PAST, 128), ins["cache_b_v"][:, 0],
                              ins["cache_c_v"][:, 0].reshape(DEPTH, PAST, 256)], 2)
    arrays = {"weights": _pack_weights(ins, np), "x_in": x, "ln_gb": gb, "rms_g": rg, "sinks": sinks,
              "k_cache": k_cache, "v_cache": v_cache, "tables": tab, "mats": mats, "masks": masks}
    arrays = {k: np.ascontiguousarray(v) for k, v in arrays.items()}
    outs = {"out_y": (P, KD, TOK), "out_k": (DEPTH, P, 7, TOK), "out_ka": (DEPTH, P, 96),
            "out_v": (DEPTH, P, 2, 448), "out_vs": (DEPTH, 32, 448), "out_va": (DEPTH, 96, 128)}
    nc = bacc.Bacc("TRN2", target_bir_lowering=False, num_devices=1)
    args = [nc.dram_tensor(k, v.shape, mybir.dt.from_np(v.dtype), kind="ExternalInput").ap() for k, v in arrays.items()]
    args += [nc.dram_tensor(k, s, F32, kind="ExternalOutput").ap() for k, s in outs.items()]
    encoder_program(nc, *args)
    r = run_bass_kernel_spmd(nc, [arrays], core_ids=[0]).results[0]

    y = r["out_y"].transpose(1, 0, 2).reshape(D_MODEL, TOK).T
    k = r["out_k"].transpose(0, 3, 2, 1)
    v = np.concatenate([r["out_v"].transpose(0, 2, 1, 3).reshape(DEPTH, SEQ, 448), r["out_vs"]], 1)
    ka_s = np.concatenate([r["out_ka"].transpose(0, 2, 1), k[:, SEQ:, KA]], 1)
    va_s = np.concatenate([r["out_va"], v[:, SEQ:, 0:128]], 1)

    def states(s, a_k, a_v):
        n = s.stop - s.start
        kc_ = k[:, s, KC:KC + 2].reshape(DEPTH, 1, n, 4, 64)
        return (a_k.reshape(DEPTH, 1, 128, 2, 64), a_v.reshape(DEPTH, 1, 128, 2, 64), k[:, None, s, KB, 0:64],
                v[:, None, s, V_B:V_B + 64], k[:, None, s, KI, 0:64], kc_,
                v[:, None, s, V_C:V_C + 256].reshape(DEPTH, 1, n, 4, 64), k[:, None, s, CKV], k[:, None, s, KR, 0:32])

    res = (y[None, 0:SEQ], y[None, SEQ:TOK]) \
        + states(slice(0, SEQ), k[:, 128:SEQ, KA], v[:, 128:SEQ, 0:128]) + states(slice(SEQ, TOK), ka_s, va_s)
    return tuple(np.ascontiguousarray(a) for a in res)
```

```python
from contextlib import ExitStack

import concourse.bass as bass
from concourse import mybir

ALU = mybir.AluOpType
ACT = mybir.ActivationFunctionType
F32 = mybir.dt.float32
F32R = mybir.dt.float32r
BF16 = mybir.dt.bfloat16
AX_X = mybir.AxisListType.X

P = 128
DEPTH = 2
D_MODEL, D_FF = 1024, 2816
SEQ, DEC, PAST = 256, 32, 128
TOK = SEQ + DEC
KEYS = TOK + PAST
SKEYS = PAST + DEC
KD = D_MODEL // P
KF = D_FF // P
HD = 64
Q_LORA, KV_LORA, ROPE_D = 256, 128, 32
V_A, V_B, V_C, W_I = 0, 128, 192, 448
V_TOK = 452
TOPK_PROMPT, TOPK_SAMPLE = min(256, SEQ // 4), min(256, SKEYS // 4)
DN_ALPHA = (2 * DEPTH) ** 0.25
LN_EPS, RMS_EPS = 1e-5, 1e-6
HIDE = -1e30
TAKEN = -3e38

CH = 2048
GU_CHUNKS = KF
DOWN_SPLIT = (8, 8, 6)
DOWN_CHUNKS = 4 * len(DOWN_SPLIT)
FFN_CHUNKS = GU_CHUNKS + DOWN_CHUNKS
TM_CHUNKS, FM_CHUNKS = 2, 9
MIX_CHUNKS = TM_CHUNKS + FM_CHUNKS + 1
WO_CHUNKS = 4
FFN0_AT, MIX_AT = 0, FFN_CHUNKS
WO_AT = MIX_AT + MIX_CHUNKS
FFN1_AT = WO_AT + WO_CHUNKS
LAYER_CHUNKS = FFN1_AT + FFN_CHUNKS
POOL_LOW = range(WO_AT + 1, FFN1_AT + 2)
NRAW, NSPLIT = 3, 3
assert LAYER_CHUNKS % NRAW == 0 and LAYER_CHUNKS % NSPLIT == 0


def chunk_width(local):
    for at in (FFN0_AT, FFN1_AT):
        if at + GU_CHUNKS <= local < at + FFN_CHUNKS:
            return DOWN_SPLIT[(local - at - GU_CHUNKS) % 3] * 256
    if MIX_AT <= local < MIX_AT + TM_CHUNKS:
        return 4 * V_TOK
    if local == MIX_AT + TM_CHUNKS + 7:
        return 8 * P
    if local == WO_AT - 1:
        return 2 * 3 * P + 512
    return CH


QI, QB, QA, QC = 0, 2, 4, 6
KI, KB, KR, KA, CKV, KC = 0, 1, 2, 3, 4, 5
ROPE_PAIRS = (("q", QI), ("k", KI), ("k", KR), ("q", QA), ("q", QB))
ROPE_CHUNKS = (0, 1, 4, 5, 8)
LATENT_Q, LATENT_KV, C_FIRST, C_LAST = 2, 3, 6, 7
RUN = ("A", "C", "D", "B")
WO_ROW = {"A": 0, "B": 1, "C": 2, "D": 3}
PV_BANK = (6, 0, 6, 6)
WO_PARTS = (("A", "C"), ("D", "B"))


def encoder_program(nc, weights, x_in, ln_gb, rms_g, sinks, k_cache, v_cache, tables, mats, masks,
                    out_y, out_k, out_ka, out_v, out_vs, out_va):
    ctx = ExitStack()
    with ctx:
        at = [16512]

        def sb(name, shape, dt=F32, offset=None):
            size = 2 if dt == BF16 else 4
            n = size
            for d in shape[1:]:
                n *= d
            n = (n + 31) // 32 * 32
            if offset is None:
                offset = at[0]
                at[0] += n
            return nc.alloc_sbuf_tensor_at(name, shape, dt, offset=offset), offset + n

        raw, _ = sb("raw", [P, NRAW, CH])
        w_high, _ = sb("w_high", [P, NSPLIT, CH], F32R)
        w_low, _ = sb("w_low", [P, NSPLIT, CH], F32R)
        hT, _ = sb("hT", [P, KD, TOK])
        x_high, _ = sb("x_high", [P, KD, TOK], F32R)
        x_low, _ = sb("x_low", [P, KD, TOK], F32R)
        z_at = at[0]
        z, _ = sb("z", [P, KD, TOK])
        rope_x, e = sb("rope_x", [P, 2, 2, TOK], offset=z_at)
        rope_a, e = sb("rope_a", [P, 2, TOK], offset=e)
        rope_b, e = sb("rope_b", [P, 2, TOK], offset=e)
        tab, _ = sb("tab", [P, 2, 2, TOK])
        mat, _ = sb("mat", [P, 5, P])
        msk, _ = sb("msk", [P, 1056], BF16)
        gb, _ = sb("gb", [P, DEPTH, 3, 2, KD])
        rg, _ = sb("rg", [P, DEPTH, 3])
        snk, _ = sb("snk", [P, DEPTH, 9])
        eps, _ = sb("eps", [P, 1])
        c_z, _ = sb("c_z", [P, 1792], offset=at[0])
        zsq, _ = sb("zsq", [P, 2, TOK])
        zsum, _ = sb("zsum", [P, 2, TOK])
        zsqsum, _ = sb("zsqsum", [P, 2, TOK])
        msq, _ = sb("msq", [P, TOK])
        var, _ = sb("var", [P, TOK])
        rstd, _ = sb("rstd", [P, TOK])
        phase_at = at[0]
        hid_high, e = sb("hid_high", [P, KF, TOK], F32R, offset=phase_at)
        hid_low, e = sb("hid_low", [P, KF, TOK], F32R, offset=e)
        silu_g, e = sb("silu_g", [P, 2, TOK], offset=e)
        gated, e = sb("gated", [P, 2, TOK], offset=e)
        ends = [e]
        qT, e = sb("qT", [P, 8, TOK], offset=phase_at)
        kT, e = sb("kT", [P, 7, KEYS], offset=e)
        qd, e = sb("qd", [P, 3, TOK], offset=e)
        kd, e = sb("kd", [P, 2, KEYS], offset=e)
        cq_x, e = sb("cq_x", [P, 2, TOK], offset=e)
        cq_high, e = sb("cq_high", [P, 2, TOK], F32R, offset=e)
        cq_low, e = sb("cq_low", [P, 2, TOK], F32R, offset=e)
        ckv_high, e = sb("ckv_high", [P, KEYS], F32R, offset=e)
        ckv_low, e = sb("ckv_low", [P, KEYS], F32R, offset=e)
        v_tok, e = sb("v_tok", [P, 3, V_TOK], offset=e)
        v_past, e = sb("v_past", [P, 448], offset=e)
        v_d, e = sb("v_d", [P, 4, 256], offset=e)
        prob, e = sb("prob", [P, 2, 1792], offset=e)
        probT, e = sb("probT", [P, 1792], offset=e)
        relu_l, e = sb("relu_l", [P, 1024], offset=e)
        score, e = sb("score", [P, 128 + 256 + 160], offset=e)
        hide_b, e = sb("hide_b", [P, 128 + 256 + 160], BF16, offset=e)
        w_idx, e = sb("w_idx", [P, 3, 4], offset=e)
        best8, e = sb("best8", [P, 8], offset=e)
        top_s, e = sb("top_s", [P, 9], offset=e)
        neg_m, e = sb("neg_m", [P, 9], offset=e)
        sums, e = sb("sums", [P, 9], offset=e)
        sink_e, e = sb("sink_e", [P, 9], offset=e)
        recip, e = sb("recip", [P, 9], offset=e)
        ends.append(e)
        assert max(ends) <= 229344, ends
        ps = ctx.enter_context(nc.psum_tensor("ps", [P, 8, 512], F32))

        swap_r, swap_a, ident, ones, later = (mat[:, i, :] for i in range(5))
        m_blk0, m_a1, m_c1 = msk[:, 0:128], msk[:, 128:384], msk[:, 384:640]
        m_strict, id_bf = msk[:, 640:896], msk[:, 896:1024]
        zeros_bf, _ = sb("zeros_bf", [P, 160], BF16, offset=max(ends))
        rep_bf, _ = sb("rep_bf", [32, P], BF16, offset=max(ends) + 320)

        def sem(name):
            return ctx.enter_context(nc.semaphore(name))

        const_landed, cache_landed = sem("const_landed"), sem("cache_landed")
        x_landed = [sem(f"x_landed{pair}") for pair in range(4)]
        first_landed = [sem(f"first_landed{part}") for part in range(4)]
        first_high, first_low, pool_link = sem("first_high"), sem("first_low"), sem("pool_link")
        h_ready, y_stored, tile6_ready, centered = sem("h_ready"), sem("y_stored"), sem("tile6_ready"), sem("centered")
        raw_landed = [sem(f"raw_landed{i}") for i in range(NRAW)]
        high_ready, low_ready, chunk_used = sem("high_ready"), sem("low_ready"), sem("chunk_used")
        x_high_ready, x_low_ready = sem("x_high_ready"), sem("x_low_ready")
        silu_ready, gated_ready, hid_high_ready, hid_low_ready = (
            sem("silu_ready"), sem("gated_ready"), sem("hid_high_ready"), sem("hid_low_ready"))
        zsq_added = sem("zsq_added")
        zsum_ready, zsqsum_ready = sem("zsum_ready"), sem("zsqsum_ready")
        z_ready, zsq_ready, stat_ready = sem("z_ready"), sem("zsq_ready"), sem("stat_ready")
        msq_ready, var_ready, rstd_ready, norm_ready = sem("msq_ready"), sem("var_ready"), sem("rstd_ready"), sem("norm_ready")
        tm_copied, proj_copied, swapped, roped = sem("tm_copied"), sem("proj_copied"), sem("swapped"), sem("roped")
        plain_copied, rms_sq, rms_sum, rms_rstd = sem("plain_copied"), sem("rms_sq"), sem("rms_sum"), sem("rms_rstd")
        rms_done, rms_high, rms_low = sem("rms_done"), sem("rms_high"), sem("rms_low")
        logits_ready, relu_ready, scored = sem("logits_ready"), sem("relu_ready"), sem("scored")
        d_proj, d_copied = sem("d_proj"), sem("d_copied")
        s_ready, max_ready, exp_ready, p_ready = sem("s_ready"), sem("max_ready"), sem("exp_ready"), sem("p_ready")
        t_ready, t_act, t_dve = sem("t_ready"), sem("t_act"), sem("t_dve")
        pv_ready, o_high, o_low = sem("pv_ready"), sem("o_high"), sem("o_low")
        c_copied, c_ln, c_soft, c_sum, c_w, c_a = (sem("c_copied"), sem("c_ln"), sem("c_soft"), sem("c_sum"),
                                                   sem("c_w"), sem("c_a"))
        topk_done = sem("topk_done")
        part_ready, part_added, wo_ready = sem("part_ready"), sem("part_added"), sem("wo_ready")
        act_link, dve_link, pe_link, stored = sem("act_link"), sem("dve_link"), sem("pe_link"), sem("stored")

        def ge(eng, semaphore, value):
            if value > 0:
                eng.wait_ge(semaphore, value)

        def first_part(chunk0, pair):
            return chunk0.rearrange("p (g k n) -> p g k n", g=2, k=KD)[:, :, 2 * pair:2 * pair + 2, :]

        def landed(c):
            return 16 * (c // NRAW + (c % NRAW > 0))

        def t_bank(s, g):
            return g if s == 2 else g % 2

        def chunk(local):
            n = chunk_width(local)
            return raw[:, local % NRAW, 0:n], w_high[:, local % NSPLIT, 0:n], w_low[:, local % NSPLIT, 0:n]

        block = ctx.enter_context(nc.Block())

        @block.sync
        def _(sp):
            for pair in range(4):
                sp.dma_start(first_part(raw[:, 0, :], pair), first_part(weights[0, 0], pair)).then_inc(first_landed[pair], 16)
                sp.dma_start(hT[:, 2 * pair:2 * pair + 2, :], x_in[:, 2 * pair:2 * pair + 2, :]).then_inc(x_landed[pair], 16)
            for l in range(DEPTH):
                for local in range(l == 0, LAYER_CHUNKS):
                    c = l * LAYER_CHUNKS + local
                    ge(sp, low_ready, c - NRAW + 1)
                    n = chunk_width(local)
                    sp.dma_start(raw[:, local % NRAW, 0:n], weights[l, local, :, 0:n]).then_inc(raw_landed[c % NRAW], 16)
            for pair in range(4):
                sp.wait_ge(h_ready, KD * (3 * DEPTH - 1) + 2 * pair + 2)
                sp.dma_start(out_y[:, 2 * pair:2 * pair + 2, :], hT[:, 2 * pair:2 * pair + 2, :]).then_inc(y_stored, 16)
            sp.wait_ge(y_stored, 4 * 16)

        @block.gpsimd
        def _(pool):
            pool.wait_ge(raw_landed[1], 16)
            for dst, src in ((tab, tables), (mat, mats), (gb, ln_gb), (rg, rms_g), (snk, sinks)):
                pool.dma_start(dst[:], src).then_inc(const_landed, 16)
            pool.dma_start(msk[:, 0:1024], masks[:, 0:1024]).then_inc(const_landed, 16)
            pool.dma_start(zeros_bf[:, :], masks[:, 1024:1184]).then_inc(const_landed, 16)
            pool.dma_start(rep_bf[:, :], masks[0:32, 1184:1312]).then_inc(const_landed, 16)
            links = [0]

            def link(ins):
                links[0] += 1
                ins.then_inc(pool_link, 1)
                pool.wait_ge(pool_link, links[0])

            def square_sums(n):
                for q in (1, 2):
                    pool.wait_ge(zsq_ready, 5 * n + q + 1)
                    pool.tensor_tensor(zsqsum[:, :, :], zsqsum[:, :, :], zsq[:, :, :], ALU.add).then_inc(zsq_added, 1)
                    pool.wait_ge(zsq_added, 2 * n + q)
                link(pool.tensor_tensor(zsqsum[:, 0, :], zsqsum[:, 0, :], zsqsum[:, 1, :], ALU.add))
                pool.wait_ge(zsq_ready, 5 * n + 4)
                pool.tensor_tensor(zsqsum[:, 0, :], zsqsum[:, 0, :], zsq[:, 0, :], ALU.add).then_inc(zsqsum_ready, 1)

            def low(l, local):
                c = l * LAYER_CHUNKS + local
                r, wh, wl = chunk(local)
                pool.wait_ge(low_ready, c)
                pool.wait_ge(high_ready, c + 1)
                pool.tensor_tensor(wl, r, wh.bitcast(F32), ALU.subtract).then_inc(low_ready, 1)

            for l in range(DEPTH):
                square_sums(3 * l)
                pool.wait_ge(chunk_used, l * LAYER_CHUNKS + FFN_CHUNKS)
                pool.dma_start(kT[:, :, TOK:KEYS], k_cache[l]).then_inc(cache_landed, 16)
                pool.dma_start(v_past[:, :], v_cache[l]).then_inc(cache_landed, 16)
                pool.wait_ge(tm_copied, 3 * (l + 1))
                pool.dma_start(out_v[l], v_tok[:, 0:2, 0:448]).then_inc(stored, 16)
                pool.dma_start(out_vs[l], v_tok[0:32, 2, 0:448]).then_inc(stored, 16)
                pool.wait_ge(cache_landed, 32 * (l + 1))
                pool.dma_start(out_va[l], v_past[32:128, 0:128]).then_inc(stored, 16)
                pool.wait_ge(roped, 6 * l + 3)
                pool.wait_ge(rms_done, 2 * (l + 1))
                pool.wait_ge(proj_copied, FM_CHUNKS * l + C_LAST + 1)
                pool.dma_start(out_k[l], kT[:, :, 0:TOK]).then_inc(stored, 16)
                pool.dma_start(out_ka[l], kT[:, KA, TOK + 32:KEYS]).then_inc(stored, 16)
                for local in POOL_LOW[:-1]:
                    low(l, local)
                square_sums(3 * l + 1)
                low(l, POOL_LOW[-1])
                pool.wait_ge(stored, 5 * 16 * (l + 1))
                square_sums(3 * l + 2)

        @block.tensor
        def _(pe):
            links = [0]

            def link(mm):
                links[0] += 1
                mm.then_inc(pe_link, 1)
                pe.wait_ge(pe_link, links[0])

            def three(out, wh, wl, xh, xl, first, last):
                pe.matmul(out, wh, xh, start=first, stop=False, skip_group_check=True)
                pe.matmul(out, wh, xl, start=False, stop=False, skip_group_check=True)
                return pe.matmul(out, wl, xh, start=False, stop=last, skip_group_check=True)

            def ffn(l, i):
                f, base = 2 * l + i, (FFN0_AT, FFN1_AT)[i]
                event = 3 * l + (0, 2)[i]

                def gate_up(t, k):
                    _, wh, wl = (a.rearrange("p (g k n) -> p g k n", g=2, k=KD) for a in chunk(base + t))
                    if l == i == t == 0:
                        if k < 6:
                            pe.wait_ge(first_low, k // 2 + 1)
                        else:
                            pe.wait_ge(low_ready, 1)
                    elif k == 0:
                        pe.wait_ge(low_ready, l * LAYER_CHUNKS + base + t + 1)
                    if k == 0:
                        ge(pe, gated_ready, f * KF + t - 1)
                    for g in range(2):
                        mm = three(ps[:, 6 * (t % 2) + g, 0:TOK], wh[:, g, k, :], wl[:, g, k, :],
                                   x_high[:, k, :], x_low[:, k, :], k == 0, k == KD - 1)
                    if k == KD - 1:
                        mm.then_inc(chunk_used, 1)

                for k in range(KD):
                    pe.wait_ge(x_low_ready, KD * event + k + 1)
                    gate_up(0, k)
                    if event > 0:
                        gate_up(1, k)
                for t in range(1 + (event > 0), GU_CHUNKS):
                    for k in range(KD):
                        gate_up(t, k)
                for q in range(4):
                    ge(pe, z_ready, 5 * event + q - 1)
                    tile = 0
                    for third, n in enumerate(DOWN_SPLIT):
                        local = base + GU_CHUNKS + 3 * q + third
                        _, wh, wl = (a.rearrange("p (f n) -> p f n", f=n) for a in chunk(local))
                        pe.wait_ge(low_ready, l * LAYER_CHUNKS + local + 1)
                        order = [(j, d) for j in range(n) for d in range(2)]
                        if q == 3 and third == 2:
                            order.sort(key=lambda jd: jd[1])
                        for j, d in order:
                            if q == 3 and third == 2 and (j, d) == (n - 1, 1):
                                stats_most(event)
                            if q == 0 and d == 0:
                                pe.wait_ge(hid_low_ready, f * KF + tile + j + 1)
                            mm = three(ps[:, 4 + 2 * (q % 2) + d, 0:TOK], wh[:, j, d * P:(d + 1) * P],
                                       wl[:, j, d * P:(d + 1) * P], hid_high[:, tile + j, :], hid_low[:, tile + j, :],
                                       tile + j == 0, tile + j == KF - 1)
                            if q == 3 and third == 2 and d == 0 and j == n - 1:
                                mm.then_inc(tile6_ready, 1)
                        tile += n
                        mm.then_inc(chunk_used, 1)

            def stats_most(n):
                if n == 0:
                    pe.wait_ge(const_landed, 8 * 16)
                pe.wait_ge(zsum_ready, n + 1)
                pe.matmul(ps[:, 2, 0:TOK], ones, zsum[:, 0, :], start=True, stop=False)

            def stats_rest(n):
                pe.wait_ge(zsqsum_ready, n + 1)
                pe.matmul(ps[:, 3, 0:TOK], ones, zsqsum[:, 0, :], start=True, stop=False)
                pe.wait_ge(z_ready, 5 * (n + 1))
                pe.matmul(ps[:, 2, 0:TOK], ones, z[:, 7, :], start=False, stop=True)
                pe.wait_ge(zsq_ready, 5 * (n + 1))
                pe.matmul(ps[:, 3, 0:TOK], ones, zsq[:, 1, :], start=False, stop=True).then_inc(stat_ready, 1)

            def swap(l, r):
                pe.wait_ge(proj_copied, FM_CHUNKS * l + ROPE_CHUNKS[r] + 1)
                ge(pe, roped, 6 * l + r)
                for j in range(2):
                    m = swap_r if (r == 2 and j == 0) else swap_a
                    mm = pe.matmul(ps[:, 6 + j, 0:TOK], m, rope_x[:, r % 2, j, :], start=True, stop=True)
                mm.then_inc(swapped, 1)

            def head(h):
                return slice(64 * (h % 2), 64 * (h % 2) + 64)

            def indexer(l, g):
                ge(pe, relu_ready, 3 * l + g)
                if g == 0:
                    pe.wait_ge(roped, 6 * l + 2)
                else:
                    pe.wait_ge(cache_landed, 32 * (l + 1))
                for half in range(2):
                    for h in (half, half + 2):
                        q, k = qT[head(h), QI + h // 2, :], kT[head(h), KI, :]
                        if g == 0:
                            mm = pe.matmul(ps[:, 4 + h // 2, 256 * half:256 * half + 256], q[:, 128:256], k[:, 0:256],
                                           start=True, stop=True, skip_group_check=True)
                        if g == 1:
                            mm = pe.matmul(ps[:, 4, 128 * h:128 * h + 128], q[:, 0:128], k[:, 0:128],
                                           start=True, stop=True, skip_group_check=True)
                        if g == 1 + h // 2:
                            bank, at_ = 6 - g, SKEYS * half
                            pe.matmul(ps[0:32, bank, at_:at_ + PAST], q[:, SEQ:TOK], k[:, TOK:KEYS],
                                      start=True, stop=True, skip_group_check=True)
                            mm = pe.matmul(ps[0:32, bank, at_ + PAST:at_ + SKEYS], q[:, SEQ:TOK], k[:, SEQ:TOK],
                                           start=True, stop=True, skip_group_check=True)
                    if half == 0:
                        link(mm)
                mm.then_inc(logits_ready, 1)

            def scores(l, s, groups, mask1, mask0, mask_s):
                for b in range(2):
                    pe.matmul(ps[:, 2 + b, :], id_bf, bcast(mask1, 2), start=True, stop=False, skip_group_check=True)
                pe.matmul(ps[:, 4, :], id_bf, bcast(mask0, 4), start=True, stop=False, skip_group_check=True)
                mm = pe.matmul(ps[:, 5, 0:SKEYS], rep_bf[:, :], mask_s, start=True, stop=False, skip_group_check=True)
                for group in groups:
                    link(mm)
                    last = group is groups[-1]
                    for h, q, k in group:
                        pe.matmul(ps[:, 2 + h // 2, 256 * (h % 2):256 * (h % 2) + 256], q[:, 128:256], k[:, 0:256],
                                  start=False, stop=last, skip_group_check=True)
                        pe.matmul(ps[:, 4, 128 * h:128 * h + 128], q[:, 0:128], k[:, 0:128],
                                  start=False, stop=last, skip_group_check=True)
                        pe.matmul(ps[32 * h:32 * h + 32, 5, 0:PAST], q[:, SEQ:TOK], k[:, TOK:KEYS],
                                  start=False, stop=False, skip_group_check=True)
                        mm = pe.matmul(ps[32 * h:32 * h + 32, 5, PAST:SKEYS], q[:, SEQ:TOK], k[:, SEQ:TOK],
                                       start=False, stop=last, skip_group_check=True)
                mm.then_inc(s_ready, 1)

            def bcast(m, n):
                return m.rearrange("p (o k) -> p o k", o=1).to_broadcast([P, n, m.shape[-1]])

            def transposes(l, s):
                pe.wait_ge(p_ready, 3 * l + s + 1)
                pr = prob[:, s % 2, :]
                for g in range(4):
                    u = 4 * (3 * l + s) + g
                    if s < 2 or g < 2:
                        ge(pe, (t_act, t_dve)[g % 2], u // 2)
                    bank = t_bank(s, g)
                    if g < 3:
                        for h in range(4):
                            src = pr[:, 128 * h:128 * h + 128] if g == 0 else \
                                pr[:, 512 + 256 * h + 128 * (g - 1):512 + 256 * h + 128 * g]
                            mm = pe.transpose(ps[:, bank, 128 * h:128 * h + 128], src, ident)
                    else:
                        pe.transpose(ps[:, bank, 0:128], pr[:, 1536:1664], ident)
                        mm = pe.transpose(ps[0:32, bank, 128:256], pr[:, 1664:1696], ident)
                    mm.then_inc(t_ready, 1)

            def values(name, h):
                if name == "D":
                    c = slice(64 * h, 64 * h + 64)
                    return v_d[:, 0, c], v_d[:, 1, c], v_d[:, 3, c], v_d[0:32, 2, c]
                c = {"A": V_A + 64 * (h // 2), "B": V_B, "C": V_C + 64 * h}[name]
                c = slice(c, c + 64)
                return v_tok[:, 0, c], v_tok[:, 1, c], v_past[:, c], v_tok[0:32, 2, c]

            def weighted(l, run):
                name = RUN[run]
                if name == "C":
                    pe.wait_ge(c_a, l + 1)
                for h in range(4):
                    v0, v1, vp, vn = values(name, h)
                    o = ps[64 * (h % 2):64 * (h % 2) + 64, PV_BANK[run] + h // 2, :]
                    if name == "C":
                        a0, a1 = c_z[:, 256 * h:256 * h + 256], c_z[:, 1024 + 128 * h:1152 + 128 * h]
                        sp_, sn = c_z[:, 1536 + 32 * h:1568 + 32 * h], c_z[0:32, 1664 + 32 * h:1696 + 32 * h]
                        pe.matmul(o[:, 0:256], v0, a0, start=True, stop=False, skip_group_check=True)
                        pe.matmul(o[:, 128:256], v1, a1, start=False, stop=True, skip_group_check=True)
                    else:
                        if h == 0:
                            s = {"A": 0, "D": 1, "B": 2}[name]
                            u = 2 * (3 * l + s) + 2
                            pe.wait_ge(t_act, u)
                            pe.wait_ge(t_dve, u)
                        p0 = probT[:, 128 * h:128 * h + 128]
                        p10, p11 = (probT[:, 512 * (1 + b) + 128 * h:512 * (1 + b) + 128 * h + 128] for b in range(2))
                        sp_, sn = probT[:, 1536 + 32 * h:1568 + 32 * h], probT[0:32, 1664 + 32 * h:1696 + 32 * h]
                        pe.matmul(o[:, 0:128], v0, p0, start=True, stop=True, skip_group_check=True)
                        pe.matmul(o[:, 128:256], v0, p10, start=True, stop=False, skip_group_check=True)
                        pe.matmul(o[:, 128:256], v1, p11, start=False, stop=True, skip_group_check=True)
                    pe.matmul(o[:, 256:288], vp, sp_, start=True, stop=False, skip_group_check=True)
                    mm = pe.matmul(o[:, 256:288], vn, sn, start=False, stop=True, skip_group_check=True)
                mm.then_inc(pv_ready, 1)

            def heads_of(q0, k0, shared):
                return [[(h, qT[head(h), q0 + h // 2, :], kT[head(h), k0 if shared else k0 + h // 2, :])
                         for h in (half, half + 2)] for half in range(2)]

            groups_a = [[(h, qT[64 * g:64 * g + 64, QA + h % 2, :], kT[64 * g:64 * g + 64, KA, :])
                         for h in (2 * g, 2 * g + 1)] for g in range(2)]
            groups_d = [[(h, qd[head(h), h // 2, :], kd[head(h), h // 2, :]) for h in (half, half + 2)]
                        for half in range(2)] + \
                [[(h, qd[32 * h:32 * h + 32, 2, :], kT[32 * h:32 * h + 32, KR, :])] for h in range(4)]

            def mixer(l):
                event = 3 * l + 1
                for half in range(2):
                    local = MIX_AT + half
                    _, wh, wl = (a.rearrange("p (k n) -> p k n", k=4) for a in chunk(local))
                    pe.wait_ge(low_ready, l * LAYER_CHUNKS + local + 1)
                    for kk in range(4):
                        k = 4 * half + kk
                        pe.wait_ge(x_low_ready, KD * event + k + 1)
                        for b, (lo, hi) in enumerate(((0, 128), (128, 256), (256, 288))):
                            out = ps[0:hi - lo, 4 + b, 0:V_TOK]
                            pe.matmul(out, x_high[:, k, lo:hi], wh[:, kk, :], start=(k == 0), stop=False, skip_group_check=True)
                            pe.matmul(out, x_low[:, k, lo:hi], wh[:, kk, :], start=False, stop=False, skip_group_check=True)
                            mm = pe.matmul(out, x_high[:, k, lo:hi], wl[:, kk, :], start=False, stop=(k == KD - 1),
                                           skip_group_check=True)
                    mm.then_inc(chunk_used, 1)
                for i in range(FM_CHUNKS):
                    local = MIX_AT + TM_CHUNKS + i
                    tiles = chunk_width(local) // (KD * P)
                    _, wh, wl = (a.rearrange("p (k n) -> p k n", k=KD) for a in chunk(local))
                    pe.wait_ge(low_ready, l * LAYER_CHUNKS + local + 1)
                    if i >= 2:
                        pe.wait_ge(proj_copied, FM_CHUNKS * l + i - 1)
                    for k in range(KD):
                        for j in range(tiles):
                            mm = three(ps[:, 2 * (i % 2) + j, 0:TOK], wh[:, k, j * P:(j + 1) * P],
                                       wl[:, k, j * P:(j + 1) * P], x_high[:, k, :], x_low[:, k, :],
                                       k == 0, k == KD - 1)
                    mm.then_inc(chunk_used, 1)
                    if i == 1:
                        pe.wait_ge(tm_copied, 3 * (l + 1))
                        swap(l, 0)
                    if i == 2:
                        swap(l, 1)
                    if 3 <= i <= 5:
                        indexer(l, i - 3)
                    if i == 3 or i == 4:
                        r = i - 3
                        pe.wait_ge(rms_sq, 2 * l + r + 1)
                        pe.wait_ge(roped, 6 * l + 2)
                        for j in range(2 - r):
                            mm = pe.matmul(ps[:, 6 + r, 0:TOK], ones, zsq[:, j, :] if r == 0 else zsum[:, 0, :],
                                           start=(j == 0), stop=(j == 1 - r))
                        mm.then_inc(rms_sum, 1)
                    if i == 5:
                        pe.wait_ge(rms_rstd, 2 * (l + 1))
                        swap(l, 2)
                    if i == 6:
                        swap(l, 3)
                pe.wait_ge(proj_copied, FM_CHUNKS * l + C_LAST + 1)
                pe.wait_ge(relu_ready, 3 * (l + 1))
                for b in range(2):
                    pe.matmul(ps[:, 2 + b, :], id_bf, bcast(m_strict, 2), start=True, stop=False, skip_group_check=True)
                pe.matmul(ps[:, 4, :], id_bf, bcast(m_strict[:, 0:128], 4), start=True, stop=False, skip_group_check=True)
                pe.matmul(ps[:, 5, 0:128], id_bf, zeros_bf[:, 0:128], start=True, stop=False, skip_group_check=True)
                mm = pe.matmul(ps[:, 5, 128:256], id_bf, bcast(m_strict[:, 0:32], 4), start=False, stop=False,
                               skip_group_check=True)
                for half, group in enumerate(heads_of(QC, KC, False)):
                    link(mm)
                    for h, q, k in group:
                        pe.matmul(ps[:, 2 + h // 2, 256 * (h % 2):256 * (h % 2) + 256], k[:, 0:128], q[:, 0:256],
                                  start=False, stop=(half == 1), skip_group_check=True)
                        pe.matmul(ps[:, 4, 128 * h:128 * h + 128], k[:, 128:256], q[:, 128:256],
                                  start=False, stop=(half == 1), skip_group_check=True)
                        pe.matmul(ps[:, 5, 32 * h:32 * h + 32], k[:, TOK:KEYS], q[:, SEQ:TOK],
                                  start=False, stop=(half == 1), skip_group_check=True)
                        mm = pe.matmul(ps[0:32, 5, 128 + 32 * h:160 + 32 * h], k[:, SEQ:TOK], q[:, SEQ:TOK],
                                       start=False, stop=(half == 1), skip_group_check=True)
                mm.then_inc(c_sum, 1)
                swap(l, 4)
                local = WO_AT - 1
                _, wh, wl = chunk(local)
                uqh, uql = (a[:, 0:768].rearrange("p (k n) -> p k n", k=2) for a in (wh, wl))
                ukh, ukl = (a[:, 768:1280] for a in (wh, wl))
                pe.wait_ge(low_ready, l * LAYER_CHUNKS + local + 1)
                pe.wait_ge(rms_low, 2 * l + 2)
                pe.wait_ge(proj_copied, FM_CHUNKS * (l + 1))

                def d_queries(j, bank):
                    for k in range(2):
                        last = three(ps[:, bank, 0:TOK], uqh[:, k, j * P:(j + 1) * P], uql[:, k, j * P:(j + 1) * P],
                                     cq_high[:, k, :], cq_low[:, k, :], k == 0, k == 1)
                    return last

                d_queries(0, 0)
                d_queries(1, 1).then_inc(d_proj, 1)
                pe.wait_ge(c_copied, l + 1)
                scores(l, 0, groups_a, m_a1, m_blk0, zeros_bf[0:32, :])
                pe.wait_ge(roped, 6 * l + 5)
                d_queries(2, 6).then_inc(d_proj, 1)
                pe.wait_ge(d_copied, 4 * l + 2)
                pe.matmul(ps[:, 7, 0:TOK], swap_r, rope_x[:, 1, 0, :], start=True, stop=True).then_inc(swapped, 1)

                def d_values(bank):
                    for half in range(2):
                        lo, rows = ((0, 128), (128, 128), (256, 32), (288, 128))[2 * (bank - 6) + half]
                        xh, xl = ckv_high[:, lo:lo + rows], ckv_low[:, lo:lo + rows]
                        out = ps[0:rows, bank, 256 * half:256 * half + 256]
                        pe.matmul(out, xh, ukh[:, 256:512], start=True, stop=False, skip_group_check=True)
                        pe.matmul(out, xl, ukh[:, 256:512], start=False, stop=False, skip_group_check=True)
                        last = pe.matmul(out, xh, ukl[:, 256:512], start=False, stop=True, skip_group_check=True)
                    return last

                d_values(6).then_inc(d_proj, 1)
                for j in range(2):
                    mm = three(ps[:, j, 0:KEYS], ukh[:, j * P:(j + 1) * P], ukl[:, j * P:(j + 1) * P],
                               ckv_high[:, :], ckv_low[:, :], True, True)
                mm.then_inc(d_proj, 1)
                pe.wait_ge(roped, 6 * (l + 1))
                d_values(7).then_inc(chunk_used, 1)
                pe.wait_ge(exp_ready, 3 * l + 1)
                pe.wait_ge(c_soft, l + 1)
                sp_ = prob[:, 1, :]
                for b in range(2):
                    pe.matmul(ps[:, 2 + b, :], later, sp_[:, 512 * b:512 * b + 512], start=True, stop=False,
                              skip_group_check=True)
                    for j in range(2):
                        pe.matmul(ps[:, 2 + b, 256 * j + 128:256 * j + 256], ones,
                                  sp_[:, 1024 + 128 * (2 * b + j):1152 + 128 * (2 * b + j)],
                                  start=False, stop=(j == 1), skip_group_check=True)
                pe.matmul(ps[:, 4, :], later, sp_[:, 1024:1536], start=True, stop=True)
                pe.matmul(ps[:, 5, 0:256], later, sp_[:, 1536:1792], start=True, stop=False, skip_group_check=True)
                pe.matmul(ps[:, 5, 0:128], ones, sp_[:, 1664:1792], start=False, stop=True,
                          skip_group_check=True).then_inc(c_sum, 1)
                pe.wait_ge(d_copied, 4 * (l + 1))
                transposes(l, 0)
                pe.wait_ge(c_w, l + 1)
                scores(l, 1, groups_d, m_c1, m_blk0, zeros_bf[0:32, :])
                weighted(l, 0)
                weighted(l, 1)
                out_projection(l, WO_AT, 0, 6, ONE)
                out_projection(l, WO_AT, 0, 6, OTHER).then_inc(part_ready, 1)
                out_projection(l, WO_AT, 1, 0, BOTH).then_inc(chunk_used, 1)
                pe.wait_ge(exp_ready, 3 * l + 2)
                pe.wait_ge(topk_done, l + 1)
                scores(l, 2, heads_of(QB, KB, True), hide_b[:, 128:384], hide_b[:, 0:128], hide_b[0:32, 384:544])
                pe.wait_ge(part_added, 4 * l + 2)
                transposes(l, 1)
                weighted(l, 2)
                out_projection(l, WO_AT + 1, 0, 0, BOTH).then_inc(part_ready, 1)
                pe.wait_ge(o_low, 4 * l + 3)
                out_projection(l, WO_AT + 1, 1, 6, BOTH).then_inc(chunk_used, 1)
                pe.wait_ge(part_added, 4 * l + 3)
                transposes(l, 2)
                out_projection(l, WO_AT + 2, 0, 4, ONE)
                pe.wait_ge(part_added, 4 * (l + 1))
                weighted(l, 3)
                out_projection(l, WO_AT + 2, 1, 0, ONE)
                out_projection(l, WO_AT + 2, 0, 4, OTHER).then_inc(wo_ready, 1)
                out_projection(l, WO_AT + 2, 1, 0, OTHER).then_inc(chunk_used, 1)
                out_projection(l, WO_AT + 3, 0, 6, BOTH).then_inc(wo_ready, 1)
                pe.wait_ge(z_ready, 5 * event + 1)
                out_projection(l, WO_AT + 3, 1, 4, BOTH, (0,)).then_inc(tile6_ready, 1)
                out_projection(l, WO_AT + 3, 1, 4, range(3), (1,))
                stats_most(event)
                out_projection(l, WO_AT + 3, 1, 4, range(3, 4), (1,)).then_inc(chunk_used, 1)

            ONE, OTHER, BOTH = range(0, 2), range(2, 4), range(0, 4)

            def out_projection(l, local, side, bank, rows, tiles=(0, 1)):
                _, wh, wl = (a.rearrange("p (k n) -> p k n", k=4) for a in chunk(local))
                pe.wait_ge(low_ready, l * LAYER_CHUNKS + local + 1)
                names = WO_PARTS[(local - WO_AT) // 2]
                pe.wait_ge(o_low, 4 * l + RUN.index(names[rows[-1] // 2]) + 1)
                for k in rows:
                    x = 2 * WO_ROW[names[k // 2]] + k % 2
                    for d in tiles:
                        c = (2 * side + d) * P
                        mm = three(ps[:, bank + d, 0:TOK], wh[:, k, c:c + P], wl[:, k, c:c + P], x_high[:, x, :],
                                   x_low[:, x, :], k == 0, k == 3)
                return mm

            for l in range(DEPTH):
                ffn(l, 0)
                stats_rest(3 * l)
                mixer(l)
                stats_rest(3 * l + 1)
                ffn(l, 1)
                stats_rest(3 * l + 2)

        @block.scalar
        def _(act):
            links = [0]

            def link(ins):
                links[0] += 1
                ins.then_inc(act_link, 1)
                act.wait_ge(act_link, links[0])

            split = [1]

            def high_until(n):
                while split[0] < min(n, DEPTH * LAYER_CHUNKS):
                    c = split[0]
                    local = c % LAYER_CHUNKS
                    r, wh, _ = chunk(local)
                    act.wait_ge(raw_landed[c % NRAW], landed(c))
                    ge(act, chunk_used, c - NSPLIT + 1)
                    act.activation(wh, r, ACT.Copy).then_inc(high_ready, 1)
                    split[0] += 1

            def ffn(l, i):
                f, base = 2 * l + i, l * LAYER_CHUNKS + (FFN0_AT, FFN1_AT)[i]

                def high(t):
                    act.wait_ge(gated_ready, f * KF + t + 1)
                    act.activation(hid_high[:, t, :], gated[:, t % 2, :], ACT.Copy).then_inc(hid_high_ready, 1)

                act.preload_act_table_set("silu_and_others")
                if i == 1:
                    act.wait_ge(stored, 80 * (l + 1))
                for t in range(GU_CHUNKS):
                    high_until(base + t + NSPLIT)
                    act.wait_ge(chunk_used, base + t + 1)
                    ge(act, gated_ready, f * KF + t - 1)
                    act.activation(silu_g[:, t % 2, :], ps[:, 6 * (t % 2), 0:TOK], ACT.Silu).then_inc(silu_ready, 1)
                    if t > 0:
                        high(t - 1)
                high(GU_CHUNKS - 1)
                act.preload_act_table_set("natural_log_exp_and_others")
                for q in range(4):
                    for third in range(3):
                        high_until(base + GU_CHUNKS + 3 * q + third + NSPLIT)
                    square(3 * l + (0, 2)[i], q)

            def square(n, q):
                act.wait_ge(z_ready, 5 * n + q + 1)
                if q == 0:
                    act.activation(zsqsum[:, :, :], z[:, 0:2, :], ACT.Square).then_inc(zsq_ready, 1)
                else:
                    if q == 2:
                        act.wait_ge(zsq_added, 2 * n + 1)
                    if q == 3:
                        act.wait_ge(zsq_added, 2 * n + 2)
                        act.activation(zsq[:, 0, :], z[:, 6, :], ACT.Square).then_inc(zsq_ready, 1)
                        act.wait_ge(z_ready, 5 * (n + 1))
                        act.activation(zsq[:, 1, :], z[:, 7, :], ACT.Square).then_inc(zsq_ready, 1)
                        return
                    act.activation(zsq[:, :, :], z[:, 2 * q:2 * q + 2, :], ACT.Square).then_inc(zsq_ready, 1)

            def norm(n):
                l, which = n // 3, n % 3
                act.wait_ge(stat_ready, n + 1)
                act.activation(msq[:, :], ps[:, 2, 0:TOK], ACT.Square, scale=1.0 / D_MODEL).then_inc(msq_ready, 1)
                act.wait_ge(var_ready, n + 1)
                link(act.activation(rstd[:, :], var[:, :], ACT.Ln))
                act.activation(rstd[:, :], rstd[:, :], ACT.Exp, scale=-0.5).then_inc(rstd_ready, 1)
                for j in range(KD):
                    act.wait_ge(norm_ready, KD * n + j + 1)
                    bias = gb[:, l, which, 1, j:j + 1]
                    if n < 3 * DEPTH - 1:
                        act.activation(x_high[:, j, :], z[:, j, :], ACT.Identity, bias=bias).then_inc(x_high_ready, 1)
                    act.activation(hT[:, j, :], z[:, j, :], ACT.Identity, bias=bias).then_inc(h_ready, 1)

            def softmax(l, s, scale, between=None):
                act.wait_ge(max_ready, 3 * l + s + 1)
                pr = prob[:, s % 2, :]
                for h in range(4):
                    act.activation(pr[:, 512 + 256 * h:768 + 256 * h], ps[:, 2 + h // 2, 256 * (h % 2):256 * (h % 2) + 256],
                                   ACT.Exp, bias=neg_m[:, 4 + h:5 + h], scale=scale, accum_out=sums[:, 4 + h:5 + h])
                if between is not None:
                    between()
                for h in range(4):
                    act.activation(pr[:, 128 * h:128 * h + 128], ps[:, 4, 128 * h:128 * h + 128],
                                   ACT.Exp, bias=neg_m[:, h:h + 1], scale=scale, accum_out=sums[:, h:h + 1])
                if s == 0:
                    act.activation(sink_e[:, :], top_s[:, :], ACT.Exp)
                act.activation(pr[:, 1536:1696], ps[:, 5, 0:SKEYS], ACT.Exp, bias=neg_m[:, 8:9], scale=scale,
                               accum_out=sums[:, 8:9]).then_inc(exp_ready, 1)

            def copy_t(l, s):
                for g in (0, 2):
                    act.wait_ge(t_ready, 4 * (3 * l + s) + g + 1)
                    if g == 0 and s > 0:
                        act.wait_ge(pv_ready, 4 * l + (1, 1, 3)[s])
                    act.activation(probT[:, 512 * g:512 * g + 512], ps[:, t_bank(s, g), :], ACT.Copy).then_inc(t_act, 1)

            def out_high(l, run):
                act.wait_ge(pv_ready, 4 * l + run + 1)
                k = 2 * WO_ROW[RUN[run]]
                act.activation(x_high[:, k:k + 2, :], ps[:, PV_BANK[run]:PV_BANK[run] + 2, 0:TOK], ACT.Copy).then_inc(o_high, 1)

            def mixer(l):
                base = l * LAYER_CHUNKS + MIX_AT
                high_until(base + 1 + NSPLIT)
                act.wait_ge(chunk_used, base + 2)
                for b in range(3):
                    rows = 32 if b == 2 else 128
                    act.activation(v_tok[0:rows, b, :], ps[0:rows, 4 + b, 0:V_TOK], ACT.Copy).then_inc(tm_copied, 1)
                for b in range(3):
                    rows = 32 if b == 2 else 128
                    ins = act.activation(w_idx[0:rows, b, :], ps[0:rows, 4 + b, W_I:V_TOK], ACT.Copy, scale=1.0 / 16)
                link(ins)
                for i in range(FM_CHUNKS):
                    c = base + TM_CHUNKS + i
                    high_until(c + NSPLIT)
                    act.wait_ge(chunk_used, c + 1)
                    pair = ps[:, 2 * (i % 2):2 * (i % 2) + 2, 0:TOK]
                    if i in ROPE_CHUNKS:
                        r = ROPE_CHUNKS.index(i)
                        if r >= 2:
                            act.wait_ge(roped, 6 * l + r - 1)
                        act.activation(rope_x[:, r % 2, :, :], pair, ACT.Copy).then_inc(proj_copied, 1)
                    if i == LATENT_Q:
                        act.activation(zsq[:, :, :], pair, ACT.Square).then_inc(rms_sq, 1)
                        act.activation(cq_x[:, :, :], pair, ACT.Copy).then_inc(proj_copied, 1)
                    if i == LATENT_KV:
                        act.activation(zsum[:, 0, :], pair[:, 0, :], ACT.Square).then_inc(rms_sq, 1)
                        act.activation(kT[:, CKV, 0:TOK], pair[:, 0, :], ACT.Copy)
                        act.activation(kT[:, KC, 0:TOK], pair[:, 1, :], ACT.Copy).then_inc(proj_copied, 1)
                    if i == C_FIRST:
                        act.activation(kT[:, KC + 1, 0:TOK], pair[:, 0, :], ACT.Copy)
                        act.activation(qT[:, QC, :], pair[:, 1, :], ACT.Copy).then_inc(proj_copied, 1)
                    if i == C_LAST:
                        act.activation(qT[:, QC + 1, :], pair[:, 0, :], ACT.Copy).then_inc(proj_copied, 1)
                    if 3 <= i <= 5:
                        g = i - 3
                        act.wait_ge(logits_ready, 3 * l + g + 1)
                        ge(act, scored, 3 * l + g)
                        if g == 0:
                            act.activation(relu_l[:, :], ps[:, 4:6, :], ACT.Relu).then_inc(relu_ready, 1)
                        if g == 1:
                            act.activation(relu_l[:, 0:512], ps[:, 4, :], ACT.Relu)
                            act.activation(relu_l[0:32, 512:832], ps[0:32, 5, 0:320], ACT.Relu).then_inc(relu_ready, 1)
                        if g == 2:
                            act.activation(relu_l[0:32, 0:320], ps[0:32, 4, 0:320], ACT.Relu).then_inc(relu_ready, 1)
                    if i == 3 or i == 4:
                        r = i - 3
                        act.wait_ge(rms_sum, 2 * l + r + 1)
                        out = (msq, var)[r]
                        link(act.activation(out[:, :], ps[:, 6 + r, 0:TOK], ACT.Ln, bias=eps[:, :],
                                            scale=1.0 / (Q_LORA, KV_LORA)[r]))
                        act.activation(out[:, :], out[:, :], ACT.Exp, scale=-0.5).then_inc(rms_rstd, 1)
                    if i == 5:
                        act.wait_ge(rms_done, 2 * l + 1)
                        act.activation(cq_high[:, :, :], cq_x[:, :, :], ACT.Copy).then_inc(rms_high, 1)
                        act.wait_ge(rms_done, 2 * l + 2)
                        act.wait_ge(cache_landed, 32 * (l + 1))
                        act.activation(ckv_high[:, :], kT[:, CKV, :], ACT.Copy).then_inc(rms_high, 1)
                high_until(base + MIX_CHUNKS - 1 + NSPLIT)
                act.wait_ge(c_sum, 2 * l + 1)
                zc, ec = c_z[:, :], prob[:, 1, :]
                flat = ps[:, 2:6, :].rearrange("p b n -> p (b n)")[:, 0:1792]
                act.activation(zc, flat, ACT.Copy, scale=0.125).then_inc(c_copied, 1)
                act.wait_ge(c_copied, l + 1)
                link(act.activation(ec, zc, ACT.Abs))
                link(act.activation(ec, ec, ACT.Exp, scale=-1.0))
                act.activation(ec, ec, ACT.Ln, bias=1.0).then_inc(c_ln, 1)
                act.wait_ge(d_proj, 4 * l + 1)
                act.activation(qd[:, 0:2, :], ps[:, 0:2, 0:TOK], ACT.Copy).then_inc(d_copied, 1)
                act.wait_ge(d_proj, 4 * l + 2)
                act.activation(rope_x[:, 1, 0, :], ps[:, 6, 0:TOK], ACT.Copy).then_inc(d_copied, 1)
                softmax(l, 0, 0.125)
                act.wait_ge(d_proj, 4 * l + 3)
                act.activation(v_d[:, 0:2, :], ps[:, 6, :], ACT.Copy)
                act.wait_ge(d_proj, 4 * (l + 1))
                act.activation(kd[:, :, :], ps[:, 0:2, 0:KEYS], ACT.Copy).then_inc(d_copied, 1)
                act.wait_ge(chunk_used, base + MIX_CHUNKS)
                act.activation(v_d[0:32, 2, :], ps[0:32, 7, 0:256], ACT.Copy)
                act.activation(v_d[:, 3, :], ps[:, 7, 256:512], ACT.Copy).then_inc(d_copied, 1)
                copy_t(l, 0)
                high_until(base + MIX_CHUNKS + NSPLIT)
                act.wait_ge(c_w, l + 1)
                act.activation(zc, zc, ACT.Exp).then_inc(c_a, 1)
                out_high(l, 0)
                softmax(l, 1, 96 ** -0.5)
                out_high(l, 1)
                high_until(base + MIX_CHUNKS + 1 + NSPLIT)
                copy_t(l, 1)
                softmax(l, 2, 0.125, between=lambda: out_high(l, 2))
                high_until(base + MIX_CHUNKS + 2 + NSPLIT)
                copy_t(l, 2)
                out_high(l, 3)
                square(3 * l + 1, 0)
                high_until(base + MIX_CHUNKS + 3 + NSPLIT)
                for q in range(1, 4):
                    square(3 * l + 1, q)

            for pair in range(4):
                act.wait_ge(first_landed[pair], 16)
                act.activation(first_part(w_high[:, 0, :], pair), first_part(raw[:, 0, :], pair),
                               ACT.Copy).then_inc(first_high if pair < 3 else high_ready, 1)
                act.wait_ge(x_landed[pair], 16)
                for j in (2 * pair, 2 * pair + 1):
                    act.activation(x_high[:, j, :], hT[:, j, :], ACT.Copy).then_inc(x_high_ready, 1)
            for l in range(DEPTH):
                ffn(l, 0)
                norm(3 * l)
                mixer(l)
                norm(3 * l + 1)
                ffn(l, 1)
                norm(3 * l + 2)

        @block.vector
        def _(dve):
            links = [0]

            def link(ins):
                links[0] += 1
                ins.then_inc(dve_link, 1)
                dve.wait_ge(dve_link, links[0])

            split = [1]

            def low_until(n):
                while split[0] < min(n, DEPTH * LAYER_CHUNKS):
                    c = split[0]
                    if c % LAYER_CHUNKS in POOL_LOW:
                        split[0] += 1
                        continue
                    if (c - 1) % LAYER_CHUNKS in POOL_LOW:
                        dve.wait_ge(low_ready, c)
                    r, wh, wl = chunk(c % LAYER_CHUNKS)
                    dve.wait_ge(high_ready, c + 1)
                    dve.tensor_tensor(wl, r, wh.bitcast(F32), ALU.subtract).then_inc(low_ready, 1)
                    split[0] += 1

            def ffn(l, i):
                f, base = 2 * l + i, l * LAYER_CHUNKS + (FFN0_AT, FFN1_AT)[i]

                def low(t):
                    dve.wait_ge(hid_high_ready, f * KF + t + 1)
                    dve.tensor_tensor(hid_low[:, t, :], gated[:, t % 2, :], hid_high[:, t, :].bitcast(F32),
                                      ALU.subtract).then_inc(hid_low_ready, 1)

                for t in range(GU_CHUNKS):
                    low_until(base + t + NSPLIT)
                    dve.wait_ge(silu_ready, f * KF + t + 1)
                    ge(dve, hid_low_ready, f * KF + t - 1)
                    dve.scalar_tensor_tensor(out=gated[:, t % 2, :], in0=silu_g[:, t % 2, :], scalar=0.5,
                                             in1=ps[:, 6 * (t % 2) + 1, 0:TOK], op0=ALU.mult, op1=ALU.mult)\
                       .then_inc(gated_ready, 1)
                    if t > 0:
                        low(t - 1)
                low(GU_CHUNKS - 1)
                for q in range(4):
                    for third in range(3):
                        low_until(base + GU_CHUNKS + 3 * q + third + NSPLIT)
                    residual(3 * l + (0, 2)[i], q, base + GU_CHUNKS + 3 * q + 3)

            def residual(n, q, used):
                ge(dve, h_ready, KD * n)
                bank = (4, 0, 6, 4)[q] if n % 3 == 1 else 4 + 2 * (q % 2)
                if n % 3 == 1:
                    dve.wait_ge(part_added, 4 * (n // 3) + q + 1)
                for tiles in ((2 * q, 2),) if q < 3 else ((6, 1), (7, 1)):
                    at_, count = tiles
                    if at_ == 6:
                        dve.wait_ge(tile6_ready, n + 1)
                    elif used is not None:
                        dve.wait_ge(chunk_used, used)
                    zt, out = z[:, at_:at_ + count, :], ps[:, bank + at_ % 2:bank + at_ % 2 + count, 0:TOK]
                    if n % 3 == 1:
                        dve.tensor_tensor(zt, zt, out, ALU.add).then_inc(z_ready, 1)
                    else:
                        dve.scalar_tensor_tensor(out=zt, in0=hT[:, at_:at_ + count, :], scalar=DN_ALPHA,
                                                 in1=out, op0=ALU.mult, op1=ALU.add).then_inc(z_ready, 1)
                    if at_ == 6:
                        dve.wait_ge(z_ready, 5 * n + 4)
                        dve.tensor_tensor(zsum[:, 0, :], zsum[:, 0, :], z[:, 6, :], ALU.add).then_inc(zsum_ready, 1)
                zq = z[:, 2 * q:2 * q + 2, :]
                if q in (0, 3):
                    return
                dve.wait_ge(z_ready, 5 * n + q + 1)
                link(dve.tensor_tensor(zsum[:, :, :], z[:, 0:2, :] if q == 1 else zsum[:, :, :], zq, ALU.add))
                if q == 2:
                    link(dve.tensor_tensor(zsum[:, 0, :], zsum[:, 0, :], zsum[:, 1, :], ALU.add))

            def norm(n):
                if n == 0:
                    dve.wait_ge(const_landed, 8 * 16)
                l, which = n // 3, n % 3

                def center(j):
                    dve.scalar_tensor_tensor(out=z[:, j, :], in0=ps[:, 2, 0:TOK], scalar=-1.0 / D_MODEL, in1=z[:, j, :],
                                             op0=ALU.mult, op1=ALU.add).then_inc(centered, 1)

                def scale(j):
                    dve.wait_ge(centered, KD * n + j + 1)
                    dve.scalar_tensor_tensor(out=z[:, j, :], in0=z[:, j, :], scalar=gb[:, l, which, 0, j:j + 1],
                                             in1=rstd[:, :], op0=ALU.mult, op1=ALU.mult).then_inc(norm_ready, 1)

                def low(j):
                    if n == 3 * DEPTH - 1:
                        return
                    dve.wait_ge(x_high_ready, KD * (n + 1) + j + 1)
                    dve.scalar_tensor_tensor(out=x_low[:, j, :], in0=z[:, j, :], scalar=gb[:, l, which, 1, j:j + 1],
                                             in1=x_high[:, j, :].bitcast(F32), op0=ALU.add,
                                             op1=ALU.subtract).then_inc(x_low_ready, 1)

                dve.wait_ge(msq_ready, n + 1)
                link(dve.scalar_tensor_tensor(out=var[:, :], in0=ps[:, 3, 0:TOK], scalar=1.0 / D_MODEL, in1=msq[:, :],
                                              op0=ALU.mult, op1=ALU.subtract))
                dve.tensor_scalar(var[:, :], var[:, :], 0.0, LN_EPS, ALU.max, ALU.add).then_inc(var_ready, 1)
                center(0)
                center(1)
                dve.wait_ge(rstd_ready, n + 1)
                scale(0)
                scale(1)
                for j in range(2, KD):
                    center(j)
                    low(j - 2)
                    scale(j)
                low(KD - 2)
                low(KD - 1)

            def rope(l, r):
                kind, tile = ROPE_PAIRS[r]
                both = r == 2
                dst = qT[:, tile:tile + 2, :] if kind == "q" else kT[:, tile:tile + 2, 0:TOK]
                cos, sin = (tab[:, i, :, :] if both else tab[:, i, 1:2, :].to_broadcast([P, 2, TOK]) for i in range(2))
                dve.wait_ge(proj_copied, FM_CHUNKS * l + ROPE_CHUNKS[r] + 1)
                link(dve.tensor_tensor(rope_a[:, :, :], rope_x[:, r % 2, :, :], cos, ALU.mult))
                dve.wait_ge(swapped, 6 * l + r + 1)
                link(dve.tensor_tensor(rope_b[:, :, :], ps[:, 6:8, 0:TOK], sin, ALU.mult))
                dve.tensor_tensor(dst, rope_a[:, :, :], rope_b[:, :, :], ALU.add).then_inc(roped, 1)
                dve.wait_ge(roped, 6 * l + r + 1)

            s_blk0, s_blk1, s_smp = score[:, 0:128], score[:, 128:384], score[0:32, 384:544]

            def weigh(l, out, mask, relu, h, b, rows, n):
                link(dve.scalar_tensor_tensor(out=out, in0=relu, scalar=w_idx[0:rows, b, h:h + 1],
                                              in1=mask if h == 0 else out, op0=ALU.mult, op1=ALU.add))

            def indexer(l, g):
                dve.wait_ge(relu_ready, 3 * l + g + 1)
                if g == 0:
                    for h in range(4):
                        weigh(l, s_blk1, m_c1, relu_l[:, 256 * h:256 * h + 256], h, 1, P, 256)
                if g == 1:
                    for h in range(4):
                        weigh(l, s_blk0, m_blk0, relu_l[:, 128 * h:128 * h + 128], h, 0, P, 128)
                    for h in range(2):
                        weigh(l, s_smp, zeros_bf[0:32, :], relu_l[0:32, 512 + 160 * h:672 + 160 * h], h, 2, 32, 160)
                if g == 2:
                    for h in range(2, 4):
                        weigh(l, s_smp, None, relu_l[0:32, 160 * (h - 2):160 * (h - 1)], h, 2, 32, 160)
                dve.sem_inc(scored, 1)

            def best(s, k):
                rows = s.shape[0]
                for _ in range(k // 8):
                    yield
                    link(dve.max(best8[0:rows, :], s))
                    link(dve.match_replace(s, best8[0:rows, :], s, TAKEN))

            def choose():
                yield from best(s_blk1, TOPK_PROMPT)
                yield from best(s_blk0, TOPK_PROMPT)
                yield from best(s_smp, TOPK_SAMPLE)
                yield
                for rows, a, b in ((P, 0, 128), (P, 128, 384), (32, 384, 544)):
                    link(dve.tensor_scalar(hide_b[0:rows, a:b], score[0:rows, a:b], TAKEN, HIDE,
                                           ALU.not_equal, ALU.mult))
                dve.sem_inc(topk_done, 1)

            def largest(l, s, scale):
                dve.wait_ge(s_ready, 3 * l + s + 1)
                dve.reduce_max(top_s[:, 4:8], ps[:, 2:4, :].rearrange("p b (h k) -> p (b h) k", h=2), AX_X)
                dve.reduce_max(top_s[:, 0:4], ps[:, 4, :].rearrange("p (h k) -> p h k", h=4), AX_X)
                link(dve.reduce_max(top_s[:, 8:9], ps[:, 5, 0:SKEYS], AX_X))
                if s == 0:
                    sk = snk[:, l, :]
                    link(dve.scalar_tensor_tensor(out=top_s[:, :], in0=top_s[:, :], scalar=scale, in1=sk,
                                                  op0=ALU.mult, op1=ALU.max))
                    link(dve.tensor_scalar(neg_m[:, :], top_s[:, :], -1.0, None, ALU.mult))
                    link(dve.tensor_tensor(top_s[:, :], sk, neg_m[:, :], ALU.add))
                else:
                    link(dve.tensor_scalar(neg_m[:, :], top_s[:, :], -scale, None, ALU.mult))
                dve.sem_inc(max_ready, 1)

            def divide(l, s):
                dve.wait_ge(exp_ready, 3 * l + s + 1)
                if s == 0:
                    link(dve.tensor_tensor(sums[:, :], sums[:, :], sink_e[:, :], ALU.add))
                link(dve.reciprocal(recip[:, :], sums[:, :]))
                pr = prob[:, s % 2, :]
                for a, n in ((0, 128), (512, 256)):
                    v = pr[:, a:a + 4 * n].rearrange("p (h k) -> p h k", h=4)
                    r = recip[:, 4 * (a > 0):4 * (a > 0) + 4].rearrange("p (h o) -> p h o", o=1).to_broadcast([P, 4, n])
                    dve.tensor_tensor(v, v, r, ALU.mult)
                link(dve.tensor_scalar(pr[:, 1536:1696], pr[:, 1536:1696], recip[:, 8:9], None, ALU.mult))
                dve.sem_inc(p_ready, 1)

            def copy_t(l, s):
                for g in (1, 3):
                    dve.wait_ge(t_ready, 4 * (3 * l + s) + g + 1)
                    if g == 1:
                        if s > 0:
                            dve.wait_ge(pv_ready, 4 * l + (1, 1, 3)[s])
                        dve.tensor_copy(probT[:, 512:1024], ps[:, t_bank(s, g), :]).then_inc(t_dve, 1)
                    else:
                        link(dve.tensor_copy(probT[:, 1536:1664], ps[:, t_bank(s, g), 0:128]))
                        dve.tensor_copy(probT[0:32, 1664:1792], ps[0:32, t_bank(s, g), 128:256]).then_inc(t_dve, 1)

            def out_low(l, run):
                dve.wait_ge(o_high, 4 * l + run + 1)
                k = 2 * WO_ROW[RUN[run]]
                dve.tensor_tensor(x_low[:, k:k + 2, :], ps[:, PV_BANK[run]:PV_BANK[run] + 2, 0:TOK], x_high[:, k:k + 2, :].bitcast(F32),
                                  ALU.subtract).then_inc(o_low, 1)

            def mixer(l):
                base = l * LAYER_CHUNKS + MIX_AT
                low_until(base + 1 + NSPLIT)
                rounds = choose()

                def some(n):
                    for _ in range(n):
                        next(rounds, None)

                for i in range(FM_CHUNKS):
                    low_until(base + TM_CHUNKS + i + NSPLIT)
                    if i == 1 or i == 2:
                        rope(l, i - 1)
                    if i == 5 or i == 6:
                        rope(l, i - 3)
                    if 3 <= i <= 5:
                        indexer(l, i - 3)
                    if i == 4:
                        dve.wait_ge(rms_rstd, 2 * l + 1)
                        dve.wait_ge(proj_copied, FM_CHUNKS * l + LATENT_KV + 1)
                        for j in range(2):
                            ins = dve.scalar_tensor_tensor(out=cq_x[:, j, :], in0=cq_x[:, j, :], scalar=rg[:, l, j:j + 1],
                                                           in1=msq[:, :], op0=ALU.mult, op1=ALU.mult)
                        ins.then_inc(rms_done, 1)
                    if i == 5:
                        dve.wait_ge(rms_rstd, 2 * l + 2)
                        dve.scalar_tensor_tensor(out=kT[:, CKV, 0:TOK], in0=kT[:, CKV, 0:TOK], scalar=rg[:, l, 2:3],
                                                 in1=var[:, :], op0=ALU.mult, op1=ALU.mult).then_inc(rms_done, 1)
                    if i == 6:
                        dve.wait_ge(rms_high, 2 * l + 1)
                        dve.tensor_tensor(cq_low[:, :, :], cq_x[:, :, :], cq_high[:, :, :].bitcast(F32),
                                          ALU.subtract).then_inc(rms_low, 1)
                        dve.wait_ge(rms_high, 2 * l + 2)
                        dve.tensor_tensor(ckv_low[:, :], kT[:, CKV, :], ckv_high[:, :].bitcast(F32),
                                          ALU.subtract).then_inc(rms_low, 1)
                    some((0, 0, 0, 0, 2, 0, 3, 4, 2)[i])
                low_until(base + MIX_CHUNKS - 1 + NSPLIT)
                rope(l, 4)
                some(4)
                largest(l, 0, 0.125)
                dve.wait_ge(d_copied, 4 * l + 2)
                link(dve.tensor_tensor(rope_a[:, 0, :], rope_x[:, 1, 0, :], tab[:, 0, 0, :], ALU.mult))
                dve.wait_ge(swapped, 6 * (l + 1))
                link(dve.tensor_tensor(rope_b[:, 0, :], ps[:, 7, 0:TOK], tab[:, 1, 0, :], ALU.mult))
                dve.tensor_tensor(qd[:, 2, :], rope_a[:, 0, :], rope_b[:, 0, :], ALU.add).then_inc(roped, 1)
                dve.wait_ge(c_ln, l + 1)
                dve.scalar_tensor_tensor(out=prob[:, 1, :], in0=c_z[:, :], scalar=0.0, in1=prob[:, 1, :],
                                         op0=ALU.max, op1=ALU.add).then_inc(c_soft, 1)
                divide(l, 0)
                dve.wait_ge(c_sum, 2 * l + 2)
                flat = ps[:, 2:6, :].rearrange("p b n -> p (b n)")[:, 0:1792]
                dve.scalar_tensor_tensor(out=c_z[:, :], in0=flat, scalar=-1.0, in1=c_z[:, :],
                                         op0=ALU.mult, op1=ALU.add).then_inc(c_w, 1)
                copy_t(l, 0)
                some(TOPK_PROMPT // 4 + TOPK_SAMPLE // 8 + 1)
                largest(l, 1, 96 ** -0.5)
                out_low(l, 0)
                out_low(l, 1)
                divide(l, 1)
                part(l, 0)
                part(l, 1)
                copy_t(l, 1)
                largest(l, 2, 0.125)
                out_low(l, 2)
                part(l, 2)
                divide(l, 2)
                part(l, 3)
                copy_t(l, 2)
                out_low(l, 3)
                for q in range(4):
                    if q % 2 == 0:
                        dve.wait_ge(wo_ready, 2 * l + q // 2 + 1)
                        residual(3 * l + 1, q, None)
                    else:
                        residual(3 * l + 1, q, base + MIX_CHUNKS + 2 + q // 2 + 1)
                low_until(base + MIX_CHUNKS + 3 + NSPLIT)

            def part(l, q):
                if q % 2 == 0:
                    dve.wait_ge(part_ready, 2 * l + q // 2 + 1)
                else:
                    dve.wait_ge(chunk_used, l * LAYER_CHUNKS + WO_AT + q // 2 + 1)
                dve.wait_ge(roped, 6 * (l + 1))
                bank = (6, 0, 0, 6)[q]
                dve.scalar_tensor_tensor(out=z[:, 2 * q:2 * q + 2, :], in0=hT[:, 2 * q:2 * q + 2, :], scalar=DN_ALPHA,
                                         in1=ps[:, bank:bank + 2, 0:TOK], op0=ALU.mult, op1=ALU.add)\
                   .then_inc(part_added, 1)

            dve.memset(eps[:, :], RMS_EPS).then_inc(dve_link, 1)
            links[0] += 1
            for j in range(KD):
                if j % 2 == 0:
                    pair = j // 2
                    if pair < 3:
                        dve.wait_ge(first_high, pair + 1)
                    else:
                        dve.wait_ge(high_ready, 1)
                    dve.tensor_tensor(first_part(w_low[:, 0, :], pair), first_part(raw[:, 0, :], pair),
                                      first_part(w_high[:, 0, :], pair).bitcast(F32),
                                      ALU.subtract).then_inc(first_low if pair < 3 else low_ready, 1)
                dve.wait_ge(x_high_ready, j + 1)
                dve.tensor_tensor(x_low[:, j, :], hT[:, j, :], x_high[:, j, :].bitcast(F32),
                                  ALU.subtract).then_inc(x_low_ready, 1)
            for l in range(DEPTH):
                ffn(l, 0)
                norm(3 * l)
                mixer(l)
                norm(3 * l + 1)
                ffn(l, 1)
                norm(3 * l + 2)


def _pack_weights(ins, np):
    w = np.zeros((DEPTH, LAYER_CHUNKS, P, CH), np.float32)
    offs = {}
    at = 0
    for name, n in (("qa", 256), ("ka", 128), ("va", 128), ("qb", 256), ("kb", 64), ("vb", 64), ("qi", 256),
                    ("ki", 64), ("wi", 4), ("qc", 256), ("kc", 256), ("vc", 256), ("cq", 256), ("ckv", 128), ("kr", 32)):
        offs[name] = np.arange(at, at + n)
        at += n

    def heads(name, *hs):
        return np.concatenate([offs[name][64 * h:64 * h + 64] for h in hs])

    fm = [heads("qi", 0, 1, 2, 3), heads("ki", 0, 0), heads("kb", 0, 0), offs["cq"], offs["ckv"],
          heads("kc", 0, 1), np.tile(offs["kr"], 4), offs["ka"], heads("qa", 0, 2, 1, 3), heads("kc", 2, 3),
          heads("qc", 0, 1), heads("qc", 2, 3), heads("qb", 0, 1, 2, 3)]
    fm = np.split(np.concatenate(fm), [256 * i for i in range(1, 8)] + [256 * 7 + 128])
    tm = np.concatenate([offs["va"], offs["vb"], offs["vc"], offs["wi"]])

    def tiles(a, k):
        return a.reshape(k, P, -1).transpose(1, 0, 2).reshape(P, -1)

    for l in range(DEPTH):
        for i, base in enumerate((FFN0_AT, FFN1_AT)):
            g, u, d = ins["ffn_gate"][l, i], ins["ffn_up"][l, i], ins["ffn_down"][l, i]
            for t in range(KF):
                w[l, base + t, :, 0:1024] = tiles(g[:, t * P:(t + 1) * P], KD)
                w[l, base + t, :, 1024:2048] = tiles(u[:, t * P:(t + 1) * P], KD)
            for q in range(4):
                f = 0
                for third, n in enumerate(DOWN_SPLIT):
                    w[l, base + KF + 3 * q + third, :, 0:256 * n] = tiles(
                        d[f * P:(f + n) * P, 256 * q:256 * q + 256], n)
                    f += n
        win = ins["w_in"][l]
        for half in range(2):
            w[l, MIX_AT + half, :, 0:4 * V_TOK] = tiles(win[512 * half:512 * half + 512][:, tm], 4)
        for i in range(FM_CHUNKS):
            w[l, MIX_AT + 2 + i, :, 0:8 * len(fm[i])] = tiles(win[:, fm[i]], KD)
        uq = ins["w_uq"][l].reshape(Q_LORA, 4, 96)
        uq = np.concatenate([uq[:, :, 0:64].reshape(Q_LORA, 256), uq[:, :, 64:96].reshape(Q_LORA, 128)], 1)
        ukv = ins["w_ukv"][l].reshape(KV_LORA, 4, 128)
        w[l, WO_AT - 1, :, 0:768] = tiles(uq, 2)
        w[l, WO_AT - 1, :, 768:1024] = ukv[:, :, 0:64].reshape(KV_LORA, 256)
        w[l, WO_AT - 1, :, 1024:1280] = ukv[:, :, 64:128].reshape(KV_LORA, 256)
        for part, names in enumerate(WO_PARTS):
            rows = np.concatenate([np.arange(256 * WO_ROW[name], 256 * WO_ROW[name] + 256) for name in names])
            for half in range(2):
                w[l, WO_AT + 2 * part + half] = tiles(ins["w_o"][l][rows, 512 * half:512 * half + 512], 4)
    return w


def _constants(np, bf16):
    pos = np.arange(TOK, dtype=np.float32)
    pos[SEQ:] += PAST - SEQ
    tab = np.zeros((P, 2, 2, TOK), np.float32)
    mats = np.zeros((P, 5, P), np.float32)
    for which, half in ((0, 16), (1, 32)):
        inv = np.power(np.float32(10000.0), -np.arange(half, dtype=np.float32) / np.float32(half)).astype(np.float32)
        p = np.arange(P)
        ang = (pos[None, :] * inv[p % half][:, None]).astype(np.float32).astype(np.float64)
        sign = np.where(p % (2 * half) < half, -1.0, 1.0)[:, None]
        tab[:, 0, which] = np.cos(ang)
        tab[:, 1, which] = sign * np.sin(ang)
        mats[p, which, np.where(p % (2 * half) < half, p + half, p - half)] = 1.0
    i = np.arange(P)
    mats[i, 2, i] = 1.0
    mats[:, 3, :] = 1.0
    mats[:, 4, :] = i[:, None] >= i[None, :]
    masks = np.zeros((P, 1312), np.float32)
    q0, q1, k = i[:, None], i[:, None] + 128, np.arange(256)[None, :]
    masks[:, 0:128] = np.where(k[:, 0:128] // 64 <= q0 // 64, 0.0, HIDE)
    masks[:, 128:384] = np.where((k // 64 <= q1 // 64) & (k // 64 >= q1 // 64 - 2), 0.0, HIDE)
    masks[:, 384:640] = np.where(k // 64 <= q1 // 64, 0.0, HIDE)
    masks[:, 640:896] = np.where(i[:, None] < k, 0.0, HIDE)
    masks[i, 896 + i] = 1.0
    for h in range(4):
        j = np.arange(32)
        masks[j, 1184 + 32 * h + j] = 1.0
    return tab, mats, masks.astype(bf16)


def kernel(**inputs):
    import ml_dtypes
    import numpy as np
    import concourse.bacc as bacc
    from concourse.bass_utils import run_bass_kernel_spmd

    ins = {k: np.asarray(v) for k, v in inputs.items()}
    tab, mats, masks = _constants(np, ml_dtypes.bfloat16)
    x = np.concatenate([ins["x_prompt"][0], ins["x_sample"][0]], 0)
    x = x.T.reshape(KD, P, TOK).transpose(1, 0, 2)
    gb = np.stack([ins["ln_g"], ins["ln_b"]], 2).reshape(DEPTH, 3, 2, KD, P).transpose(4, 0, 1, 2, 3)
    rg = np.concatenate([ins["g_cq"], ins["g_ckv"]], 1).reshape(DEPTH, 3, P).transpose(2, 0, 1)
    sink = ins["attn_sinks"]
    sinks = np.concatenate([np.broadcast_to(sink, (P, DEPTH, 4)), np.broadcast_to(sink, (P, DEPTH, 4)),
                            np.repeat(sink, 32, axis=1).T[:, :, None]], 2)
    bk, bi, kr = (ins[n][:, 0].transpose(0, 2, 1) for n in ("cache_b_k", "cache_b_kidx", "cache_d_krope"))
    ka = ins["cache_a_k"][:, 0].reshape(DEPTH, PAST, 128).transpose(0, 2, 1)
    kc = ins["cache_c_k"][:, 0].reshape(DEPTH, PAST, 256).transpose(0, 2, 1)
    k_cache = np.stack([np.tile(bi, (1, 2, 1)), np.tile(bk, (1, 2, 1)), np.tile(kr, (1, 4, 1)), ka,
                        ins["cache_d_ckv"][:, 0].transpose(0, 2, 1), kc[:, 0:128], kc[:, 128:256]], 2)
    v_cache = np.concatenate([ins["cache_a_v"][:, 0].reshape(DEPTH, PAST, 128), ins["cache_b_v"][:, 0],
                              ins["cache_c_v"][:, 0].reshape(DEPTH, PAST, 256)], 2)
    arrays = {"weights": _pack_weights(ins, np), "x_in": x, "ln_gb": gb, "rms_g": rg, "sinks": sinks,
              "k_cache": k_cache, "v_cache": v_cache, "tables": tab, "mats": mats, "masks": masks}
    arrays = {k: np.ascontiguousarray(v) for k, v in arrays.items()}
    outs = {"out_y": (P, KD, TOK), "out_k": (DEPTH, P, 7, TOK), "out_ka": (DEPTH, P, 96),
            "out_v": (DEPTH, P, 2, 448), "out_vs": (DEPTH, 32, 448), "out_va": (DEPTH, 96, 128)}
    nc = bacc.Bacc("TRN2", target_bir_lowering=False, num_devices=1)
    args = [nc.dram_tensor(k, v.shape, mybir.dt.from_np(v.dtype), kind="ExternalInput").ap() for k, v in arrays.items()]
    args += [nc.dram_tensor(k, s, F32, kind="ExternalOutput").ap() for k, s in outs.items()]
    encoder_program(nc, *args)
    r = run_bass_kernel_spmd(nc, [arrays], core_ids=[0]).results[0]

    y = r["out_y"].transpose(1, 0, 2).reshape(D_MODEL, TOK).T
    k = r["out_k"].transpose(0, 3, 2, 1)
    v = np.concatenate([r["out_v"].transpose(0, 2, 1, 3).reshape(DEPTH, SEQ, 448), r["out_vs"]], 1)
    ka_s = np.concatenate([r["out_ka"].transpose(0, 2, 1), k[:, SEQ:, KA]], 1)
    va_s = np.concatenate([r["out_va"], v[:, SEQ:, 0:128]], 1)

    def states(s, a_k, a_v):
        n = s.stop - s.start
        kc_ = k[:, s, KC:KC + 2].reshape(DEPTH, 1, n, 4, 64)
        return (a_k.reshape(DEPTH, 1, 128, 2, 64), a_v.reshape(DEPTH, 1, 128, 2, 64), k[:, None, s, KB, 0:64],
                v[:, None, s, V_B:V_B + 64], k[:, None, s, KI, 0:64], kc_,
                v[:, None, s, V_C:V_C + 256].reshape(DEPTH, 1, n, 4, 64), k[:, None, s, CKV], k[:, None, s, KR, 0:32])

    res = (y[None, 0:SEQ], y[None, SEQ:TOK]) \
        + states(slice(0, SEQ), k[:, 128:SEQ, KA], v[:, 128:SEQ, 0:128]) + states(slice(SEQ, TOK), ka_s, va_s)
    return tuple(np.ascontiguousarray(a) for a in res)
```

```python
from contextlib import ExitStack

import concourse.bass as bass
from concourse import mybir

ALU = mybir.AluOpType
ACT = mybir.ActivationFunctionType
F32 = mybir.dt.float32
F32R = mybir.dt.float32r
BF16 = mybir.dt.bfloat16
AX_X = mybir.AxisListType.X

P = 128
DEPTH = 2
D_MODEL, D_FF = 1024, 2816
SEQ, DEC, PAST = 256, 32, 128
TOK = SEQ + DEC
KEYS = TOK + PAST
SKEYS = PAST + DEC
KD = D_MODEL // P
KF = D_FF // P
HD = 64
Q_LORA, KV_LORA, ROPE_D = 256, 128, 32
V_A, V_B, V_C, W_I = 0, 128, 192, 448
V_TOK = 452
TOPK_PROMPT, TOPK_SAMPLE = min(256, SEQ // 4), min(256, SKEYS // 4)
DN_ALPHA = (2 * DEPTH) ** 0.25
LN_EPS, RMS_EPS = 1e-5, 1e-6
HIDE = -1e30
TAKEN = -3e38

CH = 2048
GU_CHUNKS = KF
DOWN_SPLIT = (8, 8, 6)
DOWN_CHUNKS = 4 * len(DOWN_SPLIT)
FFN_CHUNKS = GU_CHUNKS + DOWN_CHUNKS
TM_CHUNKS, FM_CHUNKS = 2, 9
MIX_CHUNKS = TM_CHUNKS + FM_CHUNKS + 1
WO_CHUNKS = 4
FFN0_AT, MIX_AT = 0, FFN_CHUNKS
WO_AT = MIX_AT + MIX_CHUNKS
FFN1_AT = WO_AT + WO_CHUNKS
LAYER_CHUNKS = FFN1_AT + FFN_CHUNKS
POOL_LOW = (1, MIX_AT + 1, *range(WO_AT, FFN1_AT + 2))
NRAW, NSPLIT = 3, 3
TURN, ALONE = 6, 2
KEEP_CLOCK = 16
TURNS = (GU_CHUNKS - 2 * ALONE) // TURN
assert TURNS * TURN + 2 * ALONE == GU_CHUNKS and TURN % NRAW == 0 and TURN % NSPLIT == 0
assert LAYER_CHUNKS % NRAW == 0 and LAYER_CHUNKS % NSPLIT == 0


def chunk_width(local):
    for at in (FFN0_AT, FFN1_AT):
        if at + GU_CHUNKS <= local < at + FFN_CHUNKS:
            return DOWN_SPLIT[(local - at - GU_CHUNKS) % 3] * 256
    if MIX_AT <= local < MIX_AT + TM_CHUNKS:
        return 4 * V_TOK
    if local == MIX_AT + TM_CHUNKS + 7:
        return 8 * P
    if local == WO_AT - 1:
        return 2 * 3 * P + 512
    return CH


QI, QB, QA, QC = 0, 2, 4, 6
KI, KB, KR, KA, CKV, KC = 0, 1, 2, 3, 4, 5
ROPE_PAIRS = (("q", QI), ("k", KI), ("k", KR), ("q", QA), ("q", QB))
ROPE_CHUNKS = (0, 1, 4, 5, 8)
ROTATION = (0, 1, 2, 3, 5)
LATENT_Q, LATENT_KV, C_FIRST, C_LAST = 2, 3, 6, 7
RUN = ("A", "C", "D", "B")
WO_ROW = {"A": 0, "B": 1, "C": 2, "D": 3}
PV_BANK = (6, 0, 6, 6)
WO_PARTS = (("A", "C"), ("D", "B"))


def encoder_program(nc, weights, x_in, ln_gb, rms_g, sinks, k_cache, v_cache, tables, mats, masks,
                    out_y, out_k, out_ka, out_v, out_vs, out_va):
    ctx = ExitStack()
    with ctx:
        at = [16512]

        def sb(name, shape, dt=F32, offset=None):
            size = 2 if dt == BF16 else 4
            n = size
            for d in shape[1:]:
                n *= d
            n = (n + 31) // 32 * 32
            if offset is None:
                offset = at[0]
                at[0] += n
            return nc.alloc_sbuf_tensor_at(name, shape, dt, offset=offset), offset + n

        raw, _ = sb("raw", [P, NRAW, CH])
        w_high, _ = sb("w_high", [P, NSPLIT, CH], F32R)
        w_low, _ = sb("w_low", [P, NSPLIT, CH], F32R)
        hT, _ = sb("hT", [P, KD, TOK])
        x_high, _ = sb("x_high", [P, KD, TOK], F32R)
        x_low, _ = sb("x_low", [P, KD, TOK], F32R)
        z_at = at[0]
        z, _ = sb("z", [P, KD, TOK])
        rope_x, e = sb("rope_x", [P, 2, 2, TOK], offset=z_at)
        rope_a, e = sb("rope_a", [P, 2, TOK], offset=e)
        rope_b, e = sb("rope_b", [P, 2, TOK], offset=e)
        tab, _ = sb("tab", [P, 2, 2, TOK])
        mat, _ = sb("mat", [P, 5, P])
        msk, _ = sb("msk", [P, 1024], BF16)
        gb, _ = sb("gb", [P, DEPTH, 3, 2, KD])
        rg, _ = sb("rg", [P, DEPTH, 3])
        snk, _ = sb("snk", [P, DEPTH, 9])
        eps, _ = sb("eps", [P, 1])
        c_z, _ = sb("c_z", [P, 1792], offset=at[0])
        zsq, _ = sb("zsq", [P, 2, TOK])
        zsum, _ = sb("zsum", [P, 2, TOK])
        zsqsum, _ = sb("zsqsum", [P, 2, TOK])
        msq, _ = sb("msq", [P, TOK])
        var, _ = sb("var", [P, TOK])
        rstd, _ = sb("rstd", [P, TOK])
        phase_at = at[0]
        hid_high, e = sb("hid_high", [P, KF, TOK], F32R, offset=phase_at)
        hid_low, e = sb("hid_low", [P, KF, TOK], F32R, offset=e)
        silu_g, e = sb("silu_g", [P, 2, TOK], offset=e)
        gated, e = sb("gated", [P, 2, TOK], offset=e)
        ends = [e]
        qT, e = sb("qT", [P, 8, TOK], offset=phase_at)
        kT, e = sb("kT", [P, 7, KEYS], offset=e)
        kd, e = sb("kd", [96, 4, KEYS], offset=e)
        qd_rot, e = sb("qd_rot", [P, TOK], offset=e)
        qd, _ = sb("qd", [96, 4, TOK], offset=e)
        cq_x, e = sb("cq_x", [P, 2, TOK], offset=e)
        relu_l, e = sb("relu_l", [P, 1024], offset=e)
        cq_high, e = sb("cq_high", [P, 2, TOK], F32R, offset=e)
        cq_low, e = sb("cq_low", [P, 2, TOK], F32R, offset=e)
        ckv_high, e = sb("ckv_high", [P, KEYS], F32R, offset=e)
        ckv_low, e = sb("ckv_low", [P, KEYS], F32R, offset=e)
        v_tok, e = sb("v_tok", [P, 3, V_TOK], offset=e)
        v_past, e = sb("v_past", [P, 448], offset=e)
        v_d, e = sb("v_d", [P, 4, 256], offset=e)
        prob, e = sb("prob", [P, 2, 1792], offset=e)
        probT, e = sb("probT", [P, 1792], offset=e)
        score, e = sb("score", [P, 128 + 256 + 160], offset=e)
        hide_b, e = sb("hide_b", [P, 128 + 256 + 160], BF16, offset=e)
        w_idx, e = sb("w_idx", [P, 3, 4], offset=e)
        best8, e = sb("best8", [P, 8], offset=e)
        top_s, e = sb("top_s", [P, 9], offset=e)
        neg_m, e = sb("neg_m", [P, 9], offset=e)
        sums, e = sb("sums", [P, 9], offset=e)
        sink_e, e = sb("sink_e", [P, 9], offset=e)
        recip, e = sb("recip", [P, 9], offset=e)
        ends.append(e)
        assert max(ends) <= 229344 - 320 - 256, ends
        ps = ctx.enter_context(nc.psum_tensor("ps", [P, 8, 512], F32))

        swap_r, swap_a, ident, ones, later = (mat[:, i, :] for i in range(5))
        m_blk0, m_a1, m_c1 = msk[:, 0:128], msk[:, 128:384], msk[:, 384:640]
        m_strict, id_bf = msk[:, 640:896], msk[:, 896:1024]
        zeros_bf, _ = sb("zeros_bf", [P, 160], BF16, offset=max(ends))
        rep_bf, _ = sb("rep_bf", [32, P], BF16, offset=max(ends) + 320)

        def sem(name):
            return ctx.enter_context(nc.semaphore(name))

        const_landed = sem("const_landed")
        cache_landed = sem("cache_landed")
        x_landed = [sem(f"x_landed{pair}") for pair in range(4)]
        first_landed = [sem(f"first_landed{part}") for part in range(4)]
        raw_landed = [sem(f"raw_landed{i}") for i in range(NRAW)]
        stored, y_stored = sem("stored"), sem("y_stored")
        first_high, first_low = sem("first_high"), sem("first_low")
        high_ready = sem("high_ready")
        low_ready = sem("low_ready")
        chunk_used = sem("chunk_used")
        x_high_ready, x_low_ready = sem("x_high_ready"), sem("x_low_ready")
        h_ready = sem("h_ready")
        silu_ready, gated_ready = sem("silu_ready"), sem("gated_ready")
        hid_high_ready, hid_low_ready = sem("hid_high_ready"), sem("hid_low_ready")
        tile6_ready = sem("tile6_ready")
        z_ready = sem("z_ready")
        zsq_ready = sem("zsq_ready")
        zsq_added = sem("zsq_added")
        zsum_ready, zsqsum_ready = sem("zsum_ready"), sem("zsqsum_ready")
        stat_ready = sem("stat_ready")
        msq_ready, var_ready = sem("msq_ready"), sem("var_ready")
        rstd_ready = sem("rstd_ready")
        centered, norm_ready = sem("centered"), sem("norm_ready")
        values_copied = sem("values_copied")
        proj_copied = sem("proj_copied")
        swapped = sem("swapped")
        roped = sem("roped")
        latent_squared, latent_summed = sem("latent_squared"), sem("latent_summed")
        latent_rstd_ready, latent_ready = sem("latent_rstd_ready"), sem("latent_ready")
        latent_high_ready, latent_low_ready = sem("latent_high_ready"), sem("latent_low_ready")
        d_projected = sem("d_projected")
        d_copied = sem("d_copied")
        d_rotated = sem("d_rotated")
        logits_ready, relu_ready, scored = sem("logits_ready"), sem("relu_ready"), sem("scored")
        topk_done = sem("topk_done")
        scores_ready, max_ready = sem("scores_ready"), sem("max_ready")
        exp_ready, probs_ready = sem("exp_ready"), sem("probs_ready")
        transposed = sem("transposed")
        t_copied_act, t_copied_dve = sem("t_copied_act"), sem("t_copied_dve")
        c_scores_copied, c_log_ready = sem("c_scores_copied"), sem("c_log_ready")
        softplus_ready, c_log_weights_ready = sem("softplus_ready"), sem("c_log_weights_ready")
        c_sum_ready, c_weights_ready = sem("c_sum_ready"), sem("c_weights_ready")
        weighted_ready = sem("weighted_ready")
        o_high_ready, o_low_ready = sem("o_high_ready"), sem("o_low_ready")
        part_ready, part_added = sem("part_ready"), sem("part_added")
        wo_ready = sem("wo_ready")
        act_link, dve_link, pe_link, pool_link = sem("act_link"), sem("dve_link"), sem("pe_link"), sem("pool_link")

        def ge(eng, semaphore, value):
            if value > 0:
                eng.wait_ge(semaphore, value)

        def first_part(chunk0, pair):
            return chunk0.rearrange("p (g k n) -> p g k n", g=2, k=KD)[:, :, 2 * pair:2 * pair + 2, :]

        def gate_bank(t):
            return (0, 6, 4)[t % 3]

        def down_bank(q):
            return (6, 4)[q % 2]

        def by_pool(c):
            return c % LAYER_CHUNKS in POOL_LOW and c > 1

        def landed(c):
            return 16 * (c // NRAW + (c % NRAW > 0))

        def hidden(tensor, t, m):
            if isinstance(m, int):
                return tensor[:, t, :]
            return tensor[:, bass.ds(TURN * m + t, 1), :].rearrange("p o n -> p (o n)")

        def t_bank(s, g):
            return g if s == 2 else g % 2

        def chunk(local):
            n = chunk_width(local)
            return raw[:, local % NRAW, 0:n], w_high[:, local % NSPLIT, 0:n], w_low[:, local % NSPLIT, 0:n]

        block = ctx.enter_context(nc.Block())

        @block.sync
        def _(sp):
            def load(l, local, m):
                c = l * LAYER_CHUNKS + local
                n = chunk_width(local)
                src = weights[l, local, :, 0:n] if isinstance(m, int) else \
                    weights[l, bass.ds(TURN * m + local, 1), :, 0:n].rearrange("o p n -> (o p) n")
                if c >= NRAW:
                    sp.wait_ge(low_ready, TURN * m + (c - NRAW + 1))
                sp.dma_start(raw[:, local % NRAW, 0:n], src).then_inc(raw_landed[c % NRAW], 16)

            for pair in range(4):
                sp.dma_start(first_part(raw[:, 0, :], pair), first_part(weights[0, 0], pair)).then_inc(first_landed[pair], 16)
                sp.dma_start(hT[:, 2 * pair:2 * pair + 2, :], x_in[:, 2 * pair:2 * pair + 2, :]).then_inc(x_landed[pair], 16)
            for l in range(DEPTH):
                local = int(l == 0)
                while local < LAYER_CHUNKS:
                    if local in (FFN0_AT + 2 * ALONE, FFN1_AT + 2 * ALONE):
                        with sp.Fori(0, TURNS) as m:
                            for u in range(TURN):
                                load(l, local + u, m)
                        local += TURNS * TURN
                    else:
                        load(l, local, 0)
                        local += 1
            for pair in range(4):
                sp.wait_ge(h_ready, KD * (3 * DEPTH - 1) + 2 * pair + 2)
                sp.dma_start(out_y[:, 2 * pair:2 * pair + 2, :], hT[:, 2 * pair:2 * pair + 2, :]).then_inc(y_stored, 16)
            sp.wait_ge(y_stored, 4 * 16)

        @block.gpsimd
        def _(pool):
            pool.wait_ge(raw_landed[1], 16)
            for dst, src in ((tab, tables), (mat, mats), (gb, ln_gb), (rg, rms_g), (snk, sinks)):
                pool.dma_start(dst[:], src).then_inc(const_landed, 16)
            pool.dma_start(msk[:, 0:1024], masks[:, 0:1024]).then_inc(const_landed, 16)
            pool.dma_start(zeros_bf[:, :], masks[:, 1024:1184]).then_inc(const_landed, 16)
            pool.dma_start(rep_bf[:, :], masks[0:32, 1184:1312]).then_inc(const_landed, 16)
            links = [0]

            def link(ins):
                links[0] += 1
                ins.then_inc(pool_link, 1)
                pool.wait_ge(pool_link, links[0])

            def square_sums(n):
                for q in (1, 2):
                    pool.wait_ge(zsq_ready, 5 * n + q + 1)
                    pool.tensor_tensor(zsqsum[:, :, :], zsqsum[:, :, :], zsq[:, :, :], ALU.add).then_inc(zsq_added, 1)
                    pool.wait_ge(zsq_added, 2 * n + q)
                link(pool.tensor_tensor(zsqsum[:, 0, :], zsqsum[:, 0, :], zsqsum[:, 1, :], ALU.add))
                pool.wait_ge(zsq_ready, 5 * n + 4)
                pool.tensor_tensor(zsqsum[:, 0, :], zsqsum[:, 0, :], zsq[:, 0, :], ALU.add).then_inc(zsqsum_ready, 1)

            def low(l, local):
                c = l * LAYER_CHUNKS + local
                r, wh, wl = chunk(local)
                pool.wait_ge(low_ready, c)
                pool.wait_ge(high_ready, c + 1)
                pool.tensor_tensor(wl, r, wh.bitcast(F32), ALU.subtract).then_inc(low_ready, 1)

            for l in range(DEPTH):
                square_sums(3 * l)
                low(l, MIX_AT + 1)
                pool.wait_ge(chunk_used, l * LAYER_CHUNKS + FFN_CHUNKS)
                pool.dma_start(kT[:, :, TOK:KEYS], k_cache[l]).then_inc(cache_landed, 16)
                pool.dma_start(v_past[:, :], v_cache[l]).then_inc(cache_landed, 16)
                pool.wait_ge(values_copied, 3 * (l + 1))
                pool.dma_start(out_v[l], v_tok[:, 0:2, 0:448]).then_inc(stored, 16)
                pool.dma_start(out_vs[l], v_tok[0:32, 2, 0:448]).then_inc(stored, 16)
                pool.wait_ge(cache_landed, 32 * (l + 1))
                pool.dma_start(out_va[l], v_past[32:128, 0:128]).then_inc(stored, 16)
                pool.wait_ge(roped, 6 * l + 3)
                pool.wait_ge(latent_ready, 2 * (l + 1))
                pool.wait_ge(proj_copied, FM_CHUNKS * l + C_LAST + 1)
                kr = kT[64:96, KR, :].rearrange("p (o t) -> p o t", o=1).to_broadcast([32, 4, KEYS])
                link(pool.tensor_copy(kd[64:96, :, :], kr))
                pool.dma_start(out_k[l], kT[:, :, 0:TOK]).then_inc(stored, 16)
                pool.dma_start(out_ka[l], kT[:, KA, TOK + 32:KEYS]).then_inc(stored, 16)
                low(l, WO_AT)
                pool.wait_ge(roped, 6 * l + 5)
                pool.wait_ge(low_ready, l * LAYER_CHUNKS + WO_AT + 1)
                for h in range(4):
                    link(pool.tensor_copy(qd[64:96, h, :], qd_rot[32 * h:32 * h + 32, :]))
                pool.sem_inc(d_rotated, 1)
                for local in range(WO_AT + 1, FFN1_AT + 1):
                    low(l, local)
                square_sums(3 * l + 1)
                low(l, FFN1_AT + 1)
                pool.wait_ge(stored, 5 * 16 * (l + 1))
                square_sums(3 * l + 2)
                if l < DEPTH - 1:
                    low(l + 1, FFN0_AT + 1)

        @block.tensor
        def _(pe):
            links = [0]

            def link(mm):
                links[0] += 1
                mm.then_inc(pe_link, 1)
                pe.wait_ge(pe_link, links[0])

            def three(out, wh, wl, xh, xl, first, last):
                pe.matmul(out, wh, xh, start=first, stop=False, skip_group_check=True)
                pe.matmul(out, wh, xl, start=False, stop=False, skip_group_check=True)
                return pe.matmul(out, wl, xh, start=False, stop=last, skip_group_check=True)

            def ffn(l, i):
                f, base = 2 * l + i, (FFN0_AT, FFN1_AT)[i]
                event = 3 * l + (0, 2)[i]

                def gate_up(t, k, m=0):
                    _, wh, wl = (a.rearrange("p (g k n) -> p g k n", g=2, k=KD) for a in chunk(base + t))
                    if l == i == t == 0:
                        if k < 6:
                            pe.wait_ge(first_low, k // 2 + 1)
                        else:
                            pe.wait_ge(low_ready, 1)
                    elif k == 0:
                        pe.wait_ge(low_ready, TURN * m + (l * LAYER_CHUNKS + base + t + 1))
                    if k == 0 and f * KF + t > 2:
                        pe.wait_ge(gated_ready, TURN * m + (f * KF + t - 2))
                    for g in range(2):
                        mm = three(ps[:, gate_bank(t) + g, 0:TOK], wh[:, g, k, :], wl[:, g, k, :],
                                   x_high[:, k, :], x_low[:, k, :], k == 0, k == KD - 1)
                    if k == KD - 1:
                        mm.then_inc(chunk_used, 1)

                for k in range(KD):
                    pe.wait_ge(x_low_ready, KD * event + k + 1)
                    gate_up(0, k)
                    if event > 0:
                        gate_up(1, k)
                if event == 0:
                    for k in range(KD):
                        gate_up(1, k)
                with pe.Fori(0, TURNS) as m:
                    for t in range(ALONE, ALONE + TURN):
                        for k in range(KD):
                            gate_up(t, k, m)
                for t in range(GU_CHUNKS - ALONE, GU_CHUNKS):
                    for k in range(KD):
                        gate_up(t, k)
                pe.wait_ge(gated_ready, f * KF + GU_CHUNKS - 1)
                for q in range(4):
                    if q > 1:
                        pe.wait_ge(z_ready, 5 * event + q - 1)
                    tile = 0
                    for third, n in enumerate(DOWN_SPLIT):
                        local = base + GU_CHUNKS + 3 * q + third
                        _, wh, wl = (a.rearrange("p (f n) -> p f n", f=n) for a in chunk(local))
                        pe.wait_ge(low_ready, l * LAYER_CHUNKS + local + 1)
                        order = [(j, d) for j in range(n) for d in range(2)]
                        if q == 3 and third == 2:
                            order.sort(key=lambda jd: jd[1])
                        for j, d in order:
                            if q == 0 and d == 0:
                                pe.wait_ge(hid_low_ready, f * KF + tile + j + 1)
                            mm = three(ps[:, down_bank(q) + d, 0:TOK], wh[:, j, d * P:(d + 1) * P],
                                       wl[:, j, d * P:(d + 1) * P], hid_high[:, tile + j, :], hid_low[:, tile + j, :],
                                       tile + j == 0, tile + j == KF - 1)
                            if q == 3 and third == 2 and d == 0 and j == n - 1:
                                mm.then_inc(tile6_ready, 1)
                        tile += n
                        mm.then_inc(chunk_used, 1)
                stats_most(event)

            def stats_most(n):
                if n == 0:
                    pe.wait_ge(const_landed, 8 * 16)
                pe.wait_ge(zsum_ready, n + 1)
                pe.matmul(ps[:, 2, 0:TOK], ones, zsum[:, 0, :], start=True, stop=False)

            def stats_rest(n):
                pe.wait_ge(zsqsum_ready, n + 1)
                pe.matmul(ps[:, 3, 0:TOK], ones, zsqsum[:, 0, :], start=True, stop=False)
                pe.wait_ge(z_ready, 5 * (n + 1))
                pe.matmul(ps[:, 2, 0:TOK], ones, z[:, 7, :], start=False, stop=True)
                pe.wait_ge(zsq_ready, 5 * (n + 1))
                pe.matmul(ps[:, 3, 0:TOK], ones, zsq[:, 1, :], start=False, stop=True).then_inc(stat_ready, 1)
                if n < 3 * DEPTH - 1:
                    for _ in range(KEEP_CLOCK):
                        pe.matmul(ps[:, 5, :], id_bf, bcast(m_blk0, 4), start=True, stop=True)

            def swap(l, r):
                pe.wait_ge(proj_copied, FM_CHUNKS * l + ROPE_CHUNKS[r] + 1)
                ge(pe, roped, 6 * l + ROTATION[r])
                for j in range(2):
                    m = swap_r if (r == 2 and j == 0) else swap_a
                    mm = pe.matmul(ps[:, 6 + j, 0:TOK], m, rope_x[:, r % 2, j, :], start=True, stop=True)
                mm.then_inc(swapped, 1)

            def head(h):
                return slice(64 * (h % 2), 64 * (h % 2) + 64)

            def indexer(l, g):
                ge(pe, relu_ready, 3 * l + g)
                if g == 0:
                    pe.wait_ge(roped, 6 * l + 2)
                else:
                    pe.wait_ge(cache_landed, 32 * (l + 1))
                for half in range(2):
                    for h in (half, half + 2):
                        q, k = qT[head(h), QI + h // 2, :], kT[head(h), KI, :]
                        if g == 0:
                            mm = pe.matmul(ps[:, 4 + h // 2, 256 * half:256 * half + 256], q[:, 128:256], k[:, 0:256],
                                           start=True, stop=True, skip_group_check=True)
                        if g == 1:
                            mm = pe.matmul(ps[:, 4, 128 * h:128 * h + 128], q[:, 0:128], k[:, 0:128],
                                           start=True, stop=True, skip_group_check=True)
                        if g == 1 + h // 2:
                            bank, at_ = 6 - g, SKEYS * half
                            pe.matmul(ps[0:32, bank, at_:at_ + PAST], q[:, SEQ:TOK], k[:, TOK:KEYS],
                                      start=True, stop=True, skip_group_check=True)
                            mm = pe.matmul(ps[0:32, bank, at_ + PAST:at_ + SKEYS], q[:, SEQ:TOK], k[:, SEQ:TOK],
                                           start=True, stop=True, skip_group_check=True)
                    if half == 0:
                        link(mm)
                mm.then_inc(logits_ready, 1)

            def scores(l, s, groups, mask1, mask0, mask_s):
                for b in range(2):
                    pe.matmul(ps[:, 2 + b, :], id_bf, bcast(mask1, 2), start=True, stop=False, skip_group_check=True)
                pe.matmul(ps[:, 4, :], id_bf, bcast(mask0, 4), start=True, stop=False, skip_group_check=True)
                mm = pe.matmul(ps[:, 5, 0:SKEYS], rep_bf[:, :], mask_s, start=True, stop=False, skip_group_check=True)
                for group in groups:
                    link(mm)
                    last = group is groups[-1]
                    for h, q, k in group:
                        pe.matmul(ps[:, 2 + h // 2, 256 * (h % 2):256 * (h % 2) + 256], q[:, 128:256], k[:, 0:256],
                                  start=False, stop=last, skip_group_check=True)
                        pe.matmul(ps[:, 4, 128 * h:128 * h + 128], q[:, 0:128], k[:, 0:128],
                                  start=False, stop=last, skip_group_check=True)
                        pe.matmul(ps[32 * h:32 * h + 32, 5, 0:PAST], q[:, SEQ:TOK], k[:, TOK:KEYS],
                                  start=False, stop=False, skip_group_check=True)
                        mm = pe.matmul(ps[32 * h:32 * h + 32, 5, PAST:SKEYS], q[:, SEQ:TOK], k[:, SEQ:TOK],
                                       start=False, stop=last, skip_group_check=True)
                mm.then_inc(scores_ready, 1)

            def bcast(m, n):
                return m.rearrange("p (o k) -> p o k", o=1).to_broadcast([P, n, m.shape[-1]])

            def transposes(l, s):
                pe.wait_ge(probs_ready, 3 * l + s + 1)
                pr = prob[:, s % 2, :]
                for g in range(4):
                    if s == 0 and g >= 2:
                        pe.wait_ge(t_copied_act, 7 * l + g - 1)
                    if s == 1 and g == 2:
                        pe.wait_ge(t_copied_act, 7 * l + 4)
                    if s == 1 and g == 3:
                        pe.wait_ge(t_copied_dve, 5 * l + 2)
                    bank = t_bank(s, g)
                    if g < 3:
                        for h in range(4):
                            src = pr[:, 128 * h:128 * h + 128] if g == 0 else \
                                pr[:, 512 + 256 * h + 128 * (g - 1):512 + 256 * h + 128 * g]
                            mm = pe.transpose(ps[:, bank, 128 * h:128 * h + 128], src, ident)
                    else:
                        pe.transpose(ps[:, bank, 0:128], pr[:, 1536:1664], ident)
                        mm = pe.transpose(ps[0:32, bank, 128:256], pr[:, 1664:1696], ident)
                    mm.then_inc(transposed, 1)

            def values(name, h):
                if name == "D":
                    c = slice(64 * h, 64 * h + 64)
                    return v_d[:, 0, c], v_d[:, 1, c], v_d[:, 3, c], v_d[0:32, 2, c]
                c = {"A": V_A + 64 * (h // 2), "B": V_B, "C": V_C + 64 * h}[name]
                c = slice(c, c + 64)
                return v_tok[:, 0, c], v_tok[:, 1, c], v_past[:, c], v_tok[0:32, 2, c]

            def weighted(l, run):
                name = RUN[run]
                s = {"A": 0, "C": None, "D": 1, "B": 2}[name]
                if name == "C":
                    pe.wait_ge(c_weights_ready, l + 1)
                else:
                    pe.wait_ge(t_copied_act, 7 * l + (3, 5, 7)[s])
                    if s > 0:
                        pe.wait_ge(t_copied_dve, 5 * l + (0, 2, 4)[s])
                outs = [ps[64 * (h % 2):64 * (h % 2) + 64, PV_BANK[run] + h // 2, :] for h in range(4)]
                for h, o in enumerate(outs):
                    v0, v1, _, _ = values(name, h)
                    if name == "C":
                        a0, a1 = c_z[:, 256 * h:256 * h + 256], c_z[:, 1024 + 128 * h:1152 + 128 * h]
                        pe.matmul(o[:, 0:256], v0, a0, start=True, stop=False, skip_group_check=True)
                        pe.matmul(o[:, 128:256], v1, a1, start=False, stop=True, skip_group_check=True)
                    else:
                        p0 = probT[:, 128 * h:128 * h + 128]
                        p10, p11 = (probT[:, 512 * (1 + b) + 128 * h:512 * (1 + b) + 128 * h + 128] for b in range(2))
                        pe.matmul(o[:, 0:128], v0, p0, start=True, stop=True, skip_group_check=True)
                        pe.matmul(o[:, 128:256], v0, p10, start=True, stop=False, skip_group_check=True)
                        pe.matmul(o[:, 128:256], v1, p11, start=False, stop=True, skip_group_check=True)
                if name != "C":
                    pe.wait_ge(t_copied_dve, 5 * l + (1, 3, 5)[s])
                at_, buffer = (1536, c_z if name == "C" else probT)
                for h, o in enumerate(outs):
                    _, _, vp, vn = values(name, h)
                    past, new = (buffer[0:rows, a + 32 * h:a + 32 * h + 32] for rows, a in ((P, at_), (32, at_ + P)))
                    pe.matmul(o[:, 256:288], vp, past, start=True, stop=False, skip_group_check=True)
                    mm = pe.matmul(o[:, 256:288], vn, new, start=False, stop=True, skip_group_check=True)
                mm.then_inc(weighted_ready, 1)

            def heads_of(q0, k0, shared):
                return [[(h, qT[head(h), q0 + h // 2, :], kT[head(h), k0 if shared else k0 + h // 2, :])
                         for h in (half, half + 2)] for half in range(2)]

            groups_a = [[(h, qT[64 * g:64 * g + 64, QA + h % 2, :], kT[64 * g:64 * g + 64, KA, :])
                         for h in (2 * g, 2 * g + 1)] for g in range(2)]
            groups_d = [[(h, qd[:, h, :], kd[:, h, :]) for h in range(4)]]

            ONE, OTHER, BOTH = range(0, 2), range(2, 4), range(0, 4)

            def out_projection(l, local, side, bank, rows, tiles=(0, 1)):
                _, wh, wl = (a.rearrange("p (k n) -> p k n", k=4) for a in chunk(local))
                pe.wait_ge(low_ready, l * LAYER_CHUNKS + local + 1)
                names = WO_PARTS[(local - WO_AT) // 2]
                pe.wait_ge(o_low_ready, 4 * l + RUN.index(names[rows[-1] // 2]) + 1)
                for k in rows:
                    x = 2 * WO_ROW[names[k // 2]] + k % 2
                    for d in tiles:
                        c = (2 * side + d) * P
                        mm = three(ps[:, bank + d, 0:TOK], wh[:, k, c:c + P], wl[:, k, c:c + P], x_high[:, x, :],
                                   x_low[:, x, :], k == 0, k == 3)
                return mm

            def c_scores(l):
                pe.wait_ge(proj_copied, FM_CHUNKS * l + C_LAST + 1)
                pe.wait_ge(relu_ready, 3 * (l + 1))
                for b in range(2):
                    pe.matmul(ps[:, 2 + b, :], id_bf, bcast(m_strict, 2), start=True, stop=False, skip_group_check=True)
                pe.matmul(ps[:, 4, :], id_bf, bcast(m_strict[:, 0:128], 4), start=True, stop=False, skip_group_check=True)
                pe.matmul(ps[:, 5, 0:128], id_bf, zeros_bf[:, 0:128], start=True, stop=False, skip_group_check=True)
                mm = pe.matmul(ps[:, 5, 128:256], id_bf, bcast(m_strict[:, 0:32], 4), start=False, stop=False,
                               skip_group_check=True)
                for half, group in enumerate(heads_of(QC, KC, False)):
                    link(mm)
                    for h, q, k in group:
                        pe.matmul(ps[:, 2 + h // 2, 256 * (h % 2):256 * (h % 2) + 256], k[:, 0:128], q[:, 0:256],
                                  start=False, stop=(half == 1), skip_group_check=True)
                        pe.matmul(ps[:, 4, 128 * h:128 * h + 128], k[:, 128:256], q[:, 128:256],
                                  start=False, stop=(half == 1), skip_group_check=True)
                        pe.matmul(ps[:, 5, 32 * h:32 * h + 32], k[:, TOK:KEYS], q[:, SEQ:TOK],
                                  start=False, stop=(half == 1), skip_group_check=True)
                        mm = pe.matmul(ps[0:32, 5, 128 + 32 * h:160 + 32 * h], k[:, SEQ:TOK], q[:, SEQ:TOK],
                                       start=False, stop=(half == 1), skip_group_check=True)
                mm.then_inc(c_sum_ready, 1)

            def mixer(l):
                event = 3 * l + 1
                for half in range(2):
                    local = MIX_AT + half
                    _, wh, wl = (a.rearrange("p (k n) -> p k n", k=4) for a in chunk(local))
                    pe.wait_ge(low_ready, l * LAYER_CHUNKS + local + 1)
                    for kk in range(4):
                        k = 4 * half + kk
                        pe.wait_ge(x_low_ready, KD * event + k + 1)
                        for b, (lo, hi) in enumerate(((0, 128), (128, 256), (256, 288))):
                            out = ps[0:hi - lo, 4 + b, 0:V_TOK]
                            pe.matmul(out, x_high[:, k, lo:hi], wh[:, kk, :], start=(k == 0), stop=False, skip_group_check=True)
                            pe.matmul(out, x_low[:, k, lo:hi], wh[:, kk, :], start=False, stop=False, skip_group_check=True)
                            mm = pe.matmul(out, x_high[:, k, lo:hi], wl[:, kk, :], start=False, stop=(k == KD - 1),
                                           skip_group_check=True)
                    mm.then_inc(chunk_used, 1)
                for i in range(FM_CHUNKS):
                    local = MIX_AT + TM_CHUNKS + i
                    tiles = chunk_width(local) // (KD * P)
                    _, wh, wl = (a.rearrange("p (k n) -> p k n", k=KD) for a in chunk(local))
                    pe.wait_ge(low_ready, l * LAYER_CHUNKS + local + 1)
                    if i >= 2:
                        pe.wait_ge(proj_copied, FM_CHUNKS * l + i - 1)
                    for k in range(KD):
                        for j in range(tiles):
                            mm = three(ps[:, 2 * (i % 2) + j, 0:TOK], wh[:, k, j * P:(j + 1) * P],
                                       wl[:, k, j * P:(j + 1) * P], x_high[:, k, :], x_low[:, k, :],
                                       k == 0, k == KD - 1)
                    mm.then_inc(chunk_used, 1)
                    if i == 1:
                        pe.wait_ge(values_copied, 3 * (l + 1))
                        swap(l, 0)
                    if i == 2:
                        swap(l, 1)
                    if 3 <= i <= 5:
                        indexer(l, i - 3)
                    if i == 3 or i == 4:
                        r = i - 3
                        pe.wait_ge(latent_squared, 2 * l + r + 1)
                        pe.wait_ge(roped, 6 * l + 2)
                        for j in range(2 - r):
                            mm = pe.matmul(ps[:, 6 + r, 0:TOK], ones, zsq[:, j, :] if r == 0 else zsum[:, 0, :],
                                           start=(j == 0), stop=(j == 1 - r))
                        mm.then_inc(latent_summed, 1)
                    if i == 5:
                        pe.wait_ge(latent_rstd_ready, 2 * (l + 1))
                        swap(l, 2)
                    if i == C_LAST:
                        swap(l, 3)
                        c_scores(l)
                pe.wait_ge(c_scores_copied, l + 1)
                pe.wait_ge(roped, 6 * l + 4)
                scores(l, 0, groups_a, m_a1, m_blk0, zeros_bf[0:32, :])
                local = WO_AT - 1
                _, wh, wl = chunk(local)
                uqh, uql = (a[:, 0:768].rearrange("p (k n) -> p k n", k=2) for a in (wh, wl))
                ukh, ukl = (a[:, 768:1280] for a in (wh, wl))
                pe.wait_ge(low_ready, l * LAYER_CHUNKS + local + 1)
                pe.wait_ge(latent_low_ready, 2 * l + 2)
                pe.wait_ge(proj_copied, FM_CHUNKS * (l + 1))

                def d_queries(j, bank):
                    for k in range(2):
                        last = three(ps[:, bank, 0:TOK], uqh[:, k, j * P:(j + 1) * P], uql[:, k, j * P:(j + 1) * P],
                                     cq_high[:, k, :], cq_low[:, k, :], k == 0, k == 1)
                    return last

                d_queries(0, 0)
                d_queries(1, 1).then_inc(d_projected, 1)
                d_queries(2, 6).then_inc(d_projected, 1)
                pe.wait_ge(d_copied, 4 * l + 2)
                pe.matmul(ps[:, 7, 0:TOK], swap_r, rope_x[:, 1, 0, :], start=True, stop=True).then_inc(swapped, 1)

                def d_values(bank):
                    for half in range(2):
                        lo, rows = ((0, 128), (128, 128), (256, 32), (288, 128))[2 * (bank - 6) + half]
                        xh, xl = ckv_high[:, lo:lo + rows], ckv_low[:, lo:lo + rows]
                        out = ps[0:rows, bank, 256 * half:256 * half + 256]
                        pe.matmul(out, xh, ukh[:, 256:512], start=True, stop=False, skip_group_check=True)
                        pe.matmul(out, xl, ukh[:, 256:512], start=False, stop=False, skip_group_check=True)
                        last = pe.matmul(out, xh, ukl[:, 256:512], start=False, stop=True, skip_group_check=True)
                    return last

                d_values(6).then_inc(d_projected, 1)
                for j in range(2):
                    mm = three(ps[:, j, 0:KEYS], ukh[:, j * P:(j + 1) * P], ukl[:, j * P:(j + 1) * P],
                               ckv_high[:, :], ckv_low[:, :], True, True)
                mm.then_inc(d_projected, 1)
                pe.wait_ge(roped, 6 * l + 5)
                d_values(7).then_inc(chunk_used, 1)
                pe.wait_ge(exp_ready, 3 * l + 1)
                pe.wait_ge(softplus_ready, l + 1)
                sp_ = prob[:, 1, :]
                for b in range(2):
                    pe.matmul(ps[:, 2 + b, :], later, sp_[:, 512 * b:512 * b + 512], start=True, stop=False,
                              skip_group_check=True)
                    for j in range(2):
                        pe.matmul(ps[:, 2 + b, 256 * j + 128:256 * j + 256], ones,
                                  sp_[:, 1024 + 128 * (2 * b + j):1152 + 128 * (2 * b + j)],
                                  start=False, stop=(j == 1), skip_group_check=True)
                pe.matmul(ps[:, 4, :], later, sp_[:, 1024:1536], start=True, stop=True)
                pe.matmul(ps[:, 5, 0:256], later, sp_[:, 1536:1792], start=True, stop=False, skip_group_check=True)
                pe.matmul(ps[:, 5, 0:128], ones, sp_[:, 1664:1792], start=False, stop=True,
                          skip_group_check=True).then_inc(c_sum_ready, 1)
                pe.wait_ge(d_copied, 4 * (l + 1))
                transposes(l, 0)
                swap(l, 4)
                pe.wait_ge(c_log_weights_ready, l + 1)
                pe.wait_ge(d_rotated, l + 1)
                scores(l, 1, groups_d, m_c1, m_blk0, zeros_bf[0:32, :])
                pe.wait_ge(roped, 6 * (l + 1))
                weighted(l, 0)
                weighted(l, 1)
                out_projection(l, WO_AT, 0, 6, ONE)
                out_projection(l, WO_AT, 0, 6, OTHER).then_inc(part_ready, 1)
                out_projection(l, WO_AT, 1, 0, BOTH).then_inc(chunk_used, 1)
                pe.wait_ge(exp_ready, 3 * l + 2)
                pe.wait_ge(topk_done, l + 1)
                scores(l, 2, heads_of(QB, KB, True), hide_b[:, 128:384], hide_b[:, 0:128], hide_b[0:32, 384:544])
                pe.wait_ge(part_added, 4 * l + 2)
                transposes(l, 1)
                weighted(l, 2)
                out_projection(l, WO_AT + 1, 0, 0, BOTH).then_inc(part_ready, 1)
                pe.wait_ge(o_low_ready, 4 * l + 3)
                out_projection(l, WO_AT + 1, 1, 6, BOTH).then_inc(chunk_used, 1)
                pe.wait_ge(part_added, 4 * l + 3)
                transposes(l, 2)
                out_projection(l, WO_AT + 2, 0, 4, ONE)
                pe.wait_ge(part_added, 4 * (l + 1))
                weighted(l, 3)
                out_projection(l, WO_AT + 2, 1, 0, ONE)
                out_projection(l, WO_AT + 2, 0, 4, OTHER).then_inc(wo_ready, 1)
                out_projection(l, WO_AT + 2, 1, 0, OTHER).then_inc(chunk_used, 1)
                out_projection(l, WO_AT + 3, 0, 6, BOTH).then_inc(wo_ready, 1)
                pe.wait_ge(z_ready, 5 * event + 1)
                out_projection(l, WO_AT + 3, 1, 4, BOTH, (0,)).then_inc(tile6_ready, 1)
                out_projection(l, WO_AT + 3, 1, 4, BOTH, (1,)).then_inc(chunk_used, 1)
                stats_most(event)

            for l in range(DEPTH):
                ffn(l, 0)
                stats_rest(3 * l)
                mixer(l)
                stats_rest(3 * l + 1)
                ffn(l, 1)
                stats_rest(3 * l + 2)

        @block.scalar
        def _(act):
            links = [0]

            def link(ins):
                links[0] += 1
                ins.then_inc(act_link, 1)
                act.wait_ge(act_link, links[0])

            split = [1]

            def high_until(n):
                while split[0] < min(n, DEPTH * LAYER_CHUNKS):
                    high_part(split[0])
                    split[0] += 1

            def high_part(c, m=0):
                r, wh, _ = chunk(c % LAYER_CHUNKS)
                act.wait_ge(raw_landed[c % NRAW], 16 * TURN // NRAW * m + landed(c))
                if c >= NSPLIT:
                    act.wait_ge(chunk_used, TURN * m + (c - NSPLIT + 1))
                act.activation(wh, r, ACT.Copy).then_inc(high_ready, 1)

            def ffn(l, i):
                f, base = 2 * l + i, l * LAYER_CHUNKS + (FFN0_AT, FFN1_AT)[i]

                def high(t, m=0):
                    act.wait_ge(gated_ready, TURN * m + (f * KF + t + 1))
                    act.activation(hidden(hid_high, t, m), gated[:, t % 2, :], ACT.Copy).then_inc(hid_high_ready, 1)

                def silu(t, m=0):
                    if isinstance(m, int):
                        high_until(base + t + NSPLIT)
                    else:
                        high_part(base + t + NSPLIT - 1, m)
                    act.wait_ge(chunk_used, TURN * m + (base + t + 1))
                    if f * KF + t > 1:
                        act.wait_ge(gated_ready, TURN * m + (f * KF + t - 1))
                    act.activation(silu_g[:, t % 2, :], ps[:, gate_bank(t), 0:TOK], ACT.Silu).then_inc(silu_ready, 1)
                    if t > 0:
                        high(t - 1, m)

                if f == 0:
                    act.preload_act_table_set("silu_and_others")
                if i == 1:
                    act.wait_ge(stored, 5 * 16 * (l + 1))
                for t in range(ALONE):
                    silu(t)
                assert split[0] == base + ALONE + NSPLIT - 1
                with act.Fori(0, TURNS) as m:
                    for t in range(ALONE, ALONE + TURN):
                        silu(t, m)
                split[0] += TURNS * TURN
                for t in range(GU_CHUNKS - ALONE, GU_CHUNKS):
                    silu(t)
                high(GU_CHUNKS - 1)
                act.preload_act_table_set("natural_log_exp_and_others")
                for q in range(4):
                    for third in range(3):
                        high_until(base + GU_CHUNKS + 3 * q + third + NSPLIT)
                    square(3 * l + (0, 2)[i], q)

            def square(n, q):
                act.wait_ge(z_ready, 5 * n + q + 1)
                if q == 0:
                    act.activation(zsqsum[:, :, :], z[:, 0:2, :], ACT.Square).then_inc(zsq_ready, 1)
                else:
                    if q == 2:
                        act.wait_ge(zsq_added, 2 * n + 1)
                    if q == 3:
                        act.wait_ge(zsq_added, 2 * n + 2)
                        act.activation(zsq[:, 0, :], z[:, 6, :], ACT.Square).then_inc(zsq_ready, 1)
                        act.wait_ge(z_ready, 5 * (n + 1))
                        act.activation(zsq[:, 1, :], z[:, 7, :], ACT.Square).then_inc(zsq_ready, 1)
                        return
                    act.activation(zsq[:, :, :], z[:, 2 * q:2 * q + 2, :], ACT.Square).then_inc(zsq_ready, 1)

            def norm(n):
                l, which = n // 3, n % 3
                act.wait_ge(stat_ready, n + 1)
                act.activation(msq[:, :], ps[:, 2, 0:TOK], ACT.Square, scale=1.0 / D_MODEL).then_inc(msq_ready, 1)
                act.wait_ge(var_ready, n + 1)
                link(act.activation(rstd[:, :], var[:, :], ACT.Ln))
                act.activation(rstd[:, :], rstd[:, :], ACT.Exp, scale=-0.5).then_inc(rstd_ready, 1)
                if n < 3 * DEPTH - 1:
                    for j in range(KD):
                        act.wait_ge(norm_ready, KD * n + j + 1)
                        act.activation(x_high[:, j, :], z[:, j, :], ACT.Identity,
                                       bias=gb[:, l, which, 1, j:j + 1]).then_inc(x_high_ready, 1)
                        if which > 0 and j == 4:
                            act.preload_act_table_set("silu_and_others")
                    high_until((l + (which == 2)) * LAYER_CHUNKS + (MIX_AT, FFN1_AT, FFN0_AT)[which] + NSPLIT)
                for j in range(KD):
                    act.wait_ge(norm_ready, KD * n + j + 1)
                    act.activation(hT[:, j, :], z[:, j, :], ACT.Identity,
                                   bias=gb[:, l, which, 1, j:j + 1]).then_inc(h_ready, 1)

            def softmax(l, s, scale, between=None):
                act.wait_ge(max_ready, 3 * l + s + 1)
                pr = prob[:, s % 2, :]
                for h in range(4):
                    act.activation(pr[:, 512 + 256 * h:768 + 256 * h], ps[:, 2 + h // 2, 256 * (h % 2):256 * (h % 2) + 256],
                                   ACT.Exp, bias=neg_m[:, 4 + h:5 + h], scale=scale, accum_out=sums[:, 4 + h:5 + h])
                if between is not None:
                    between()
                for h in range(4):
                    act.activation(pr[:, 128 * h:128 * h + 128], ps[:, 4, 128 * h:128 * h + 128],
                                   ACT.Exp, bias=neg_m[:, h:h + 1], scale=scale, accum_out=sums[:, h:h + 1])
                if s == 0:
                    act.activation(sink_e[:, :], top_s[:, :], ACT.Exp)
                act.activation(pr[:, 1536:1696], ps[:, 5, 0:SKEYS], ACT.Exp, bias=neg_m[:, 8:9], scale=scale,
                               accum_out=sums[:, 8:9]).then_inc(exp_ready, 1)

            def copy_t(l, s):
                for g in ((0, 1, 2) if s == 0 else (0, 2)):
                    act.wait_ge(transposed, 4 * (3 * l + s) + g + 1)
                    if g == 0 and s > 0:
                        act.wait_ge(weighted_ready, 4 * l + (1, 1, 3)[s])
                    act.activation(probT[:, 512 * g:512 * g + 512], ps[:, t_bank(s, g), :], ACT.Copy).then_inc(t_copied_act, 1)

            def out_high(l, run):
                act.wait_ge(weighted_ready, 4 * l + run + 1)
                k = 2 * WO_ROW[RUN[run]]
                act.activation(x_high[:, k:k + 2, :], ps[:, PV_BANK[run]:PV_BANK[run] + 2, 0:TOK],
                               ACT.Copy).then_inc(o_high_ready, 1)

            def mixer(l):
                base = l * LAYER_CHUNKS + MIX_AT
                high_until(base + 1 + NSPLIT)
                act.wait_ge(chunk_used, base + 2)
                for b in range(3):
                    rows = 32 if b == 2 else 128
                    act.activation(v_tok[0:rows, b, :], ps[0:rows, 4 + b, 0:V_TOK], ACT.Copy).then_inc(values_copied, 1)
                for b in range(3):
                    rows = 32 if b == 2 else 128
                    ins = act.activation(w_idx[0:rows, b, :], ps[0:rows, 4 + b, W_I:V_TOK], ACT.Copy, scale=1.0 / 16)
                link(ins)
                for i in range(FM_CHUNKS):
                    c = base + TM_CHUNKS + i
                    if i < FM_CHUNKS - 1:
                        high_until(c + NSPLIT)
                    act.wait_ge(chunk_used, c + 1)
                    pair = ps[:, 2 * (i % 2):2 * (i % 2) + 2, 0:TOK]
                    if i in ROPE_CHUNKS:
                        r = ROPE_CHUNKS.index(i)
                        if r >= 2:
                            act.wait_ge(roped, 6 * l + r - 1)
                        act.activation(rope_x[:, r % 2, :, :], pair, ACT.Copy).then_inc(proj_copied, 1)
                    if i == LATENT_Q:
                        act.activation(zsq[:, :, :], pair, ACT.Square).then_inc(latent_squared, 1)
                        act.activation(cq_x[:, :, :], pair, ACT.Copy).then_inc(proj_copied, 1)
                    if i == LATENT_KV:
                        act.activation(zsum[:, 0, :], pair[:, 0, :], ACT.Square).then_inc(latent_squared, 1)
                        act.activation(kT[:, CKV, 0:TOK], pair[:, 0, :], ACT.Copy)
                        act.activation(kT[:, KC, 0:TOK], pair[:, 1, :], ACT.Copy).then_inc(proj_copied, 1)
                    if i == C_FIRST:
                        act.activation(kT[:, KC + 1, 0:TOK], pair[:, 0, :], ACT.Copy)
                        act.activation(qT[:, QC, :], pair[:, 1, :], ACT.Copy).then_inc(proj_copied, 1)
                    if i == C_LAST:
                        act.activation(qT[:, QC + 1, :], pair[:, 0, :], ACT.Copy).then_inc(proj_copied, 1)
                        act.wait_ge(c_sum_ready, 2 * l + 1)
                        zc, ec = c_z[:, :], prob[:, 1, :]
                        flat = ps[:, 2:6, :].rearrange("p b n -> p (b n)")[:, 0:1792]
                        act.activation(zc, flat, ACT.Copy, scale=0.125).then_inc(c_scores_copied, 1)
                        act.wait_ge(c_scores_copied, l + 1)
                        link(act.activation(ec, zc, ACT.Abs))
                        link(act.activation(ec, ec, ACT.Exp, scale=-1.0))
                        act.activation(ec, ec, ACT.Ln, bias=1.0).then_inc(c_log_ready, 1)
                    if 3 <= i <= 5:
                        g = i - 3
                        act.wait_ge(logits_ready, 3 * l + g + 1)
                        ge(act, scored, 3 * l + g)
                        if g == 0:
                            act.activation(relu_l[:, :], ps[:, 4:6, :], ACT.Relu).then_inc(relu_ready, 1)
                        if g == 1:
                            act.activation(relu_l[:, 0:512], ps[:, 4, :], ACT.Relu)
                            act.activation(relu_l[0:32, 512:832], ps[0:32, 5, 0:320], ACT.Relu).then_inc(relu_ready, 1)
                        if g == 2:
                            act.activation(relu_l[0:32, 0:320], ps[0:32, 4, 0:320], ACT.Relu).then_inc(relu_ready, 1)
                    if i == 3 or i == 4:
                        r = i - 3
                        act.wait_ge(latent_summed, 2 * l + r + 1)
                        out = (msq, var)[r]
                        link(act.activation(out[:, :], ps[:, 6 + r, 0:TOK], ACT.Ln, bias=eps[:, :],
                                            scale=1.0 / (Q_LORA, KV_LORA)[r]))
                        act.activation(out[:, :], out[:, :], ACT.Exp, scale=-0.5).then_inc(latent_rstd_ready, 1)
                    if i == 5:
                        act.wait_ge(latent_ready, 2 * l + 1)
                        act.activation(cq_high[:, :, :], cq_x[:, :, :], ACT.Copy).then_inc(latent_high_ready, 1)
                        act.wait_ge(latent_ready, 2 * l + 2)
                        act.wait_ge(cache_landed, 32 * (l + 1))
                        act.activation(ckv_high[:, :], kT[:, CKV, :], ACT.Copy).then_inc(latent_high_ready, 1)
                high_until(base + MIX_CHUNKS - 1 + NSPLIT)
                act.wait_ge(d_projected, 4 * l + 1)
                act.activation(qd[0:64, 0:4:2, :], ps[0:64, 0:2, 0:TOK], ACT.Copy)
                act.activation(qd[0:64, 1:4:2, :], ps[64:128, 0:2, 0:TOK], ACT.Copy).then_inc(d_copied, 1)
                act.wait_ge(d_projected, 4 * l + 2)
                act.activation(rope_x[:, 1, 0, :], ps[:, 6, 0:TOK], ACT.Copy).then_inc(d_copied, 1)
                softmax(l, 0, 0.125)
                act.wait_ge(d_projected, 4 * l + 3)
                act.activation(v_d[:, 0:2, :], ps[:, 6, :], ACT.Copy)
                act.wait_ge(d_projected, 4 * (l + 1))
                act.activation(kd[0:64, 0:4:2, :], ps[0:64, 0:2, 0:KEYS], ACT.Copy)
                act.activation(kd[0:64, 1:4:2, :], ps[64:128, 0:2, 0:KEYS], ACT.Copy).then_inc(d_copied, 1)
                act.wait_ge(chunk_used, base + MIX_CHUNKS)
                act.activation(v_d[0:32, 2, :], ps[0:32, 7, 0:256], ACT.Copy)
                act.activation(v_d[:, 3, :], ps[:, 7, 256:512], ACT.Copy).then_inc(d_copied, 1)
                copy_t(l, 0)
                high_until(base + MIX_CHUNKS + NSPLIT)
                act.wait_ge(c_log_weights_ready, l + 1)
                act.activation(zc, zc, ACT.Exp).then_inc(c_weights_ready, 1)
                out_high(l, 0)
                softmax(l, 1, 96 ** -0.5, between=lambda: out_high(l, 1))
                high_until(base + MIX_CHUNKS + 1 + NSPLIT)
                copy_t(l, 1)
                softmax(l, 2, 0.125, between=lambda: out_high(l, 2))
                high_until(base + MIX_CHUNKS + 2 + NSPLIT)
                copy_t(l, 2)
                out_high(l, 3)
                square(3 * l + 1, 0)
                high_until(base + MIX_CHUNKS + 3 + NSPLIT)
                for q in range(1, 4):
                    square(3 * l + 1, q)

            for pair in range(4):
                act.wait_ge(first_landed[pair], 16)
                act.activation(first_part(w_high[:, 0, :], pair), first_part(raw[:, 0, :], pair),
                               ACT.Copy).then_inc(first_high if pair < 3 else high_ready, 1)
                act.wait_ge(x_landed[pair], 16)
                for j in (2 * pair, 2 * pair + 1):
                    act.activation(x_high[:, j, :], hT[:, j, :], ACT.Copy).then_inc(x_high_ready, 1)
            for l in range(DEPTH):
                ffn(l, 0)
                norm(3 * l)
                mixer(l)
                norm(3 * l + 1)
                ffn(l, 1)
                norm(3 * l + 2)

        @block.vector
        def _(dve):
            links = [0]

            def link(ins):
                links[0] += 1
                ins.then_inc(dve_link, 1)
                dve.wait_ge(dve_link, links[0])

            split = [1]

            def low_until(n):
                while split[0] < min(n, DEPTH * LAYER_CHUNKS):
                    c = split[0]
                    if by_pool(c):
                        split[0] += 1
                        continue
                    if by_pool(c - 1):
                        dve.wait_ge(low_ready, c)
                    low_part(c)
                    split[0] += 1

            def low_part(c, m=0):
                r, wh, wl = chunk(c % LAYER_CHUNKS)
                dve.wait_ge(high_ready, TURN * m + (c + 1))
                dve.tensor_tensor(wl, r, wh.bitcast(F32), ALU.subtract).then_inc(low_ready, 1)

            def ffn(l, i):
                f, base = 2 * l + i, l * LAYER_CHUNKS + (FFN0_AT, FFN1_AT)[i]

                def low(t, m=0):
                    dve.wait_ge(hid_high_ready, TURN * m + (f * KF + t + 1))
                    dve.tensor_tensor(hidden(hid_low, t, m), gated[:, t % 2, :], hidden(hid_high, t, m).bitcast(F32),
                                      ALU.subtract).then_inc(hid_low_ready, 1)

                def gate(t, m=0):
                    if isinstance(m, int):
                        low_until(base + t + NSPLIT)
                    else:
                        low_part(base + t + NSPLIT - 1, m)
                    dve.wait_ge(silu_ready, TURN * m + (f * KF + t + 1))
                    if f * KF + t > 1:
                        dve.wait_ge(hid_low_ready, TURN * m + (f * KF + t - 1))
                    dve.scalar_tensor_tensor(out=gated[:, t % 2, :], in0=silu_g[:, t % 2, :], scalar=0.5,
                                             in1=ps[:, gate_bank(t) + 1, 0:TOK], op0=ALU.mult, op1=ALU.mult)\
                       .then_inc(gated_ready, 1)
                    if t > 0:
                        low(t - 1, m)

                for t in range(ALONE):
                    gate(t)
                assert split[0] == base + ALONE + NSPLIT - 1
                with dve.Fori(0, TURNS) as m:
                    for t in range(ALONE, ALONE + TURN):
                        gate(t, m)
                split[0] += TURNS * TURN
                for t in range(GU_CHUNKS - ALONE, GU_CHUNKS):
                    gate(t)
                low(GU_CHUNKS - 1)
                for q in range(4):
                    for third in range(3):
                        low_until(base + GU_CHUNKS + 3 * q + third + NSPLIT)
                    residual(3 * l + (0, 2)[i], q, base + GU_CHUNKS + 3 * q + 3)

            def residual(n, q, used):
                ge(dve, h_ready, KD * n)
                bank = (4, 0, 6, 4)[q] if n % 3 == 1 else down_bank(q)
                if n % 3 == 1:
                    dve.wait_ge(part_added, 4 * (n // 3) + q + 1)
                for tiles in ((2 * q, 2),) if q < 3 else ((6, 1), (7, 1)):
                    at_, count = tiles
                    if at_ == 6:
                        dve.wait_ge(tile6_ready, n + 1)
                    elif used is not None:
                        dve.wait_ge(chunk_used, used)
                    zt, out = z[:, at_:at_ + count, :], ps[:, bank + at_ % 2:bank + at_ % 2 + count, 0:TOK]
                    if n % 3 == 1:
                        dve.tensor_tensor(zt, zt, out, ALU.add).then_inc(z_ready, 1)
                    else:
                        dve.scalar_tensor_tensor(out=zt, in0=hT[:, at_:at_ + count, :], scalar=DN_ALPHA,
                                                 in1=out, op0=ALU.mult, op1=ALU.add).then_inc(z_ready, 1)
                    if at_ == 6:
                        dve.wait_ge(z_ready, 5 * n + 4)
                        dve.tensor_tensor(zsum[:, 0, :], zsum[:, 0, :], z[:, 6, :], ALU.add).then_inc(zsum_ready, 1)
                zq = z[:, 2 * q:2 * q + 2, :]
                if q in (0, 3):
                    return
                dve.wait_ge(z_ready, 5 * n + q + 1)
                link(dve.tensor_tensor(zsum[:, :, :], z[:, 0:2, :] if q == 1 else zsum[:, :, :], zq, ALU.add))
                if q == 2:
                    link(dve.tensor_tensor(zsum[:, 0, :], zsum[:, 0, :], zsum[:, 1, :], ALU.add))

            def norm(n):
                if n == 0:
                    dve.wait_ge(const_landed, 8 * 16)
                l, which = n // 3, n % 3

                def center(j):
                    dve.scalar_tensor_tensor(out=z[:, j, :], in0=ps[:, 2, 0:TOK], scalar=-1.0 / D_MODEL, in1=z[:, j, :],
                                             op0=ALU.mult, op1=ALU.add).then_inc(centered, 1)

                def scale(j):
                    dve.wait_ge(centered, KD * n + j + 1)
                    dve.scalar_tensor_tensor(out=z[:, j, :], in0=z[:, j, :], scalar=gb[:, l, which, 0, j:j + 1],
                                             in1=rstd[:, :], op0=ALU.mult, op1=ALU.mult).then_inc(norm_ready, 1)

                def low(j):
                    if n == 3 * DEPTH - 1:
                        return
                    dve.wait_ge(x_high_ready, KD * (n + 1) + j + 1)
                    dve.scalar_tensor_tensor(out=x_low[:, j, :], in0=z[:, j, :], scalar=gb[:, l, which, 1, j:j + 1],
                                             in1=x_high[:, j, :].bitcast(F32), op0=ALU.add,
                                             op1=ALU.subtract).then_inc(x_low_ready, 1)

                dve.wait_ge(msq_ready, n + 1)
                link(dve.scalar_tensor_tensor(out=var[:, :], in0=ps[:, 3, 0:TOK], scalar=1.0 / D_MODEL, in1=msq[:, :],
                                              op0=ALU.mult, op1=ALU.subtract))
                dve.tensor_scalar(var[:, :], var[:, :], 0.0, LN_EPS, ALU.max, ALU.add).then_inc(var_ready, 1)
                center(0)
                center(1)
                dve.wait_ge(rstd_ready, n + 1)
                scale(0)
                scale(1)
                for j in range(2, KD):
                    center(j)
                    low(j - 2)
                    scale(j)
                low(KD - 2)
                low(KD - 1)

            def rope(l, r):
                kind, tile = ROPE_PAIRS[r]
                both = r == 2
                dst = qT[:, tile:tile + 2, :] if kind == "q" else kT[:, tile:tile + 2, 0:TOK]
                cos, sin = (tab[:, i, :, :] if both else tab[:, i, 1:2, :].to_broadcast([P, 2, TOK]) for i in range(2))
                dve.wait_ge(proj_copied, FM_CHUNKS * l + ROPE_CHUNKS[r] + 1)
                link(dve.tensor_tensor(rope_a[:, :, :], rope_x[:, r % 2, :, :], cos, ALU.mult))
                dve.wait_ge(swapped, 6 * l + ROTATION[r] + 1)
                link(dve.tensor_tensor(rope_b[:, :, :], ps[:, 6:8, 0:TOK], sin, ALU.mult))
                dve.tensor_tensor(dst, rope_a[:, :, :], rope_b[:, :, :], ALU.add).then_inc(roped, 1)
                dve.wait_ge(roped, 6 * l + ROTATION[r] + 1)

            s_blk0, s_blk1, s_smp = score[:, 0:128], score[:, 128:384], score[0:32, 384:544]

            def weigh(l, out, mask, relu, h, b, rows, n):
                link(dve.scalar_tensor_tensor(out=out, in0=relu, scalar=w_idx[0:rows, b, h:h + 1],
                                              in1=mask if h == 0 else out, op0=ALU.mult, op1=ALU.add))

            def indexer(l, g):
                dve.wait_ge(relu_ready, 3 * l + g + 1)
                if g == 0:
                    for h in range(4):
                        weigh(l, s_blk1, m_c1, relu_l[:, 256 * h:256 * h + 256], h, 1, P, 256)
                if g == 1:
                    for h in range(4):
                        weigh(l, s_blk0, m_blk0, relu_l[:, 128 * h:128 * h + 128], h, 0, P, 128)
                    for h in range(2):
                        weigh(l, s_smp, zeros_bf[0:32, :], relu_l[0:32, 512 + 160 * h:672 + 160 * h], h, 2, 32, 160)
                if g == 2:
                    for h in range(2, 4):
                        weigh(l, s_smp, None, relu_l[0:32, 160 * (h - 2):160 * (h - 1)], h, 2, 32, 160)
                dve.sem_inc(scored, 1)

            top_rounds = [s_blk1] * (TOPK_PROMPT // 8) + [s_blk0] * (TOPK_PROMPT // 8) + [s_smp] * (TOPK_SAMPLE // 8)

            def choose(first, last):
                for s in top_rounds[first:last]:
                    rows = s.shape[0]
                    link(dve.max(best8[0:rows, :], s))
                    link(dve.match_replace(s, best8[0:rows, :], s, TAKEN))
                if last == len(top_rounds):
                    for rows, a, b in ((P, 0, 128), (P, 128, 384), (32, 384, 544)):
                        link(dve.tensor_scalar(hide_b[0:rows, a:b], score[0:rows, a:b], TAKEN, HIDE,
                                               ALU.not_equal, ALU.mult))
                    dve.sem_inc(topk_done, 1)

            def largest(l, s, scale):
                dve.wait_ge(scores_ready, 3 * l + s + 1)
                dve.reduce_max(top_s[:, 4:8], ps[:, 2:4, :].rearrange("p b (h k) -> p (b h) k", h=2), AX_X)
                dve.reduce_max(top_s[:, 0:4], ps[:, 4, :].rearrange("p (h k) -> p h k", h=4), AX_X)
                link(dve.reduce_max(top_s[:, 8:9], ps[:, 5, 0:SKEYS], AX_X))
                if s == 0:
                    sk = snk[:, l, :]
                    link(dve.scalar_tensor_tensor(out=top_s[:, :], in0=top_s[:, :], scalar=scale, in1=sk,
                                                  op0=ALU.mult, op1=ALU.max))
                    link(dve.tensor_scalar(neg_m[:, :], top_s[:, :], -1.0, None, ALU.mult))
                    link(dve.tensor_tensor(top_s[:, :], sk, neg_m[:, :], ALU.add))
                else:
                    link(dve.tensor_scalar(neg_m[:, :], top_s[:, :], -scale, None, ALU.mult))
                dve.sem_inc(max_ready, 1)

            def divide(l, s):
                dve.wait_ge(exp_ready, 3 * l + s + 1)
                if s == 0:
                    link(dve.tensor_tensor(sums[:, :], sums[:, :], sink_e[:, :], ALU.add))
                link(dve.reciprocal(recip[:, :], sums[:, :]))
                pr = prob[:, s % 2, :]
                for a, n in ((0, 128), (512, 256)):
                    v = pr[:, a:a + 4 * n].rearrange("p (h k) -> p h k", h=4)
                    r = recip[:, 4 * (a > 0):4 * (a > 0) + 4].rearrange("p (h o) -> p h o", o=1).to_broadcast([P, 4, n])
                    dve.tensor_tensor(v, v, r, ALU.mult)
                link(dve.tensor_scalar(pr[:, 1536:1696], pr[:, 1536:1696], recip[:, 8:9], None, ALU.mult))
                dve.sem_inc(probs_ready, 1)

            def copy_t(l, s):
                for g in ((3,) if s == 0 else (1, 3)):
                    dve.wait_ge(transposed, 4 * (3 * l + s) + g + 1)
                    if g == 1:
                        if s > 0:
                            dve.wait_ge(weighted_ready, 4 * l + (1, 1, 3)[s])
                        dve.tensor_copy(probT[:, 512:1024], ps[:, t_bank(s, g), :]).then_inc(t_copied_dve, 1)
                    else:
                        link(dve.tensor_copy(probT[:, 1536:1664], ps[:, t_bank(s, g), 0:128]))
                        dve.tensor_copy(probT[0:32, 1664:1792], ps[0:32, t_bank(s, g), 128:256]).then_inc(t_copied_dve, 1)

            def out_low(l, run):
                dve.wait_ge(o_high_ready, 4 * l + run + 1)
                k = 2 * WO_ROW[RUN[run]]
                dve.tensor_tensor(x_low[:, k:k + 2, :], ps[:, PV_BANK[run]:PV_BANK[run] + 2, 0:TOK],
                                  x_high[:, k:k + 2, :].bitcast(F32), ALU.subtract).then_inc(o_low_ready, 1)

            def mixer(l):
                base = l * LAYER_CHUNKS + MIX_AT
                low_until(base + 1 + NSPLIT)
                for i in range(FM_CHUNKS):
                    low_until(base + TM_CHUNKS + i + NSPLIT)
                    if i == 1 or i == 2:
                        rope(l, i - 1)
                    if i == 5 or i == C_LAST:
                        rope(l, 2 + (i == C_LAST))
                    if 3 <= i <= 5:
                        indexer(l, i - 3)
                    if i == 4:
                        dve.wait_ge(latent_rstd_ready, 2 * l + 1)
                        dve.wait_ge(proj_copied, FM_CHUNKS * l + LATENT_KV + 1)
                        for j in range(2):
                            ins = dve.scalar_tensor_tensor(out=cq_x[:, j, :], in0=cq_x[:, j, :], scalar=rg[:, l, j:j + 1],
                                                           in1=msq[:, :], op0=ALU.mult, op1=ALU.mult)
                        ins.then_inc(latent_ready, 1)
                    if i == 5:
                        dve.wait_ge(latent_rstd_ready, 2 * l + 2)
                        dve.scalar_tensor_tensor(out=kT[:, CKV, 0:TOK], in0=kT[:, CKV, 0:TOK], scalar=rg[:, l, 2:3],
                                                 in1=var[:, :], op0=ALU.mult, op1=ALU.mult).then_inc(latent_ready, 1)
                    if i == 6:
                        dve.wait_ge(latent_high_ready, 2 * l + 1)
                        dve.tensor_tensor(cq_low[:, :, :], cq_x[:, :, :], cq_high[:, :, :].bitcast(F32),
                                          ALU.subtract).then_inc(latent_low_ready, 1)
                        dve.wait_ge(latent_high_ready, 2 * l + 2)
                        dve.tensor_tensor(ckv_low[:, :], kT[:, CKV, :], ckv_high[:, :].bitcast(F32),
                                          ALU.subtract).then_inc(latent_low_ready, 1)
                    if i >= 4:
                        choose(*((0, 3), (3, 6), (6, 10), (10, 18), (18, len(top_rounds)))[i - 4])
                largest(l, 0, 0.125)
                dve.wait_ge(d_copied, 4 * l + 2)
                link(dve.tensor_tensor(rope_a[:, 0, :], rope_x[:, 1, 0, :], tab[:, 0, 0, :], ALU.mult))
                dve.wait_ge(swapped, 6 * l + 5)
                link(dve.tensor_tensor(rope_b[:, 0, :], ps[:, 7, 0:TOK], tab[:, 1, 0, :], ALU.mult))
                dve.tensor_tensor(qd_rot[:, :], rope_a[:, 0, :], rope_b[:, 0, :], ALU.add).then_inc(roped, 1)
                dve.wait_ge(c_log_ready, l + 1)
                dve.scalar_tensor_tensor(out=prob[:, 1, :], in0=c_z[:, :], scalar=0.0, in1=prob[:, 1, :],
                                         op0=ALU.max, op1=ALU.add).then_inc(softplus_ready, 1)
                divide(l, 0)
                dve.wait_ge(c_sum_ready, 2 * l + 2)
                flat = ps[:, 2:6, :].rearrange("p b n -> p (b n)")[:, 0:1792]
                dve.scalar_tensor_tensor(out=c_z[:, :], in0=flat, scalar=-1.0, in1=c_z[:, :],
                                         op0=ALU.mult, op1=ALU.add).then_inc(c_log_weights_ready, 1)
                copy_t(l, 0)
                rope(l, 4)
                largest(l, 1, 96 ** -0.5)
                out_low(l, 0)
                out_low(l, 1)
                divide(l, 1)
                part(l, 0)
                part(l, 1)
                copy_t(l, 1)
                largest(l, 2, 0.125)
                out_low(l, 2)
                part(l, 2)
                divide(l, 2)
                part(l, 3)
                copy_t(l, 2)
                out_low(l, 3)
                for q in range(4):
                    if q % 2 == 0:
                        dve.wait_ge(wo_ready, 2 * l + q // 2 + 1)
                        residual(3 * l + 1, q, None)
                    else:
                        residual(3 * l + 1, q, base + MIX_CHUNKS + 2 + q // 2 + 1)
                low_until(base + MIX_CHUNKS + 3 + NSPLIT)

            def part(l, q):
                if q % 2 == 0:
                    dve.wait_ge(part_ready, 2 * l + q // 2 + 1)
                else:
                    dve.wait_ge(chunk_used, l * LAYER_CHUNKS + WO_AT + q // 2 + 1)
                dve.wait_ge(roped, 6 * (l + 1))
                bank = (6, 0, 0, 6)[q]
                dve.scalar_tensor_tensor(out=z[:, 2 * q:2 * q + 2, :], in0=hT[:, 2 * q:2 * q + 2, :], scalar=DN_ALPHA,
                                         in1=ps[:, bank:bank + 2, 0:TOK], op0=ALU.mult, op1=ALU.add)\
                   .then_inc(part_added, 1)

            dve.memset(eps[:, :], RMS_EPS).then_inc(dve_link, 1)
            links[0] += 1
            for j in range(KD):
                if j % 2 == 0:
                    pair = j // 2
                    if pair < 3:
                        dve.wait_ge(first_high, pair + 1)
                    else:
                        dve.wait_ge(high_ready, 1)
                    dve.tensor_tensor(first_part(w_low[:, 0, :], pair), first_part(raw[:, 0, :], pair),
                                      first_part(w_high[:, 0, :], pair).bitcast(F32),
                                      ALU.subtract).then_inc(first_low if pair < 3 else low_ready, 1)
                dve.wait_ge(x_high_ready, j + 1)
                dve.tensor_tensor(x_low[:, j, :], hT[:, j, :], x_high[:, j, :].bitcast(F32),
                                  ALU.subtract).then_inc(x_low_ready, 1)
            for l in range(DEPTH):
                ffn(l, 0)
                norm(3 * l)
                mixer(l)
                norm(3 * l + 1)
                ffn(l, 1)
                norm(3 * l + 2)


def _pack_weights(ins, np):
    w = np.zeros((DEPTH, LAYER_CHUNKS, P, CH), np.float32)
    offs = {}
    at = 0
    for name, n in (("qa", 256), ("ka", 128), ("va", 128), ("qb", 256), ("kb", 64), ("vb", 64), ("qi", 256),
                    ("ki", 64), ("wi", 4), ("qc", 256), ("kc", 256), ("vc", 256), ("cq", 256), ("ckv", 128), ("kr", 32)):
        offs[name] = np.arange(at, at + n)
        at += n

    def heads(name, *hs):
        return np.concatenate([offs[name][64 * h:64 * h + 64] for h in hs])

    fm = [heads("qi", 0, 1, 2, 3), heads("ki", 0, 0), heads("kb", 0, 0), offs["cq"], offs["ckv"],
          heads("kc", 0, 1), np.tile(offs["kr"], 4), offs["ka"], heads("qa", 0, 2, 1, 3), heads("kc", 2, 3),
          heads("qc", 0, 1), heads("qc", 2, 3), heads("qb", 0, 1, 2, 3)]
    fm = np.split(np.concatenate(fm), [256 * i for i in range(1, 8)] + [256 * 7 + 128])
    tm = np.concatenate([offs["va"], offs["vb"], offs["vc"], offs["wi"]])

    def tiles(a, k):
        return a.reshape(k, P, -1).transpose(1, 0, 2).reshape(P, -1)

    for l in range(DEPTH):
        for i, base in enumerate((FFN0_AT, FFN1_AT)):
            g, u, d = ins["ffn_gate"][l, i], ins["ffn_up"][l, i], ins["ffn_down"][l, i]
            for t in range(KF):
                w[l, base + t, :, 0:1024] = tiles(g[:, t * P:(t + 1) * P], KD)
                w[l, base + t, :, 1024:2048] = tiles(u[:, t * P:(t + 1) * P], KD)
            for q in range(4):
                f = 0
                for third, n in enumerate(DOWN_SPLIT):
                    w[l, base + KF + 3 * q + third, :, 0:256 * n] = tiles(
                        d[f * P:(f + n) * P, 256 * q:256 * q + 256], n)
                    f += n
        win = ins["w_in"][l]
        for half in range(2):
            w[l, MIX_AT + half, :, 0:4 * V_TOK] = tiles(win[512 * half:512 * half + 512][:, tm], 4)
        for i in range(FM_CHUNKS):
            w[l, MIX_AT + 2 + i, :, 0:8 * len(fm[i])] = tiles(win[:, fm[i]], KD)
        uq = ins["w_uq"][l].reshape(Q_LORA, 4, 96)
        uq = np.concatenate([uq[:, :, 0:64].reshape(Q_LORA, 256), uq[:, :, 64:96].reshape(Q_LORA, 128)], 1)
        ukv = ins["w_ukv"][l].reshape(KV_LORA, 4, 128)
        w[l, WO_AT - 1, :, 0:768] = tiles(uq, 2)
        w[l, WO_AT - 1, :, 768:1024] = ukv[:, :, 0:64].reshape(KV_LORA, 256)
        w[l, WO_AT - 1, :, 1024:1280] = ukv[:, :, 64:128].reshape(KV_LORA, 256)
        for part, names in enumerate(WO_PARTS):
            rows = np.concatenate([np.arange(256 * WO_ROW[name], 256 * WO_ROW[name] + 256) for name in names])
            for half in range(2):
                w[l, WO_AT + 2 * part + half] = tiles(ins["w_o"][l][rows, 512 * half:512 * half + 512], 4)
    return w


def _constants(np, bf16):
    pos = np.arange(TOK, dtype=np.float32)
    pos[SEQ:] += PAST - SEQ
    tab = np.zeros((P, 2, 2, TOK), np.float32)
    mats = np.zeros((P, 5, P), np.float32)
    for which, half in ((0, 16), (1, 32)):
        inv = np.power(np.float32(10000.0), -np.arange(half, dtype=np.float32) / np.float32(half)).astype(np.float32)
        p = np.arange(P)
        ang = (pos[None, :] * inv[p % half][:, None]).astype(np.float32).astype(np.float64)
        sign = np.where(p % (2 * half) < half, -1.0, 1.0)[:, None]
        tab[:, 0, which] = np.cos(ang)
        tab[:, 1, which] = sign * np.sin(ang)
        mats[p, which, np.where(p % (2 * half) < half, p + half, p - half)] = 1.0
    i = np.arange(P)
    mats[i, 2, i] = 1.0
    mats[:, 3, :] = 1.0
    mats[:, 4, :] = i[:, None] >= i[None, :]
    masks = np.zeros((P, 1312), np.float32)
    q0, q1, k = i[:, None], i[:, None] + 128, np.arange(256)[None, :]
    masks[:, 0:128] = np.where(k[:, 0:128] // 64 <= q0 // 64, 0.0, HIDE)
    masks[:, 128:384] = np.where((k // 64 <= q1 // 64) & (k // 64 >= q1 // 64 - 2), 0.0, HIDE)
    masks[:, 384:640] = np.where(k // 64 <= q1 // 64, 0.0, HIDE)
    masks[:, 640:896] = np.where(i[:, None] < k, 0.0, HIDE)
    masks[i, 896 + i] = 1.0
    for h in range(4):
        j = np.arange(32)
        masks[j, 1184 + 32 * h + j] = 1.0
    return tab, mats, masks.astype(bf16)


def kernel(**inputs):
    import ml_dtypes
    import numpy as np
    import concourse.bacc as bacc
    from concourse.bass_utils import run_bass_kernel_spmd

    ins = {k: np.asarray(v) for k, v in inputs.items()}
    tab, mats, masks = _constants(np, ml_dtypes.bfloat16)
    x = np.concatenate([ins["x_prompt"][0], ins["x_sample"][0]], 0)
    x = x.T.reshape(KD, P, TOK).transpose(1, 0, 2)
    gb = np.stack([ins["ln_g"], ins["ln_b"]], 2).reshape(DEPTH, 3, 2, KD, P).transpose(4, 0, 1, 2, 3)
    rg = np.concatenate([ins["g_cq"], ins["g_ckv"]], 1).reshape(DEPTH, 3, P).transpose(2, 0, 1)
    sink = ins["attn_sinks"]
    sinks = np.concatenate([np.broadcast_to(sink, (P, DEPTH, 4)), np.broadcast_to(sink, (P, DEPTH, 4)),
                            np.repeat(sink, 32, axis=1).T[:, :, None]], 2)
    bk, bi, kr = (ins[n][:, 0].transpose(0, 2, 1) for n in ("cache_b_k", "cache_b_kidx", "cache_d_krope"))
    ka = ins["cache_a_k"][:, 0].reshape(DEPTH, PAST, 128).transpose(0, 2, 1)
    kc = ins["cache_c_k"][:, 0].reshape(DEPTH, PAST, 256).transpose(0, 2, 1)
    k_cache = np.stack([np.tile(bi, (1, 2, 1)), np.tile(bk, (1, 2, 1)), np.tile(kr, (1, 4, 1)), ka,
                        ins["cache_d_ckv"][:, 0].transpose(0, 2, 1), kc[:, 0:128], kc[:, 128:256]], 2)
    v_cache = np.concatenate([ins["cache_a_v"][:, 0].reshape(DEPTH, PAST, 128), ins["cache_b_v"][:, 0],
                              ins["cache_c_v"][:, 0].reshape(DEPTH, PAST, 256)], 2)
    arrays = {"weights": _pack_weights(ins, np), "x_in": x, "ln_gb": gb, "rms_g": rg, "sinks": sinks,
              "k_cache": k_cache, "v_cache": v_cache, "tables": tab, "mats": mats, "masks": masks}
    arrays = {k: np.ascontiguousarray(v) for k, v in arrays.items()}
    outs = {"out_y": (P, KD, TOK), "out_k": (DEPTH, P, 7, TOK), "out_ka": (DEPTH, P, 96),
            "out_v": (DEPTH, P, 2, 448), "out_vs": (DEPTH, 32, 448), "out_va": (DEPTH, 96, 128)}
    nc = bacc.Bacc("TRN2", target_bir_lowering=False, num_devices=1)
    args = [nc.dram_tensor(k, v.shape, mybir.dt.from_np(v.dtype), kind="ExternalInput").ap() for k, v in arrays.items()]
    args += [nc.dram_tensor(k, s, F32, kind="ExternalOutput").ap() for k, s in outs.items()]
    encoder_program(nc, *args)
    r = run_bass_kernel_spmd(nc, [arrays], core_ids=[0]).results[0]

    y = r["out_y"].transpose(1, 0, 2).reshape(D_MODEL, TOK).T
    k = r["out_k"].transpose(0, 3, 2, 1)
    v = np.concatenate([r["out_v"].transpose(0, 2, 1, 3).reshape(DEPTH, SEQ, 448), r["out_vs"]], 1)
    ka_s = np.concatenate([r["out_ka"].transpose(0, 2, 1), k[:, SEQ:, KA]], 1)
    va_s = np.concatenate([r["out_va"], v[:, SEQ:, 0:128]], 1)

    def states(s, a_k, a_v):
        n = s.stop - s.start
        kc_ = k[:, s, KC:KC + 2].reshape(DEPTH, 1, n, 4, 64)
        return (a_k.reshape(DEPTH, 1, 128, 2, 64), a_v.reshape(DEPTH, 1, 128, 2, 64), k[:, None, s, KB, 0:64],
                v[:, None, s, V_B:V_B + 64], k[:, None, s, KI, 0:64], kc_,
                v[:, None, s, V_C:V_C + 256].reshape(DEPTH, 1, n, 4, 64), k[:, None, s, CKV], k[:, None, s, KR, 0:32])

    res = (y[None, 0:SEQ], y[None, SEQ:TOK]) \
        + states(slice(0, SEQ), k[:, 128:SEQ, KA], v[:, 128:SEQ, 0:128]) + states(slice(SEQ, TOK), ka_s, va_s)
    return tuple(np.ascontiguousarray(a) for a in res)
```
